# Optimizing a Trainium2 kernel written in Bass

```python
import math
import jax, jax.numpy as jnp
from jax import lax
import numpy as np

D_MODEL = 2048
BATCH = 1
SEQ = 512
DEPTH = 2

EPS = 1e-6
GRID_W = 64
HEAD_DIM = 128
ATTN_HEADS = D_MODEL // 256
KV_HEADS = max(1, ATTN_HEADS // 4)
ATTN_WIDTH = ATTN_HEADS * HEAD_DIM
KV_WIDTH = KV_HEADS * HEAD_DIM
Q_BLOCK = 128
ROPE_THETA = 10000.0
ROPE_HALF = HEAD_DIM // 2
LRU_WIDTH = D_MODEL // 2
LRU_BLOCKS = 8
LRU_BLOCK = LRU_WIDTH // LRU_BLOCKS
LRU_C = 8.0
CONV_W = 4
CONV_PAD = (2, 1)
EVEN_IN = ATTN_WIDTH + 2 * KV_WIDTH + ATTN_WIDTH + 2 * LRU_WIDTH
EVEN_MIX = ATTN_WIDTH + LRU_WIDTH
MLSTM_HEADS = 8
MLSTM_V_DIM = D_MODEL // MLSTM_HEADS
MLSTM_QK_DIM = MLSTM_V_DIM // 2
MLSTM_WIDTH = MLSTM_HEADS * MLSTM_V_DIM
MLSTM_QK_WIDTH = MLSTM_HEADS * MLSTM_QK_DIM
MLSTM_CHUNK = 128
N_GATE_SETS = 4
ODD_IN = 2 * MLSTM_QK_WIDTH + 3 * MLSTM_WIDTH + N_GATE_SETS * MLSTM_HEADS
N_EVEN = (DEPTH + 1) // 2
N_ODD = DEPTH // 2


def rmsnorm(x, g):
    xf = x.astype(jnp.float32)
    y = xf * lax.rsqrt(jnp.mean(xf * xf, axis=-1, keepdims=True) + EPS) * g.astype(jnp.float32)
    return y.astype(x.dtype)

def split_at(t, sizes):
    idx = np.cumsum(sizes)[:-1].tolist()
    return jnp.split(t, idx, axis=-1)

def axial_angles(seq_len):
    rows = seq_len // GRID_W
    row = jnp.repeat(jnp.arange(rows), GRID_W).astype(jnp.float32)
    col = jnp.tile(jnp.arange(GRID_W), rows).astype(jnp.float32)
    inv = ROPE_THETA ** (-jnp.arange(0, ROPE_HALF, 2, dtype=jnp.float32) / ROPE_HALF)
    return row[:, None] * inv, col[:, None] * inv

def rotate_half_pairs(x, ang):
    x1, x2 = jnp.split(x, 2, axis=-1)
    c = jnp.cos(ang)[None, :, None, :]
    s = jnp.sin(ang)[None, :, None, :]
    return jnp.concatenate([x1 * c - x2 * s, x1 * s + x2 * c], axis=-1)

def axial_rope(x, ang_row, ang_col):
    xr, xc = jnp.split(x, 2, axis=-1)
    return jnp.concatenate([rotate_half_pairs(xr, ang_row), rotate_half_pairs(xc, ang_col)], axis=-1)

def block_attention(q, k, v):
    B, S, H, D = q.shape
    G = H // KV_HEADS
    nb = S // Q_BLOCK
    qb = q.reshape(B, nb, Q_BLOCK, KV_HEADS, G, D).transpose(1, 0, 3, 4, 2, 5)
    scale = HEAD_DIM ** -0.5

    def one_block(qi):
        s = jnp.einsum('bkgqd,bskd->bkgqs', qi, k) * scale
        p = jax.nn.softmax(s, axis=-1)
        return jnp.einsum('bkgqs,bskd->bkgqd', p, v)

    o = lax.map(one_block, qb)
    return o.transpose(1, 0, 4, 2, 3, 5).reshape(B, S, H * D)

def lru_combine(e1, e2):
    a1, b1 = e1
    a2, b2 = e2
    return a1 * a2, a2 * b1 + b2

def rg_lru(xc, wa, ba, wx, bx, lam, reverse):
    B, S, W = xc.shape
    xb = xc.reshape(B, S, LRU_BLOCKS, LRU_BLOCK)
    r = jax.nn.sigmoid(jnp.einsum('bsnc,ncd->bsnd', xb, wa).reshape(B, S, W) + ba)
    i = jax.nn.sigmoid(jnp.einsum('bsnc,ncd->bsnd', xb, wx).reshape(B, S, W) + bx)
    log_a = LRU_C * r * jax.nn.log_sigmoid(lam)
    a = jnp.exp(log_a)
    u = jnp.sqrt(-jnp.expm1(2.0 * log_a)) * (i * xc)
    _, h = lax.associative_scan(lru_combine, (a, u), reverse=reverse, axis=1)
    return h

def even_layer(h, w_in, w_out, q_gain, k_gain, conv_w, conv_b, wa, ba, wx, bx, lam):
    B, S, _ = h.shape
    f32 = jnp.float32
    proj = h @ w_in
    q, k, v, g_attn, x_lru, g_lru = split_at(
        proj, [ATTN_WIDTH, KV_WIDTH, KV_WIDTH, ATTN_WIDTH, LRU_WIDTH, LRU_WIDTH])
    q = rmsnorm(q.reshape(B, S, ATTN_HEADS, HEAD_DIM).astype(f32), q_gain)
    k = rmsnorm(k.reshape(B, S, KV_HEADS, HEAD_DIM).astype(f32), k_gain)
    v = v.reshape(B, S, KV_HEADS, HEAD_DIM).astype(f32)
    ang_row, ang_col = axial_angles(S)
    q = axial_rope(q, ang_row, ang_col)
    k = axial_rope(k, ang_row, ang_col)
    attn = block_attention(q, k, v)
    xc = lax.conv_general_dilated(
        x_lru, conv_w[:, None, :], window_strides=(1,), padding=[CONV_PAD],
        dimension_numbers=('NWC', 'WIO', 'NWC'), feature_group_count=LRU_WIDTH) + conv_b
    xc = xc.astype(f32)
    y = (rg_lru(xc, wa[0], ba[0], wx[0], bx[0], lam[0], reverse=False)
         + rg_lru(xc, wa[1], ba[1], wx[1], bx[1], lam[1], reverse=True))
    mix = jnp.concatenate([attn * jax.nn.silu(g_attn.astype(f32)),
                           y * jax.nn.silu(g_lru.astype(f32))], axis=-1)
    return mix.astype(h.dtype) @ w_out

def mlstm_chunkwise(q, k, v, ig, lf):
    B, H, S, dk = q.shape
    dv = v.shape[-1]
    L = MLSTM_CHUNK
    nc = S // L

    def to_chunks(t):
        return jnp.moveaxis(t.reshape((B, H, nc, L) + t.shape[3:]), 2, 0)

    mask = jnp.tril(jnp.ones((L, L), dtype=bool))

    def step(carry, inp):
        C, n, m = carry
        qi, ki, vi, ii, fi = inp
        b = jnp.cumsum(fi, axis=-1)
        logd = jnp.where(mask, b[..., :, None] - b[..., None, :] + ii[..., None, :], -jnp.inf)
        m_inter = b + m[..., None]
        m_t = jnp.maximum(m_inter, jnp.max(logd, axis=-1))
        sc = jnp.einsum('bhld,bhsd->bhls', qi, ki) * jnp.exp(logd - m_t[..., None])
        inter = jnp.exp(m_inter - m_t)
        num = jnp.einsum('bhls,bhsv->bhlv', sc, vi) + inter[..., None] * jnp.einsum('bhld,bhvd->bhlv', qi, C)
        den = jnp.sum(sc, axis=-1) + inter * jnp.einsum('bhld,bhd->bhl', qi, n)
        hout = num / jnp.maximum(jnp.abs(den), jnp.exp(-m_t))[..., None]
        b_last = b[..., -1]
        w = b_last[..., None] - b + ii
        m_new = jnp.maximum(b_last + m, jnp.max(w, axis=-1))
        decay = jnp.exp(b_last + m - m_new)
        ws = jnp.exp(w - m_new[..., None])
        C_new = decay[..., None, None] * C + jnp.einsum('bhsv,bhsd->bhvd', vi * ws[..., None], ki)
        n_new = decay[..., None] * n + jnp.einsum('bhs,bhsd->bhd', ws, ki)
        return (C_new, n_new, m_new), hout

    init = (jnp.zeros((B, H, dv, dk), jnp.float32), jnp.zeros((B, H, dk), jnp.float32),
            jnp.zeros((B, H), jnp.float32))
    _, hc = lax.scan(step, init, (to_chunks(q), to_chunks(k), to_chunks(v), to_chunks(ig), to_chunks(lf)))
    return jnp.moveaxis(hc, 0, 2).reshape(B, H, S, dv)

def odd_layer(h, w_in, gate_bias, norm_gain, w_out):
    B, S, _ = h.shape
    f32 = jnp.float32
    proj = h @ w_in
    q, k, v, o, z, gates = split_at(
        proj, [MLSTM_QK_WIDTH, MLSTM_QK_WIDTH, MLSTM_WIDTH, MLSTM_WIDTH, MLSTM_WIDTH, N_GATE_SETS * MLSTM_HEADS])

    def heads(t, d):
        return t.reshape(B, S, MLSTM_HEADS, d).transpose(0, 2, 1, 3).astype(f32)

    q = heads(q, MLSTM_QK_DIM)
    k = heads(k, MLSTM_QK_DIM) * (MLSTM_QK_DIM ** -0.5)
    v = heads(v, MLSTM_V_DIM)
    g = gates.astype(f32).reshape(B, S, N_GATE_SETS, MLSTM_HEADS) + gate_bias.astype(f32)
    i_f, i_b, f_f, f_b = g.transpose(2, 0, 3, 1)
    h_f = mlstm_chunkwise(q, k, v, i_f, jax.nn.log_sigmoid(f_f))
    flip = lambda t: jnp.flip(t, axis=2)
    h_b = flip(mlstm_chunkwise(flip(q), flip(k), flip(v), flip(i_b), flip(jax.nn.log_sigmoid(f_b))))
    hs = (h_f + h_b).transpose(0, 2, 1, 3)
    hs = jax.nn.sigmoid(o.astype(f32)).reshape(B, S, MLSTM_HEADS, MLSTM_V_DIM) * hs
    hs = rmsnorm(hs, norm_gain.reshape(MLSTM_HEADS, MLSTM_V_DIM))
    hs = hs.reshape(B, S, MLSTM_WIDTH) * jax.nn.silu(z.astype(f32))
    return hs.astype(h.dtype) @ w_out

def first_inputs(seed: int = 0) -> dict:
    key = jax.random.key(seed)
    ks = jax.random.split(key, 24)
    f32 = jnp.float32
    nrm = lambda k, shape, scale: jax.random.normal(k, shape, f32) * scale
    x = nrm(ks[0], (BATCH, SEQ, D_MODEL), 1.0)
    norm_gain = 1.0 + nrm(ks[1], (DEPTH, D_MODEL), 0.05)
    final_gain = 1.0 + nrm(ks[2], (D_MODEL,), 0.05)
    even_w_in = nrm(ks[3], (N_EVEN, D_MODEL, EVEN_IN), D_MODEL ** -0.5)
    even_w_out = nrm(ks[4], (N_EVEN, EVEN_MIX, D_MODEL), EVEN_MIX ** -0.5)
    q_norm_gain = 1.0 + nrm(ks[5], (N_EVEN, HEAD_DIM), 0.05)
    k_norm_gain = 1.0 + nrm(ks[6], (N_EVEN, HEAD_DIM), 0.05)
    conv_w = nrm(ks[7], (N_EVEN, CONV_W, LRU_WIDTH), CONV_W ** -0.5)
    conv_b = nrm(ks[8], (N_EVEN, LRU_WIDTH), 0.02)
    lru_wa = nrm(ks[9], (N_EVEN, 2, LRU_BLOCKS, LRU_BLOCK, LRU_BLOCK), LRU_BLOCK ** -0.5)
    lru_ba = nrm(ks[10], (N_EVEN, 2, LRU_WIDTH), 0.1)
    lru_wx = nrm(ks[11], (N_EVEN, 2, LRU_BLOCKS, LRU_BLOCK, LRU_BLOCK), LRU_BLOCK ** -0.5)
    lru_bx = nrm(ks[12], (N_EVEN, 2, LRU_WIDTH), 0.1)
    a0 = jax.random.uniform(ks[13], (N_EVEN, 2, LRU_WIDTH), f32, minval=0.9, maxval=0.999)
    p = a0 ** (1.0 / LRU_C)
    lru_lambda = jnp.log(p) - jnp.log1p(-p)
    odd_w_in = nrm(ks[14], (N_ODD, D_MODEL, ODD_IN), D_MODEL ** -0.5)
    i_bias = nrm(ks[15], (N_ODD, 2, MLSTM_HEADS), 0.1)
    f_bias = jnp.broadcast_to(jnp.linspace(3.0, 6.0, MLSTM_HEADS, dtype=f32), (N_ODD, 2, MLSTM_HEADS)) \
        + nrm(ks[16], (N_ODD, 2, MLSTM_HEADS), 0.1)
    odd_gate_bias = jnp.concatenate([i_bias, f_bias], axis=1)
    odd_norm_gain = 1.0 + nrm(ks[17], (N_ODD, MLSTM_WIDTH), 0.05)
    odd_w_out = nrm(ks[18], (N_ODD, MLSTM_WIDTH, D_MODEL), MLSTM_WIDTH ** -0.5)
    return {'x': x, 'norm_gain': norm_gain, 'final_gain': final_gain,
            'even_w_in': even_w_in, 'even_w_out': even_w_out,
            'q_norm_gain': q_norm_gain, 'k_norm_gain': k_norm_gain,
            'conv_w': conv_w, 'conv_b': conv_b,
            'lru_wa': lru_wa, 'lru_ba': lru_ba, 'lru_wx': lru_wx, 'lru_bx': lru_bx,
            'lru_lambda': lru_lambda,
            'odd_w_in': odd_w_in, 'odd_gate_bias': odd_gate_bias,
            'odd_norm_gain': odd_norm_gain, 'odd_w_out': odd_w_out}

def first_block(x, norm_gain, final_gain, even_w_in, even_w_out, q_norm_gain, k_norm_gain,
              conv_w, conv_b, lru_wa, lru_ba, lru_wx, lru_bx, lru_lambda,
              odd_w_in, odd_gate_bias, odd_norm_gain, odd_w_out):
    for layer in range(DEPTH):
        hn = rmsnorm(x, norm_gain[layer])
        j = layer // 2
        if layer % 2 == 0:
            out = even_layer(hn, even_w_in[j], even_w_out[j], q_norm_gain[j], k_norm_gain[j],
                             conv_w[j], conv_b[j], lru_wa[j], lru_ba[j], lru_wx[j], lru_bx[j],
                             lru_lambda[j])
        else:
            out = odd_layer(hn, odd_w_in[j], odd_gate_bias[j], odd_norm_gain[j], odd_w_out[j])
        x = x + out.astype(x.dtype)
    return rmsnorm(x, final_gain)


A_WIDTH = D_MODEL // 2
A_HEADS = A_WIDTH // HEAD_DIM
DILATED_PATTERNS = ((128, 1), (512, 4), (2048, 16))
ATTN_BLOCK = 64
NEG_INF = -1e30
B_WIDTH = D_MODEL // 2
B_CONV = 3
C_WIDTH = D_MODEL
C_GROUPS = 8
C_CHUNK = 128
AB_IN_WIDTH = 4 * A_WIDTH + 4 * B_WIDTH
SG_IN_WIDTH = 3 * C_WIDTH
N_EVEN_2 = (DEPTH + 1) // 2
N_ODD_2 = DEPTH // 2


def rms_norm(x, g):
    xf = x.astype(jnp.float32)
    y = xf * lax.rsqrt(jnp.mean(xf * xf, axis=-1, keepdims=True) + EPS)
    return (y * g.astype(jnp.float32)).astype(x.dtype)

def layer_norm(x, g, b):
    xf = x.astype(jnp.float32)
    mu = jnp.mean(xf, axis=-1, keepdims=True)
    xc = xf - mu
    y = xc * lax.rsqrt(jnp.mean(xc * xc, axis=-1, keepdims=True) + EPS)
    return (y * g.astype(jnp.float32) + b.astype(jnp.float32)).astype(x.dtype)

def ada_modulation(c, w_mod, b_mod):
    m = jax.nn.silu(c) @ w_mod + b_mod
    shift, scale, gate = jnp.split(m, 3, axis=-1)
    return shift[:, None, :], scale[:, None, :], gate[:, None, :]

def rope(t, pos):
    half = t.shape[-1] // 2
    inv = ROPE_THETA ** (-jnp.arange(half, dtype=jnp.float32) / half)
    ang = pos[:, None] * inv[None, :]
    cos = jnp.cos(ang)[None, :, None, :]
    sin = jnp.sin(ang)[None, :, None, :]
    tf = t.astype(jnp.float32)
    t1, t2 = tf[..., :half], tf[..., half:]
    out = jnp.concatenate([t1 * cos - t2 * sin, t2 * cos + t1 * sin], axis=-1)
    return out.astype(t.dtype)

def dilated_window_attention(q, k, v, dilation, radius):
    b, h, s, hd = q.shape
    sub_len = s // dilation
    n_blk = -(-sub_len // ATTN_BLOCK)
    lp = n_blk * ATTN_BLOCK
    pad = lp - sub_len

    def to_sub(t):
        return t.reshape(b, h, sub_len, dilation, hd).transpose(0, 1, 3, 2, 4)

    qs = jnp.pad(to_sub(q), ((0, 0), (0, 0), (0, 0), (0, pad), (0, 0)))
    qb = qs.reshape(b, h, dilation, n_blk, ATTN_BLOCK, hd)
    halo = ((0, 0), (0, 0), (0, 0), (ATTN_BLOCK, pad + ATTN_BLOCK), (0, 0))
    kp = jnp.pad(to_sub(k), halo)
    vp = jnp.pad(to_sub(v), halo)

    def band(t):
        return jnp.concatenate(
            [t[:, :, :, o:o + lp].reshape(b, h, dilation, n_blk, ATTN_BLOCK, hd)
             for o in (0, ATTN_BLOCK, 2 * ATTN_BLOCK)], axis=-2)

    kb, vb = band(kp), band(vp)
    blk = jnp.arange(n_blk)[:, None, None] * ATTN_BLOCK
    q_idx = blk + jnp.arange(ATTN_BLOCK)[None, :, None]
    k_idx = blk - ATTN_BLOCK + jnp.arange(3 * ATTN_BLOCK)[None, None, :]
    valid = (jnp.abs(q_idx - k_idx) <= radius) & (k_idx >= 0) & (k_idx < sub_len)

    scores = jnp.einsum('bhrnqd,bhrnkd->bhrnqk', qb, kb,
                        preferred_element_type=jnp.float32) * (hd ** -0.5)
    scores = jnp.where(valid, scores, NEG_INF)
    m = jnp.max(scores, axis=-1, keepdims=True)
    p = jnp.exp(scores - m)
    den = jnp.sum(p, axis=-1, keepdims=True)
    o = jnp.einsum('bhrnqk,bhrnkd->bhrnqd', p, vb.astype(jnp.float32)) / den
    lse = (m + jnp.log(den))[..., 0]
    o = o.reshape(b, h, dilation, lp, hd)[:, :, :, :sub_len]
    o = o.transpose(0, 1, 3, 2, 4).reshape(b, h, s, hd)
    lse = lse.reshape(b, h, dilation, lp)[..., :sub_len].transpose(0, 1, 3, 2).reshape(b, h, s)
    return o, lse

def dilated_mixture_attention(q, k, v):
    outs, lses = [], []
    for window, dilation in DILATED_PATTERNS:
        o, lse = dilated_window_attention(q, k, v, dilation, window // (2 * dilation))
        outs.append(o)
        lses.append(lse)
    w = jax.nn.softmax(jnp.stack(lses, axis=0), axis=0)
    return jnp.einsum('pbhs,pbhsd->bhsd', w, jnp.stack(outs, axis=0))

def short_conv(u, w):
    return lax.conv_general_dilated(
        u, w[:, None, :].astype(u.dtype), window_strides=(1,), padding=((1, 1),),
        dimension_numbers=('NWC', 'WIO', 'NWC'), feature_group_count=u.shape[-1])

def mixer_ab(h, w_in, conv_w, w_out):
    b, s, _ = h.shape
    proj = h @ w_in
    cuts = np.cumsum([A_WIDTH] * 4 + [B_WIDTH] * 3).tolist()
    q, k, v, z_a, u_b, g_b, g_c, z_b = jnp.split(proj, cuts, axis=-1)
    pos = jnp.arange(s, dtype=jnp.float32)
    q = rope(q.reshape(b, s, A_HEADS, HEAD_DIM), pos).transpose(0, 2, 1, 3)
    k = rope(k.reshape(b, s, A_HEADS, HEAD_DIM), pos).transpose(0, 2, 1, 3)
    v = v.reshape(b, s, A_HEADS, HEAD_DIM).transpose(0, 2, 1, 3)
    attn = dilated_mixture_attention(q, k, v)
    y_a = attn.transpose(0, 2, 1, 3).reshape(b, s, A_WIDTH).astype(h.dtype) * jax.nn.silu(z_a)
    y_b = g_b * short_conv(g_c * u_b, conv_w) * jax.nn.silu(z_b)
    return jnp.concatenate([y_a, y_b], axis=-1) @ w_out

def mixer_sgu(h, w_in, ln_g, ln_b, w_s, b_s, w_out):
    b, s, _ = h.shape
    u, v, z = jnp.split(h @ w_in, 3, axis=-1)
    u = jax.nn.gelu(u)
    v = layer_norm(jax.nn.gelu(v), ln_g, ln_b)
    v = v.reshape(b, s // C_CHUNK, C_CHUNK, C_GROUPS, C_WIDTH // C_GROUPS)
    mixed = jnp.einsum('gts,bnsgc->bntgc', w_s, v) + b_s.T[None, None, :, :, None]
    y = u * mixed.reshape(b, s, C_WIDTH) * jax.nn.silu(z)
    return y @ w_out

def second_inputs(seed: int = 0) -> dict:
    key = jax.random.key(seed)
    ks = jax.random.split(key, 20)
    D = D_MODEL

    def nrm(k, shape, scale):
        return jax.random.normal(k, shape, jnp.float32) * scale

    return {
        'x': nrm(ks[0], (BATCH, SEQ, D), 1.0),
        'c': nrm(ks[1], (BATCH, D), 1.0),
        'ab_norm_g': 1.0 + nrm(ks[2], (N_EVEN_2, D), 0.02),
        'ab_w_mod': nrm(ks[3], (N_EVEN_2, D, 3 * D), 0.5 * D ** -0.5),
        'ab_b_mod': nrm(ks[4], (N_EVEN_2, 3 * D), 0.01),
        'ab_w_in': nrm(ks[5], (N_EVEN_2, D, AB_IN_WIDTH), D ** -0.5),
        'ab_conv_w': nrm(ks[6], (N_EVEN_2, B_CONV, B_WIDTH), B_CONV ** -0.5),
        'ab_w_out': nrm(ks[7], (N_EVEN_2, A_WIDTH + B_WIDTH, D), (A_WIDTH + B_WIDTH) ** -0.5),
        'sg_norm_g': 1.0 + nrm(ks[8], (N_ODD_2, D), 0.02),
        'sg_w_mod': nrm(ks[9], (N_ODD_2, D, 3 * D), 0.5 * D ** -0.5),
        'sg_b_mod': nrm(ks[10], (N_ODD_2, 3 * D), 0.01),
        'sg_w_in': nrm(ks[11], (N_ODD_2, D, SG_IN_WIDTH), D ** -0.5),
        'sg_ln_g': 1.0 + nrm(ks[12], (N_ODD_2, C_WIDTH), 0.02),
        'sg_ln_b': nrm(ks[13], (N_ODD_2, C_WIDTH), 0.01),
        'sg_w_s': nrm(ks[14], (N_ODD_2, C_GROUPS, C_CHUNK, C_CHUNK), C_CHUNK ** -0.5),
        'sg_b_s': 1.0 + nrm(ks[15], (N_ODD_2, C_GROUPS, C_CHUNK), 0.01),
        'sg_w_out': nrm(ks[16], (N_ODD_2, C_WIDTH, D), C_WIDTH ** -0.5),
        'final_norm_g': 1.0 + nrm(ks[17], (D,), 0.02),
    }

def second_block(x, c, ab_norm_g, ab_w_mod, ab_b_mod, ab_w_in, ab_conv_w, ab_w_out,
              sg_norm_g, sg_w_mod, sg_b_mod, sg_w_in, sg_ln_g, sg_ln_b, sg_w_s, sg_b_s,
              sg_w_out, final_norm_g):
    for layer in range(DEPTH):
        i = layer // 2
        if layer % 2 == 0:
            shift, scale, gate = ada_modulation(c, ab_w_mod[i], ab_b_mod[i])
            h = rms_norm(x, ab_norm_g[i]) * (1.0 + scale) + shift
            out = mixer_ab(h, ab_w_in[i], ab_conv_w[i], ab_w_out[i])
        else:
            shift, scale, gate = ada_modulation(c, sg_w_mod[i], sg_b_mod[i])
            h = rms_norm(x, sg_norm_g[i]) * (1.0 + scale) + shift
            out = mixer_sgu(h, sg_w_in[i], sg_ln_g[i], sg_ln_b[i], sg_w_s[i], sg_b_s[i], sg_w_out[i])
        x = x + gate * out
    return rms_norm(x, final_norm_g)


_first_inputs = second_inputs


def second_inputs(seed=0):
    import zlib

    import numpy as np

    out = dict(_first_inputs(seed))
    spreads = {}
    factors = {'ab_norm_g': 7.908,
     'ab_b_mod': 7.227,
     'sg_norm_g': 64.0,
     'sg_b_mod': 7.204,
     'sg_ln_g': 64.0,
     'sg_ln_b': 64.0,
     'sg_b_s': 64.0,
     'final_norm_g': 8.213}
    for name, (base, spread) in spreads.items():
        noise = np.random.default_rng([zlib.crc32(name.encode()), seed]).standard_normal(out[name].shape)
        drawn = base * np.exp(spread * noise) if base else spread * noise
        out[name] = __import__('jax').numpy.asarray(drawn.astype(out[name].dtype))
    for name, factor in factors.items():
        out[name] = (out[name] * factor).astype(out[name].dtype)
    return out


_narrow_inputs = second_inputs


def second_inputs(seed=0):

    out = dict(_narrow_inputs(seed))
    wider = {'sg_ln_g': 4.69, 'sg_ln_b': 8.81, 'sg_b_s': 9.37, 'final_norm_g': 3.26}
    for name, times in wider.items():
        mean = out[name].mean()
        out[name] = (mean + times * (out[name] - mean)).astype(out[name].dtype)
    return out


def setup_inputs(seed=0):
    out = dict(first_inputs(seed))
    for name, value in second_inputs(seed + 1).items():
        if name != "x":
            out[name + "_2"] = value
    return out


def reference(
    x, norm_gain, final_gain, even_w_in, even_w_out, q_norm_gain, k_norm_gain, conv_w, conv_b,
    lru_wa, lru_ba, lru_wx, lru_bx, lru_lambda, odd_w_in, odd_gate_bias, odd_norm_gain,
    odd_w_out, c_2, ab_norm_g_2, ab_w_mod_2, ab_b_mod_2, ab_w_in_2, ab_conv_w_2, ab_w_out_2,
    sg_norm_g_2, sg_w_mod_2, sg_b_mod_2, sg_w_in_2, sg_ln_g_2, sg_ln_b_2, sg_w_s_2, sg_b_s_2,
    sg_w_out_2, final_norm_g_2,
):
    x = first_block(
        x, norm_gain, final_gain, even_w_in, even_w_out, q_norm_gain, k_norm_gain, conv_w,
        conv_b, lru_wa, lru_ba, lru_wx, lru_bx, lru_lambda, odd_w_in, odd_gate_bias,
        odd_norm_gain, odd_w_out,
    )
    return second_block(
        x, c_2, ab_norm_g_2, ab_w_mod_2, ab_b_mod_2, ab_w_in_2, ab_conv_w_2, ab_w_out_2,
        sg_norm_g_2, sg_w_mod_2, sg_b_mod_2, sg_w_in_2, sg_ln_g_2, sg_ln_b_2, sg_w_s_2,
        sg_b_s_2, sg_w_out_2, final_norm_g_2,
    )


_drawn_inputs = setup_inputs


def setup_inputs(seed=0):
    import zlib

    import numpy as np

    out = dict(_drawn_inputs(seed))
    spreads = {}
    factors = {'q_norm_gain': 5.43, 'k_norm_gain': 6.157}
    for name, (base, spread) in spreads.items():
        noise = np.random.default_rng([zlib.crc32(name.encode()), seed]).standard_normal(out[name].shape)
        drawn = base * np.exp(spread * noise) if base else spread * noise
        out[name] = __import__('jax').numpy.asarray(drawn.astype(out[name].dtype))
    for name, factor in factors.items():
        out[name] = (out[name] * factor).astype(out[name].dtype)
    return out
```

```python
from contextlib import ExitStack

import numpy as np
import concourse.bass as bass
from concourse import mybir

F32 = mybir.dt.float32
F32R = mybir.dt.float32r
ALU = mybir.AluOpType
ACT = mybir.ActivationFunctionType
AX = mybir.AxisListType

P = 128
D = 2048
S = 512
KT = D // P
TT = S // P
W = 512
CH = 2
NCH = KT // CH
RAW_SLOTS = 4
SPLIT_SLOTS = 2
EPS = 1e-6
HD = 128
HEADS = 8
KV_HEADS = 2
LRU_W = D // 2
LRU_TILES = LRU_W // P
LRU_C = 8.0
M_HEADS = 8
M_V = D // M_HEADS
SCALE = HD ** -0.5
MOD_BLOCKS = 3 * D // W

G_XL, G_GL, G_Q, G_GA, G_KV, G_OUT1 = 0, 2, 4, 6, 8, 9
G_MQ, G_MK, G_MV, G_MO, G_MZ, G_OUT2 = 13, 15, 17, 21, 25, 29
G_CONV, G_ATT, G_OUT3 = 33, 41, 49
G_SV, G_SU, G_SZ, G_OUT4 = 53, 57, 61, 65
GROUPS = 69
MODS = 2 * MOD_BLOCKS

PAGES = 54
MOD_RING, MOD_ACC = 49, 53
XP, XR, GATE, MACC, DIAG, TMP, JUNK = 0, 16, 24, 28, 32, 33, 37
ROWS = 41
P_XL, P_GL, P_GA, P_QKV = 0, 8, 16, 24
LW, XC, GR0, GI0, GR1, GI1, TH, EA, DV = 36, 37, 38, 39, 40, 41, 42, 44, 46
P_MQ, P_MK, P_MV, KCUR, NM, EE, PP, TRI, HCUR, MROW = 0, 8, 16, 32, 33, 35, 37, 44, 45, 47
GTOK, GW = 46, 45
MO_TMP, MO_SQ, MZ_GAIN = 32, 36, 40
P_YB, C_U, C_GU, C_B, C_Z = 0, 8, 12, 16, 20
P_QH, P_KH, P_VH, P_YA = 8, 12, 16, 20
P_SV, P_MX, S_TMP, S_G, S_B, S_BS, S_WS = 0, 16, 32, 36, 40, 44, 46


COLS = {}


def _columns():
    at = 0
    for name, n in (("norm0", KT), ("norm1", KT), ("conv_w", 4 * LRU_TILES), ("conv_b", LRU_TILES),
                    ("ba", 2 * LRU_TILES), ("bx", 2 * LRU_TILES), ("lam", 2 * LRU_TILES), ("c", KT),
                    ("norm2", KT), ("shift_b2", KT), ("scale_b2", KT), ("conv3_w", 3 * LRU_TILES),
                    ("norm3", KT), ("shift_b3", KT), ("scale_b3", KT), ("zero", KT)):
        COLS[name] = at
        at += n
    return at


NCOLS = _columns()
ROW = {}


def _rows():
    at = 0
    for name, n in (("final0", D), ("final1", D), ("gate_b2", D), ("gate_b3", D), ("m_gain", D),
                    ("ln_g", D), ("ln_b", D), ("b_s", 8 * P), ("q_gain", HD), ("k_gain", HD),
                    ("m_bias", 32)):
        ROW[name] = at
        at += n
    return at


NROWS = _rows()


class Steps:

    def __init__(self, sem, names):
        self.sem, self.names = sem, names.split() if isinstance(names, str) else names
        self.n = len(self.names)

    def at(self, name, task=0, back=0):
        return self.n * (task + 1 - back) + self.names.index(name) + 1


def build_program(nc, x_in, wall, mods, cols_d, rows_d, lru_w, gate_w, ident_d, rope_d, mask_d, tri_d,
                  ws_d, x_mid, mod_mid, out, layers=4):
    with ExitStack() as ctx:
        def sb(name, shape, dt=F32):
            return ctx.enter_context(nc.sbuf_tensor(name, shape, dt))

        def sem(name):
            return ctx.enter_context(nc.semaphore(name))

        def steps(name, names):
            return Steps(sem(name), names)

        h_hi = sb("h_hi", [P, KT, S], F32R)
        h_lo = sb("h_lo", [P, KT, S], F32R)
        w_raw = sb("w_raw", [P, RAW_SLOTS, CH * W])
        w_hi = sb("w_hi", [P, SPLIT_SLOTS, CH * W], F32R)
        w_lo = sb("w_lo", [P, SPLIT_SLOTS, CH * W], F32R)
        arena = sb("arena", [P, PAGES, W])
        cols = sb("cols", [P, NCOLS])
        ident = sb("ident", [P, P])
        zero = sb("zero", [P, 1])
        one = sb("one", [P, 1])
        eps = sb("eps", [P, 1])
        c_silu = sb("c_silu", [P, KT])
        lru_decay = sb("lru_decay", [P, 2 * LRU_TILES])
        small = sb("small", [P, 160])
        ones = sb("ones", [P, P])
        m_cols = sb("m_cols", [P, P])
        bank = [ctx.enter_context(nc.psum_tensor(f"bank{i}", [P, W], F32)) for i in range(8)]

        def page(i, n=1):
            if isinstance(i, int):
                return arena[:, i:i + n, :].rearrange("p a n -> p (a n)")
            return arena[:, bass.ds(i, n), :].rearrange("p a n -> p (a n)")

        def col(name, i=0, n=1):
            return cols[:, bass.ds(COLS[name] + i, n)]

        def row(name, n):
            return rows_d[:, ROW[name]:ROW[name] + n]

        square_sum = small[:, 0:16].rearrange("p (t n) -> p t n", n=4)
        token_sum = small[:, 16:20]
        root = small[:, 20:24]
        rstd = small[:, 24:28]
        head_sq = small[:, 28:68]
        head_rstd = small[:, 68:108]
        row_max = small[:, 108:110]
        row_bias = small[:, 110:112]
        row_sum = small[:, 112:114]
        row_rec = small[:, 114:116]
        den = small[:, 116:124]
        mod_scale = small[:, 124:140]
        mod_shift = small[:, 140:156]
        mean = small[:, 156:160]

        raw_in = [sem(f"raw_in{s}") for s in range(RAW_SLOTS)]
        w_hi_done = sem("w_hi_done")
        w_ready = sem("w_ready")
        w_used = sem("w_used")
        bank_full = sem("bank_full")
        bank_free = [sem(f"bank_free{m}") for m in range(4)]
        pool_turn = sem("pool_turn")
        h_ready = sem("h_ready")
        h_hi_done = sem("h_hi_done")
        loaded = sem("loaded")
        stored = sem("stored")
        mod_in = [sem(f"mod_in{s}") for s in range(2)]
        mod_sum = steps("mod_sum", [f"k{k}" for k in range(KT)])
        mod_out = sem("mod_out")
        setup_a = steps("setup_a", "silu abs exp ln")
        setup_v = steps("setup_v", "zero one eps sums ones min sub scale")

        FULL0, WREADY0, WUSED0 = 4, NCH, NCH - 1

        def group_written(eng, g):
            for m in range(4):
                eng.wait_ge(bank_free[m], g + 2)

        def pe_chunks(pe, g, first, last, tokens_out, h_tiles):
            for c in range(first, last):
                s = c % SPLIT_SLOTS
                pe.wait_ge(h_ready, h_tiles + CH * (c + 1))
                pe.wait_ge(w_ready, NCH * g + c + 1 + WREADY0)
                for m in range(4):
                    if c == 0:
                        pe.wait_ge(bank_free[m], g + 1)
                    for kk in range(CH):
                        k = CH * c + kk
                        if tokens_out:
                            hs = slice(m * P, (m + 1) * P)
                            ws = slice(kk * W, (kk + 1) * W)
                            pairs = ((h_hi[:, k, hs], w_hi[:, s, ws]), (h_hi[:, k, hs], w_lo[:, s, ws]),
                                     (h_lo[:, k, hs], w_hi[:, s, ws]))
                        else:
                            ws = slice(kk * W + m * P, kk * W + (m + 1) * P)
                            pairs = ((w_hi[:, s, ws], h_hi[:, k, :]), (w_hi[:, s, ws], h_lo[:, k, :]),
                                     (w_lo[:, s, ws], h_hi[:, k, :]))
                        for n, (a, b) in enumerate(pairs):
                            mm = nc.tensor.matmul(bank[m][:], a, b, start=(k == 0 and n == 0),
                                                  stop=(k == KT - 1 and n == 2))
                    if c == NCH - 1:
                        mm.then_inc(bank_full, 1)
                if c < NCH - 1:
                    mm.then_inc(w_used, 1)

        def pe_group(pe, g, tokens_out, h_tiles):
            pe_chunks(pe, g, 0, NCH, tokens_out, h_tiles)

        def full(eng, g, m):
            eng.wait_ge(bank_full, 4 * g + m + 1 + FULL0)

        def act_evac(act, g, dst, func=ACT.Copy, scale=1.0, before=None):
            for m in range(4):
                full(act, g, m)
                nc.scalar.activation(dst(m), bank[m][:], func, scale=scale).then_inc(bank_free[m], 1)

        def dve_mod(v, n):
            v.wait_ge(mod_out, 16 * (n + 1))
            for c in range(NCH):
                v.wait_ge(mod_in[c % 2], 16 * (4 * n + c // 2 + 1))
                for kk in range(CH):
                    k = CH * c + kk
                    slab = page(MOD_RING + 2 * (c % 2) + kk)
                    if k == 0:
                        nc.vector.tensor_scalar(page(MOD_ACC), slab, c_silu[:, 0:1], None,
                                                ALU.mult).then_inc(mod_sum.sem, 1)
                    else:
                        v.wait_ge(mod_sum.sem, mod_sum.at(f"k{k - 1}", n))
                        nc.vector.scalar_tensor_tensor(page(MOD_ACC), slab, c_silu[:, k:k + 1], page(MOD_ACC),
                                                       ALU.mult, ALU.add).then_inc(mod_sum.sem, 1)

        def act_mod(act, n):
            act.wait_ge(mod_sum.sem, mod_sum.at(f"k{KT - 1}", n))
            act.dma_start(mod_mid[bass.ds(n, 1)].rearrange("a p n -> p (a n)"), page(MOD_ACC)).then_inc(mod_out, 16)

        tile_val = sem("tile_val")
        tile_turned = sem("tile_turned")
        turns = {0: 0, 2: 1, 3: 2, 4: 3, 6: 4}

        def pe_turn(pe, r, lhs, diag):
            q = turns[r]
            for f in range(KT):
                if f >= 4:
                    pe.wait_ge(tile_val, KT * q + f - 3)
                for t in range(TT):
                    dst = bank[4 + f % 4][:, t * P:(t + 1) * P]
                    if diag is None:
                        mm = nc.tensor.transpose(dst, lhs(f, t), ident[:])
                    else:
                        mm = nc.tensor.matmul(dst, lhs(f, t), diag[:, t, :], start=True, stop=True)
                mm.then_inc(tile_turned, 1)

        def act_turn(act, r, tmp, gain=None, shift=None):
            q = turns[r]
            for f in range(KT):
                act.wait_ge(tile_turned, KT * q + f + 1)
                if f >= 4:
                    act.wait_ge(h_ready, KT * r + f - 3)
                if gain is None:
                    nc.scalar.copy(page(tmp + f % 4), bank[4 + f % 4][:]).then_inc(tile_val, 1)
                else:
                    nc.scalar.activation(page(tmp + f % 4), bank[4 + f % 4][:], ACT.Identity,
                                         bias=shift(f), scale=gain(f)).then_inc(tile_val, 1)

        def dve_turn(v, r, tmp):
            q = turns[r]
            for f in range(KT):
                v.wait_ge(tile_val, KT * q + f + 1)
                nc.vector.tensor_copy(h_hi[:, f, :], page(tmp + f % 4)).then_inc(h_hi_done, 1)
                v.wait_ge(h_hi_done, KT * r + f + 1)
                nc.vector.tensor_tensor(h_lo[:, f, :], page(tmp + f % 4), h_hi[:, f, :].bitcast(F32),
                                        ALU.subtract).then_inc(h_ready, 1)

        def act_split(act, src):
            for f in range(KT):
                nc.scalar.copy(h_hi[:, f, :], page(src(f))).then_inc(h_hi_done, 1)

        def dve_split(v, r, src):
            for f in range(KT):
                v.wait_ge(h_hi_done, KT * r + f + 1)
                nc.vector.tensor_tensor(h_lo[:, f, :], page(src(f)), h_hi[:, f, :].bitcast(F32),
                                        ALU.subtract).then_inc(h_ready, 1)

        diag = page(DIAG).rearrange("p (t n) -> p t n", n=P)
        xp = arena[:, XP:XP + 16, :].rearrange("p a n -> p (a n)").rearrange("p (t n) -> p t n", n=D)
        norm_a = steps("norm_a", "root")
        norm_v = steps("norm_v", "total rstd d0 d1 d2 d3")

        def act_norm(act, q):
            act.wait_ge(norm_v.sem, norm_v.at("total", q))
            nc.scalar.activation(root, token_sum, ACT.Sqrt, bias=eps[:], scale=1.0 / D).then_inc(norm_a.sem, 1)

        def dve_norm(v, q):
            nc.vector.tensor_reduce(token_sum, square_sum, AX.X, ALU.add).then_inc(norm_v.sem, 1)
            v.wait_ge(norm_a.sem, norm_a.at("root", q))
            nc.vector.reciprocal(rstd, root).then_inc(norm_v.sem, 1)
            v.wait_ge(norm_v.sem, norm_v.at("rstd", q))
            for t in range(TT):
                nc.vector.tensor_scalar(diag[:, t, :], ident[:], rstd[:, t:t + 1], None,
                                        ALU.mult).then_inc(norm_v.sem, 1)

        mod_loaded = sem("mod_loaded")
        modc_p = steps("modc_p", "sum")
        modc_v = steps("modc_v", "shift scale one gain")
        gate_loaded = sem("gate_loaded")
        modg_p = steps("modg_p", "g0 g1 g2 g3")
        modg_v = steps("modg_v", "g0 g1 g2 g3")
        MODC = 16

        def act_load_mod(act, q):
            act.wait_ge(mod_out, 16 * (MODS + 1))
            act.dma_start(arena[:, MODC:MODC + 8, :],
                          mod_mid[q * MOD_BLOCKS:q * MOD_BLOCKS + 8].rearrange("b p n -> p b n")).then_inc(mod_loaded, 16)

        def pe_mod_cols(pe, q):
            pe.wait_ge(mod_loaded, 16 * (q + 1))
            for b in range(8):
                for j in range(W // P):
                    mm = nc.tensor.matmul(bank[4][:, 4 * b + j:4 * b + j + 1], page(MODC + b)[:, j * P:(j + 1) * P],
                                          one[:], start=True, stop=True)
            mm.then_inc(modc_p.sem, 1)
            pe.wait_ge(modc_v.sem, modc_v.at("scale", q))

        def dve_mod_cols(v, q):
            v.wait_ge(modc_p.sem, modc_p.at("sum", q))
            nc.vector.tensor_tensor(mod_shift, bank[4][:, 0:KT], col(f"shift_b{q + 2}", 0, KT),
                                    ALU.add).then_inc(modc_v.sem, 1)
            nc.vector.tensor_tensor(mod_scale, bank[4][:, KT:2 * KT], col(f"scale_b{q + 2}", 0, KT),
                                    ALU.add).then_inc(modc_v.sem, 1)
            v.wait_ge(modc_v.sem, modc_v.at("scale", q))
            nc.vector.tensor_scalar(mod_scale, mod_scale, 1.0, None, ALU.add).then_inc(modc_v.sem, 1)
            v.wait_ge(modc_v.sem, modc_v.at("one", q))
            nc.vector.tensor_tensor(mod_scale, mod_scale, col(f"norm{q + 2}", 0, KT), ALU.mult).then_inc(modc_v.sem, 1)

        def act_load_gate(act, lay):
            q = lay - 2
            act.dma_start(arena[:, MACC:MACC + 4, :],
                          mod_mid[q * MOD_BLOCKS + 8:(q + 1) * MOD_BLOCKS].rearrange("b p n -> p b n")).then_inc(gate_loaded, 16)
            act.dma_start(page(GATE, 4), row(f"gate_b{lay}", D)).then_inc(gate_loaded, 16)

        def pe_gate(pe, lay):
            pe.wait_ge(gate_loaded, 32 * (lay - 1))
            for n in range(4):
                nc.tensor.matmul(bank[4 + n][:], ones[:], page(MACC + n), start=True, stop=True).then_inc(modg_p.sem, 1)

        def dve_gate(v, lay):
            for n in range(4):
                v.wait_ge(modg_p.sem, modg_p.at(f"g{n}", lay - 2))
                nc.vector.tensor_tensor(page(GATE + n), bank[4 + n][:], page(GATE + n), ALU.add).then_inc(modg_v.sem, 1)
            v.wait_ge(modg_v.sem, modg_v.at("g3", lay - 2))

        old_in = sem("old_in")
        res_v = steps("res_v", "s0 s1 s2 s3")
        res_a = steps("res_a", "q0 q1 q2 q3")
        new_out = sem("new_out")
        res_task = {0: 0, 1: 0, 2: 0, 3: 4}

        def cols_of(dram, n):
            return dram.rearrange("(t p) n -> p t n", p=P)[:, :, n * W:(n + 1) * W]

        def act_residual(act, lay, g0, src, gated, store):
            def summed(n, t):
                if gated:
                    act.wait_ge(res_v.sem, res_v.at(f"s{t}", res_task[lay] + n))
                else:
                    act.wait_ge(bank_free[t], g0 + n + 2)

            act.wait_ge(h_ready, KT * (2 * lay + 2))
            act.wait_ge(new_out, (0, 64, 80, 144)[lay])
            if gated:
                act_load_gate(act, lay)
            if lay == 1:
                act_load_final(act, 0)
            if lay == 3:
                act_load_final(act, 1)
            for n in range(4):
                for ahead in ((0, 1) if n == 0 else (n + 1,) if n < 3 else ()):
                    act.dma_start(arena[:, XR + 4 * (ahead % 2):XR + 4 * (ahead % 2) + 4, :],
                                  cols_of(src, ahead)).then_inc(old_in, 16)
                    act.wait_ge(old_in, 16 * (4 * lay + ahead + 1))
                if g0 + n < MODS:
                    act_mod(act, g0 + n)
                for t in range(TT):
                    summed(n, t)
                    act.wait_ge(res_a.sem, res_a.at(f"q{t - 1}", 4 * lay + n) if t else
                                res_a.at("q3", 4 * lay + n, back=1))
                    nc.scalar.activation(page(JUNK), xp[:, t, n * W:(n + 1) * W], ACT.Square,
                                         accum_out=square_sum[:, t, n:n + 1]).then_inc(res_a.sem, 1)
                if store:
                    act.dma_start(cols_of(x_mid, n), xp[:, :, n * W:(n + 1) * W]).then_inc(new_out, 16)

        def dve_residual(v, lay, g0, gated):
            if gated:
                dve_gate(v, lay)
            for n in range(4):
                if g0 + n < MODS:
                    dve_mod(v, g0 + n)
                v.wait_ge(old_in, 16 * (4 * lay + n + 1))
                for t in range(TT):
                    new = xp[:, t, n * W:(n + 1) * W]
                    old = page(XR + 4 * (n % 2) + t)
                    full(v, g0 + n, t)
                    if gated:
                        v.wait_ge(res_v.sem, res_v.at(f"s{t}", res_task[lay] + n, back=1))
                        nc.vector.tensor_tensor(page(TMP + t), bank[t][:], page(GATE + n),
                                                ALU.mult).then_inc(bank_free[t], 1)
                    else:
                        nc.vector.tensor_tensor(new, bank[t][:], old, ALU.add).then_inc(bank_free[t], 1)
                if gated:
                    for t in range(TT):
                        v.wait_ge(bank_free[t], g0 + n + 2)
                        nc.vector.tensor_tensor(xp[:, t, n * W:(n + 1) * W], page(TMP + t),
                                                page(XR + 4 * (n % 2) + t), ALU.add).then_inc(res_v.sem, 1)

        final_in = sem("final_in")
        final_v = steps("final_v", "clear r0 r1 r2 r3")
        final_a = steps("final_a", "q0 q1 q2 q3")

        def act_load_final(act, q):
            act.dma_start(page(ROWS, 4), row(f"final{q}", D)).then_inc(final_in, 16)

        def dve_final(v, q):
            v.wait_ge(norm_v.sem, norm_v.at("total", 2 + 3 * q))
            nc.vector.memset(small[:, 0:16], 0.0).then_inc(final_v.sem, 1)
            v.wait_ge(final_in, 16 * (q + 1))
            for t in range(TT):
                nc.vector.scalar_tensor_tensor(xp[:, t, :], xp[:, t, :], rstd[:, t:t + 1], page(ROWS, 4),
                                               ALU.mult, ALU.mult).then_inc(final_v.sem, 1)

        def act_final(act, q):
            act.wait_ge(final_v.sem, final_v.at("clear", q))
            for t in range(TT):
                act.wait_ge(final_v.sem, final_v.at(f"r{t}", q))
                act.wait_ge(final_a.sem, final_a.at(f"q{t - 1}", q) if t else final_a.at("q3", q, back=1))
                nc.scalar.activation(page(JUNK, 4), xp[:, t, :], ACT.Square,
                                     accum_out=square_sum[:, t, 0:1]).then_inc(final_a.sem, 1)

        lru_in = sem("lru_in")
        lru_p = steps("lru_p", "a0 x0 a1 x1")
        lru_a = steps("lru_a", "sr0 si0 sr1 si1 tanh0 exp0 tanh1 exp1 sqrt0 sqrt1")
        lru_v = steps("lru_v", "c2 c0 c1 c3 La0 La1 ix0 ix1 den0 den1 rec0 rec1 v0 v1 u0 u1 h0 h1 y yg")

        def pe_lru(pe, j):
            pe.wait_ge(lru_in, 16 * (j + 1))
            pe.wait_ge(lru_v.sem, lru_v.at("c3", j))
            pe.wait_ge(lru_a.sem, lru_a.at("si1", j, back=1))
            for n in range(4):
                nc.tensor.matmul(bank[4 + n][:], page(LW)[:, n * P:(n + 1) * P], page(XC),
                                 start=True, stop=True).then_inc(lru_p.sem, 1)

        def act_lru(act, j):
            act.wait_ge(lru_p.sem, lru_p.at("x1", j, back=1))
            act.dma_start(page(LW), lru_w[bass.ds(j, 1)].rearrange("a p n -> p (a n)")).then_inc(lru_in, 16)
            act.wait_ge(lru_v.sem, lru_v.at("yg", j, back=1))
            for n, (bias, dst) in enumerate((("ba", GR0), ("bx", GI0), ("ba", GR1), ("bx", GI1))):
                act.wait_ge(lru_p.sem, lru_p.at(("a0", "x0", "a1", "x1")[n], j))
                nc.scalar.activation(page(dst), bank[4 + n][:], ACT.Sigmoid,
                                     bias=col(bias, LRU_TILES * (n // 2) + j)).then_inc(lru_a.sem, 1)
            for d, gr in ((0, GR0), (1, GR1)):
                act.wait_ge(lru_v.sem, lru_v.at(f"La{d}", j))
                nc.scalar.activation(page(TH + d), page(gr), ACT.Tanh).then_inc(lru_a.sem, 1)
                nc.scalar.activation(page(EA + d), page(gr), ACT.Exp).then_inc(lru_a.sem, 1)
            for d in range(2):
                act.wait_ge(lru_v.sem, lru_v.at(f"v{d}", j))
                nc.scalar.activation(page(DV + d), page(DV + d), ACT.Sqrt).then_inc(lru_a.sem, 1)

        def dve_lru(v, j):
            own = lambda name: v.wait_ge(lru_v.sem, lru_v.at(name, j))
            from_act = lambda name: v.wait_ge(lru_a.sem, lru_a.at(name, j))
            x, xc = page(P_XL + j), page(XC)
            cw = lambda w: col("conv_w", LRU_TILES * w + j)
            nc.vector.tensor_scalar(xc, x, cw(2), col("conv_b", j), ALU.mult, ALU.add).then_inc(lru_v.sem, 1)
            own("c2")
            nc.vector.scalar_tensor_tensor(xc[:, 2:S], arena_cols(P_XL + j, 0, S - 2), cw(0), xc[:, 2:S],
                                           ALU.mult, ALU.add).then_inc(lru_v.sem, 1)
            own("c0")
            nc.vector.scalar_tensor_tensor(xc[:, 1:S], arena_cols(P_XL + j, 0, S - 1), cw(1), xc[:, 1:S],
                                           ALU.mult, ALU.add).then_inc(lru_v.sem, 1)
            own("c1")
            nc.vector.scalar_tensor_tensor(xc[:, 0:S - 1], arena_cols(P_XL + j, 1, S), cw(3), xc[:, 0:S - 1],
                                           ALU.mult, ALU.add).then_inc(lru_v.sem, 1)
            own("c3")
            for d, gr in ((0, GR0), (1, GR1)):
                from_act(f"sr{d}")
                nc.vector.tensor_scalar(page(gr), page(gr), lru_decay[:, bass.ds(LRU_TILES * d + j, 1)], None,
                                        ALU.mult).then_inc(lru_v.sem, 1)
            for d, gi in ((0, GI0), (1, GI1)):
                from_act(f"si{d}")
                nc.vector.tensor_tensor(page(gi), page(gi), xc, ALU.mult).then_inc(lru_v.sem, 1)
            for d in range(2):
                from_act(f"tanh{d}")
                nc.vector.tensor_scalar(page(DV + d), page(TH + d), -1.0, 1.0, ALU.mult,
                                        ALU.add).then_inc(lru_v.sem, 1)
            for d in range(2):
                own(f"den{d}")
                nc.vector.reciprocal(page(DV + d), page(DV + d)).then_inc(lru_v.sem, 1)
            for d in range(2):
                own(f"rec{d}")
                nc.vector.scalar_tensor_tensor(page(DV + d), page(TH + d), -2.0, page(DV + d), ALU.mult,
                                               ALU.mult).then_inc(lru_v.sem, 1)
            for d, gi in ((0, GI0), (1, GI1)):
                from_act(f"sqrt{d}")
                own(f"ix{d}")
                nc.vector.tensor_tensor(page(gi), page(gi), page(DV + d), ALU.mult).then_inc(lru_v.sem, 1)
            for d, gr, gi in ((0, GR0, GI0), (1, GR1, GI1)):
                own(f"u{d}")
                turn = slice(None, None, -1) if d else slice(None)
                nc.vector.tensor_tensor_scan(page(gr)[:, turn], page(EA + d)[:, turn], page(gi)[:, turn], 0.0,
                                             ALU.mult, ALU.add).then_inc(lru_v.sem, 1)
            own("h1")
            nc.vector.tensor_tensor(page(GR0), page(GR0), page(GR1), ALU.add).then_inc(lru_v.sem, 1)
            own("y")
            nc.vector.tensor_tensor(page(P_XL + j), page(GR0), page(P_GL + j), ALU.mult).then_inc(lru_v.sem, 1)

        def arena_cols(pg, a, b):
            if isinstance(pg, int):
                return arena[:, pg, a:b]
            return arena[:, bass.ds(pg, 1), a:b].rearrange("p a n -> p (a n)")

        class Attention:

            def __init__(self, tag, normed, masked, lo, hi, pages):
                self.normed, self.masked, self.lo, self.hi, self.pg = normed, masked, lo, hi, pages
                rot = "n g A Bl Bh r" if normed else "A Bl Bh r"
                self.kv_v = steps(tag + "_kv_v", rot + " vc")
                self.kv_p = steps(tag + "_kv_p", "turned")
                self.kv_a = steps(tag + "_kv_a", "kT")
                self.q_v = steps(tag + "_q_v", rot)
                score = ["add{0}", "max{0}", "bias{0}"] if masked else ["max{0}", "bias{0}"]
                names = []
                for t in range(TT):
                    names += [x.format(t) for x in score]
                    names += [f"rec{t - 1}", f"norm{t - 1}"] if t else []
                self.s_v = steps(tag + "_s_v", names + [f"rec{TT - 1}", f"norm{TT - 1}", "gate"])
                self.p = steps(tag + "_p", "q s0 s1 t0 s2 t1 s3 t2 t3 o")
                self.a = steps(tag + "_a", "qT e0 e1 T0 e2 T1 e3 T2 T3")

            def rotate(self, v, st, task, src, dst, rs, gain):
                pg = self.pg
                tok = lambda p: page(p).rearrange("p (t n) -> p t n", n=HD)
                x = src
                if self.normed:
                    nc.vector.tensor_tensor(tok(pg["X"]), x, rs, ALU.mult).then_inc(st.sem, 1)
                    v.wait_ge(st.sem, st.at("n", task))
                    nc.vector.tensor_tensor(tok(pg["X"]), tok(pg["X"]), gain, ALU.mult).then_inc(st.sem, 1)
                    v.wait_ge(st.sem, st.at("g", task))
                    x = tok(pg["X"])
                nc.vector.tensor_tensor(tok(pg["A"]), x, tok(pg["C"]), ALU.mult).then_inc(st.sem, 1)
                lo, hi = self.lo, self.hi
                nc.vector.tensor_tensor(lo(tok(pg["B"])), hi(x), lo(tok(pg["S"])), ALU.mult).then_inc(st.sem, 1)
                nc.vector.tensor_tensor(hi(tok(pg["B"])), lo(x), hi(tok(pg["S"])), ALU.mult).then_inc(st.sem, 1)
                v.wait_ge(st.sem, st.at("Bh", task))
                nc.vector.tensor_tensor(page(dst), page(pg["A"]), page(pg["B"]), ALU.add).then_inc(st.sem, 1)

            def dve_kv(self, v, i, head, k, val, rs=None, gain=None):
                v.wait_ge(self.s_v.sem, self.s_v.at("gate", head, back=1))
                v.wait_ge(self.kv_p.sem, self.kv_p.at("turned", i, back=1))
                self.rotate(v, self.kv_v, i, k, self.pg["kcur"], rs, gain)
                nc.vector.tensor_copy(page(self.pg["vcur"]).rearrange("p (t n) -> p t n", n=HD),
                                      val).then_inc(self.kv_v.sem, 1)

            def dve_q(self, v, i, kv, q, rs=None, gain=None):
                v.wait_ge(self.kv_v.sem, self.kv_v.at("vc", kv))
                v.wait_ge(self.p.sem, self.p.at("q", i, back=1))
                self.rotate(v, self.q_v, i, q, self.pg["qcur"], rs, gain)

            def pe_kv(self, pe, i, head):
                pe.wait_ge(self.kv_v.sem, self.kv_v.at("r", i))
                pe.wait_ge(self.s_v.sem, self.s_v.at("gate", head, back=1))
                for t in range(TT):
                    mm = nc.tensor.transpose(bank[4][:, t * P:(t + 1) * P],
                                             page(self.pg["kcur"])[:, t * P:(t + 1) * P], ident[:])
                mm.then_inc(self.kv_p.sem, 1)

            def act_kv(self, act, i):
                act.wait_ge(self.kv_p.sem, self.kv_p.at("turned", i))
                nc.scalar.copy(page(self.pg["kT"]), bank[4][:]).then_inc(self.kv_a.sem, 1)

            def pe_head(self, pe, i, kv):
                pg, a, sv = self.pg, self.a, self.s_v
                score = lambda t: nc.tensor.matmul(bank[5 + t % 2][:], page(pg["qT"])[:, t * P:(t + 1) * P],
                                                   page(pg["kT"]), start=True, stop=True)

                def turn(t):
                    pe.wait_ge(sv.sem, sv.at(f"norm{t}", i))
                    pe.wait_ge(a.sem, a.at(f"T{t - 1}", i) if t else a.at("T3", i, back=1))
                    for k in range(TT):
                        mm = nc.tensor.transpose(bank[7][:, k * P:(k + 1) * P],
                                                 page(pg["P"] + t % 2)[:, k * P:(k + 1) * P], ident[:])
                    mm.then_inc(self.p.sem, 1)

                pe.wait_ge(self.kv_a.sem, self.kv_a.at("kT", kv))
                pe.wait_ge(self.q_v.sem, self.q_v.at("r", i))
                pe.wait_ge(sv.sem, sv.at("gate", i, back=1))
                for t in range(TT):
                    mm = nc.tensor.transpose(bank[4][:, t * P:(t + 1) * P],
                                             page(pg["qcur"])[:, t * P:(t + 1) * P], ident[:])
                mm.then_inc(self.p.sem, 1)
                pe.wait_ge(a.sem, a.at("qT", i))
                for t in range(TT):
                    if t >= 2:
                        pe.wait_ge(a.sem, a.at(f"e{t - 2}", i))
                        if self.masked:
                            pe.wait_ge(sv.sem, sv.at(f"add{t - 2}", i))
                    score(t).then_inc(self.p.sem, 1)
                    if t >= 1:
                        turn(t - 1)
                turn(3)
                pe.wait_ge(a.sem, a.at("T3", i))
                pe.wait_ge(self.kv_v.sem, self.kv_v.at("vc", kv))
                for k in range(TT):
                    mm = nc.tensor.matmul(bank[4][:], page(pg["vcur"])[:, k * P:(k + 1) * P], page(pg["PT"] + k),
                                          start=(k == 0), stop=(k == TT - 1))
                mm.then_inc(self.p.sem, 1)

            def act_head(self, act, i):
                pg, p, sv = self.pg, self.p, self.s_v

                def turned(t):
                    act.wait_ge(p.sem, p.at(f"t{t}", i))
                    dst = arena[:, pg["PT"]:pg["PT"] + TT, t * P:(t + 1) * P]
                    nc.scalar.copy(dst, bank[7][:].rearrange("p (k n) -> p k n", n=P)).then_inc(self.a.sem, 1)

                act.wait_ge(p.sem, p.at("q", i))
                nc.scalar.copy(page(pg["qT"]), bank[4][:]).then_inc(self.a.sem, 1)
                for t in range(TT):
                    act.wait_ge(sv.sem, sv.at(f"bias{t}", i))
                    if t >= 2:
                        act.wait_ge(p.sem, p.at(f"t{t - 2}", i))
                    src = page(pg["A"] + t % 2) if self.masked else bank[5 + t % 2][:]
                    nc.scalar.activation(page(pg["P"] + t % 2), src, ACT.Exp, bias=row_bias[:, t % 2:t % 2 + 1],
                                         scale=SCALE, accum_out=row_sum[:, t % 2:t % 2 + 1]).then_inc(self.a.sem, 1)
                    if t >= 1:
                        turned(t - 1)
                turned(3)

            def dve_head(self, v, i, gated):
                pg, p, sv = self.pg, self.p, self.s_v

                def norm(t):
                    b = t % 2
                    v.wait_ge(self.a.sem, self.a.at(f"e{t}", i))
                    nc.vector.reciprocal(row_rec[:, b:b + 1], row_sum[:, b:b + 1]).then_inc(sv.sem, 1)
                    v.wait_ge(sv.sem, sv.at(f"rec{t}", i))
                    nc.vector.tensor_scalar(page(pg["P"] + b), page(pg["P"] + b), row_rec[:, b:b + 1], None,
                                            ALU.mult).then_inc(sv.sem, 1)

                for t in range(TT):
                    b = t % 2
                    v.wait_ge(p.sem, p.at(f"s{t}", i))
                    src = bank[5 + b][:]
                    if self.masked:
                        nc.vector.tensor_tensor(page(pg["A"] + b), src, page(pg["mask"] + t), ALU.add).then_inc(sv.sem, 1)
                        v.wait_ge(sv.sem, sv.at(f"add{t}", i))
                        src = page(pg["A"] + b)
                    nc.vector.tensor_reduce(row_max[:, b:b + 1], src, AX.X, ALU.max).then_inc(sv.sem, 1)
                    v.wait_ge(sv.sem, sv.at(f"max{t}", i))
                    nc.vector.tensor_scalar(row_bias[:, b:b + 1], row_max[:, b:b + 1], -SCALE, None,
                                            ALU.mult).then_inc(sv.sem, 1)
                    if t:
                        norm(t - 1)
                norm(TT - 1)
                v.wait_ge(p.sem, p.at("o", i))
                nc.vector.tensor_tensor(gated, bank[4][:], gated, ALU.mult).then_inc(sv.sem, 1)

        def halves(n, first):
            def pick(ap):
                if 2 * n == HD:
                    return ap[:, :, 0:n] if first else ap[:, :, n:]
                v4 = ap.rearrange("p t (b h e) -> p t b h e", h=2, e=n)
                return v4[:, :, :, 0 if first else 1, :]
            return pick

        att1 = Attention("att1", True, False, halves(HD // 4, True), halves(HD // 4, False),
                         dict(C=36, S=37, A=38, B=39, qcur=40, kcur=41, vcur=42, qT=43, kT=44, P=45, X=47, PT=8))
        att3 = Attention("att3", False, True, halves(HD // 2, True), halves(HD // 2, False),
                         dict(C=28, S=29, A=30, B=31, qcur=33, kcur=34, vcur=35, qT=36, kT=37, P=38, PT=40, mask=44))

        QK = HEADS + KV_HEADS
        qkv = arena[:, P_QKV:P_QKV + 12, :].rearrange("p a n -> p (a n)").rearrange("p (t n) -> p t n", t=TT)
        gains = page(12)[:, 0:2 * HD]
        qk_v = steps("qk_v", "q0 r0 q1 r1 q2 r2 q3 r3 rec")
        qk_a = steps("qk_a", "root")
        rope_in = sem("rope_in")
        head_sq3 = head_sq[:, 0:TT * QK].rearrange("p (t n) -> p t n", t=TT)
        head_rs3 = head_rstd[:, 0:TT * QK].rearrange("p (t n) -> p t n", t=TT)

        def act_load_rope(act, lay, att):
            act.dma_start(page(att.pg["C"], 2), rope_d[lay]).then_inc(rope_in, 16)

        def dve_qk_stats(v):
            for t in range(TT):
                sq = page(13, 3)[:, 0:QK * HD]
                if t:
                    v.wait_ge(qk_v.sem, qk_v.at(f"r{t - 1}"))
                nc.vector.tensor_tensor(sq, qkv[:, t, 0:QK * HD], qkv[:, t, 0:QK * HD], ALU.mult).then_inc(qk_v.sem, 1)
                v.wait_ge(qk_v.sem, qk_v.at(f"q{t}"))
                nc.vector.tensor_reduce(head_sq3[:, t, :], sq.rearrange("p (h n) -> p h n", n=HD), AX.X,
                                        ALU.add).then_inc(qk_v.sem, 1)
            v.wait_ge(qk_a.sem, qk_a.at("root"))
            nc.vector.reciprocal(head_rstd[:, 0:TT * QK], head_rstd[:, 0:TT * QK]).then_inc(qk_v.sem, 1)
            v.wait_ge(qk_v.sem, qk_v.at("rec"))

        def head_cols(x, base, h):
            return x[:, :, bass.ds(base + h * HD, HD)]

        def rs_of(h):
            return head_rs3[:, :, bass.ds(h, 1)].to_broadcast([P, TT, HD])

        def gain_of(n):
            g = gains[:, n * HD:(n + 1) * HD]
            return g.rearrange("p (o n) -> p o n", o=1).to_broadcast([P, TT, HD])

        v3 = arena[:, P_MV:P_MV + 16, :].rearrange("p a n -> p (a n)").rearrange("p (t n) -> p t n", t=TT)
        gate_in = sem("gate_in")
        tri_in = sem("tri_in")
        gain_in = sem("gain_in")
        gate_p = steps("gate_p", "tok rows cols")
        gate_a = steps("gate_a", "i f abs exp ln em")
        gate_v = steps("gate_v", "bias lf Ff Fb g Mf Mb m cols")
        m_p = steps("m_p", "Mf Mb s0 s1 s2 s3 den n0 n1 n2 n3")
        m_a = steps("m_a", "k nf nb xf0 xb0 xf1 xb1 xf2 xb2 xf3 xb3 c0 c1 c2 c3 back")
        m_v = steps("m_v", ["Mh"] + [f"{x}{i}" for i in range(TT) for x in ("ef", "eb", "pf", "pb", "mf", "mb")]
                    + "dcopy dabs dmax drec n0 n1 n2 n3".split())
        o_v = steps("o_v", [f"{x}{t}" for t in range(TT) for x in "gsr"])
        z_v = steps("z_v", [f"{x}{t}" for t in range(TT) for x in "nwz"])
        m_root = sem("m_root")
        m_rec = sem("m_rec")
        gtok = page(GTOK)
        rows8 = lambda p: arena[0:8, p:p + 2, :].rearrange("p a n -> p (a n)")
        row8 = lambda p: arena[0:8, p, :]
        R_I, R_F, R_L, R_S, R_G = 33, 35, 37, 39, 41
        back = slice(None, None, -1)

        def pe_gates(pe):
            pe.wait_ge(gate_in, 32)
            for t in range(TT):
                for part in (h_hi, h_lo):
                    for k in range(KT):
                        mm = nc.tensor.matmul(bank[4][:, t * 32:(t + 1) * 32],
                                              part[:, k, t * P:(t + 1) * P].bitcast(F32),
                                              page(GW)[:, k * 32:(k + 1) * 32],
                                              start=(k == 0 and part is h_hi), stop=(k == KT - 1 and part is h_lo))
            mm.then_inc(gate_p.sem, 1)
            pe.wait_ge(gate_v.sem, gate_v.at("bias"))
            for n in range(4):
                for t in range(TT):
                    mm = nc.tensor.transpose(bank[4 + n][0:8, t * P:(t + 1) * P],
                                             gtok[:, t * 32 + 8 * n:t * 32 + 8 * n + 8], ident[:])
            mm.then_inc(gate_p.sem, 1)

        def pe_gate_cols(pe):
            pe.wait_ge(gate_v.sem, gate_v.at("Mb"))
            pe.wait_ge(gate_a.sem, gate_a.at("em"))
            for n, src in enumerate((R_G, R_G + 1, R_L, R_L + 1)):
                for t in range(TT):
                    mm = nc.tensor.transpose(bank[4][:, n * 32 + t * 8:n * 32 + t * 8 + 8],
                                             row8(src)[:, t * P:(t + 1) * P], ident[0:8, 0:8])
            mm.then_inc(gate_p.sem, 1)

        def act_gates(act):
            act.wait_ge(gate_p.sem, gate_p.at("rows"))
            for n, dst in enumerate((R_I, R_F)):
                nc.scalar.copy(row8(dst), bank[4 + 2 * n][0:8, :])
                nc.scalar.copy(row8(dst + 1), bank[5 + 2 * n][0:8, :]).then_inc(gate_a.sem, 1)
            act.wait_ge(gate_a.sem, gate_a.at("f"))
            nc.scalar.activation(rows8(R_L), rows8(R_F), ACT.Abs).then_inc(gate_a.sem, 1)
            act.wait_ge(gate_a.sem, gate_a.at("abs"))
            nc.scalar.activation(rows8(R_L), rows8(R_L), ACT.Exp, scale=-1.0).then_inc(gate_a.sem, 1)
            act.wait_ge(gate_a.sem, gate_a.at("exp"))
            nc.scalar.activation(rows8(R_L), rows8(R_L), ACT.Ln, bias=one[0:8]).then_inc(gate_a.sem, 1)
            act.wait_ge(gate_v.sem, gate_v.at("m"))
            nc.scalar.activation(rows8(R_L), rows8(R_S), ACT.Exp, scale=-1.0).then_inc(gate_a.sem, 1)

        def dve_gates(v):
            v.wait_ge(gate_p.sem, gate_p.at("tok"))
            bias = gtok[:, 128:160].rearrange("p (o n) -> p o n", o=1).to_broadcast([P, TT, 32])
            nc.vector.tensor_tensor(gtok[:, 0:128].rearrange("p (t n) -> p t n", n=32),
                                    bank[4][:, 0:128].rearrange("p (t n) -> p t n", n=32), bias,
                                    ALU.add).then_inc(gate_v.sem, 1)
            v.wait_ge(gate_a.sem, gate_a.at("ln"))
            nc.vector.scalar_tensor_tensor(rows8(R_F), rows8(R_F), 0.0, rows8(R_L), ALU.min,
                                           ALU.subtract).then_inc(gate_v.sem, 1)
            v.wait_ge(gate_v.sem, gate_v.at("lf"))
            for n, turn in ((0, slice(None)), (1, back)):
                nc.vector.tensor_tensor_scan(row8(R_S + n)[:, turn], one[0:8].to_broadcast([8, S]),
                                             row8(R_F + n)[:, turn], 0.0, ALU.mult, ALU.add).then_inc(gate_v.sem, 1)
            v.wait_ge(gate_v.sem, gate_v.at("Fb"))
            nc.vector.tensor_tensor(rows8(R_G), rows8(R_I), rows8(R_S), ALU.subtract).then_inc(gate_v.sem, 1)
            v.wait_ge(gate_v.sem, gate_v.at("g"))
            for n, turn in ((0, slice(None)), (1, back)):
                nc.vector.tensor_tensor_scan(row8(MROW + n)[:, turn], row8(R_G + n)[:, turn],
                                             row8(R_G + n)[:, turn], 0.0, ALU.max, ALU.max).then_inc(gate_v.sem, 1)
            v.wait_ge(gate_v.sem, gate_v.at("Mb"))
            nc.vector.tensor_tensor(rows8(R_S), rows8(R_S), rows8(MROW), ALU.add).then_inc(gate_v.sem, 1)
            v.wait_ge(gate_p.sem, gate_p.at("cols"))
            nc.vector.tensor_copy(m_cols[:], bank[4][:, 0:P]).then_inc(gate_v.sem, 1)
            v.wait_ge(gate_v.sem, gate_v.at("cols"))

        def fwd(p, i):
            return arena[:, p, i * P:S]

        def bwd(p, i):
            return arena[:, p, 0:(i + 1) * P]

        def pe_mlstm(pe, h):
            at = lambda st, name, back=0: pe.wait_ge(st.sem, st.at(name, h, back))
            at(m_v, "Mh")
            for n in range(2):
                nc.tensor.matmul(bank[4 + n][:], ones[0:8, :], row8(HCUR + n), start=True,
                                 stop=True).then_inc(m_p.sem, 1)
            at(m_a, "k")
            for i, (st, name) in enumerate(((m_a, "nf"), (m_a, "nb"), (m_v, "pb0"), (m_v, "pb1"))):
                at(st, name)
                nc.tensor.matmul(bank[4 + i % 2][:], page(KCUR)[:, i * P:(i + 1) * P], page(P_MQ + h),
                                 start=True, stop=True).then_inc(m_p.sem, 1)
            at(m_v, "mb3")
            for j in range(TT):
                for d in range(2):
                    tiles = [i for i in range(TT) if (i <= j if d == 0 else i >= j)]
                    for i in tiles:
                        mm = nc.tensor.matmul(bank[4][:, 4 * d + j:4 * d + j + 1],
                                              arena[:, PP + i + d, j * P:(j + 1) * P], one[:],
                                              start=(i == tiles[0]), stop=(i == tiles[-1]))
            mm.then_inc(m_p.sem, 1)
            for j in range(TT):
                if j >= 2:
                    at(m_v, f"n{j - 2}")
                for d in range(2):
                    tiles = [i for i in range(TT) if (i <= j if d == 0 else i >= j)]
                    for i in tiles:
                        mm = nc.tensor.matmul(bank[6 + j % 2][:, d * M_V:(d + 1) * M_V],
                                              arena[:, PP + i + d, j * P:(j + 1) * P],
                                              v3[:, i, bass.ds(h * M_V, M_V)],
                                              start=(i == tiles[0]), stop=(i == tiles[-1]))
                mm.then_inc(m_p.sem, 1)

        hcur = arena[:, HCUR:HCUR + 2, :].rearrange("p a n -> p (a n)").rearrange("p (t n) -> p t n", t=TT)

        def act_mlstm(act, h):
            at = lambda st, name, back=0: act.wait_ge(st.sem, st.at(name, h, back))
            at(m_p, "s3", 1)
            nc.scalar.copy(page(KCUR), page(P_MK + h)).then_inc(m_a.sem, 1)
            for n, name in enumerate(("Mf", "Mb")):
                at(m_p, name)
                nc.scalar.copy(page(NM + n), bank[4 + n][:]).then_inc(m_a.sem, 1)
            for i in range(TT):
                for n, (name, part) in enumerate((("ef", fwd), ("eb", bwd))):
                    at(m_v, f"{name}{i}")
                    nc.scalar.activation(part(EE + n, i), part(EE + n, i), ACT.Exp).then_inc(m_a.sem, 1)
            at(m_v, "drec")
            for j in range(TT):
                at(m_p, f"n{j}")
                nc.scalar.activation(hcur[:, j, :], bank[6 + j % 2][:, 0:M_V], ACT.Copy,
                                     scale=den[:, j:j + 1]).then_inc(m_a.sem, 1)
            at(m_v, "n3")
            nc.scalar.copy(v3[:, :, bass.ds(h * M_V, M_V)], hcur).then_inc(m_a.sem, 1)

        def dve_mlstm(v, h):
            at = lambda st, name, back=0: v.wait_ge(st.sem, st.at(name, h, back))
            at(m_a, "back", 1)
            nc.vector.tensor_scalar(rows8(HCUR), rows8(MROW), ident[0:8, bass.ds(h, 1)], -1.0, ALU.mult,
                                    ALU.mult).then_inc(m_v.sem, 1)
            for i in range(TT):
                if i:
                    at(m_v, f"mb{i - 1}")
                for n, part in enumerate((fwd, bwd)):
                    at(m_a, "nf" if n == 0 else "nb")
                    nc.vector.tensor_scalar(part(EE + n, i), part(NM + n, i),
                                            m_cols[:, bass.ds(n * 32 + i * 8 + h, 1)], 0.0, ALU.add,
                                            ALU.min).then_inc(m_v.sem, 1)
                at(m_p, f"s{i}")
                for n, part in enumerate((fwd, bwd)):
                    at(m_a, ("xf" if n == 0 else "xb") + str(i))
                    scores = bank[4 + i % 2][:, i * P:S] if n == 0 else bank[4 + i % 2][:, 0:(i + 1) * P]
                    nc.vector.tensor_tensor(part(PP + i + n, i), scores, part(EE + n, i),
                                            ALU.mult).then_inc(m_v.sem, 1)
                for n in range(2):
                    at(m_v, ("pf" if n == 0 else "pb") + str(i))
                    own = arena[:, PP + i + n, i * P:(i + 1) * P]
                    nc.vector.tensor_tensor(own, own, page(TRI)[:, n * P:(n + 1) * P], ALU.mult).then_inc(m_v.sem, 1)
            at(m_p, "den")
            nc.vector.tensor_copy(den, bank[4][:, 0:8]).then_inc(m_v.sem, 1)
            at(m_v, "dcopy")
            nc.vector.scalar_tensor_tensor(den, den, -1.0, den, ALU.mult, ALU.max).then_inc(m_v.sem, 1)
            at(m_v, "dabs")
            floor = m_cols[:, 64:P].rearrange("p (n h) -> p n h", h=8)[:, :, bass.ds(h, 1)].rearrange("p n h -> p (n h)")
            nc.vector.tensor_tensor(den, den, floor, ALU.max).then_inc(m_v.sem, 1)
            at(m_v, "dmax")
            nc.vector.reciprocal(den, den).then_inc(m_v.sem, 1)
            at(m_v, "drec")
            for j in range(TT):
                at(m_a, f"c{j}")
                nc.vector.scalar_tensor_tensor(hcur[:, j, :], bank[6 + j % 2][:, M_V:2 * M_V], den[:, 4 + j:5 + j],
                                               hcur[:, j, :], ALU.mult, ALU.add).then_inc(m_v.sem, 1)

        def act_gate_evac(act, g, st, name, task, func):
            for t in range(TT):
                act.wait_ge(st.sem, st.at(f"{name}{t}", task, back=1))
                full(act, g, t)
                nc.scalar.activation(page(MO_TMP + t), bank[t][:], func).then_inc(bank_free[t], 1)

        def dve_mo(v, n):
            for t in range(TT):
                x, sq = v3[:, t, bass.ds(n * W, W)], page(MO_SQ + t)
                v.wait_ge(bank_free[t], G_MO + n + 2)
                nc.vector.tensor_tensor(x, x, page(MO_TMP + t), ALU.mult).then_inc(o_v.sem, 1)
                v.wait_ge(o_v.sem, o_v.at(f"g{t}", n))
                v.wait_ge(o_v.sem, o_v.at(f"r{t}", n, back=1))
                nc.vector.tensor_tensor(sq, x, x, ALU.mult).then_inc(o_v.sem, 1)
                v.wait_ge(o_v.sem, o_v.at(f"s{t}", n))
                nc.vector.tensor_reduce(head_sq[:, bass.ds(t * M_HEADS + 2 * n, 2)], sq.rearrange("p (h n) -> p h n", n=M_V),
                                        AX.X, ALU.add).then_inc(o_v.sem, 1)

        def dve_mz(v, n):
            for t in range(TT):
                x = v3[:, t, bass.ds(n * W, W)]
                by_head = x.rearrange("p (h n) -> p h n", n=M_V)
                rs = head_rstd[:, bass.ds(t * M_HEADS + 2 * n, 2)].rearrange("p (h o) -> p h o", o=1)
                nc.vector.tensor_tensor(by_head, by_head, rs.to_broadcast([P, 2, M_V]), ALU.mult).then_inc(z_v.sem, 1)
                v.wait_ge(z_v.sem, z_v.at(f"n{t}", n))
                nc.vector.tensor_tensor(x, x, page(MZ_GAIN, 4)[:, bass.ds(n * W, W)], ALU.mult).then_inc(z_v.sem, 1)
                v.wait_ge(z_v.sem, z_v.at(f"w{t}", n))
                v.wait_ge(bank_free[t], G_MZ + n + 2)
                nc.vector.tensor_tensor(x, x, page(MO_TMP + t), ALU.mult).then_inc(z_v.sem, 1)

        cv_v = steps("cv_v", [f"{x}{m}" for m in range(4) for x in ("w1", "w0", "w2", "b", "z")])

        def act_conv(act, j):
            g = G_CONV + 4 * j
            act.wait_ge(cv_v.sem, cv_v.at("z3", j, back=1))
            act_evac(act, g, lambda m: page(C_U + m))
            act_evac(act, g + 2, lambda m: page(C_B + m))
            act_evac(act, g + 3, lambda m: page(C_Z + m), ACT.Silu)

        def dve_conv(v, j):
            g = G_CONV + 4 * j
            for m in range(4):
                v.wait_ge(bank_free[m], g + 2)
                full(v, g + 1, m)
                nc.vector.tensor_tensor(page(C_GU + m), bank[m][:], page(C_U + m), ALU.mult).then_inc(bank_free[m], 1)
            for m in range(4):
                own = lambda name: v.wait_ge(cv_v.sem, cv_v.at(name + str(m), j))
                gu, y = page(C_GU + m), page(P_YB + 4 * j + m)
                cw = lambda w: col("conv3_w", LRU_TILES * w + 4 * j + m)
                v.wait_ge(bank_free[m], g + 3)
                nc.vector.tensor_scalar(y, gu, cw(1), None, ALU.mult).then_inc(cv_v.sem, 1)
                own("w1")
                nc.vector.scalar_tensor_tensor(y[:, 1:S], gu[:, 0:S - 1], cw(0), y[:, 1:S], ALU.mult,
                                               ALU.add).then_inc(cv_v.sem, 1)
                own("w0")
                nc.vector.scalar_tensor_tensor(y[:, 0:S - 1], gu[:, 1:S], cw(2), y[:, 0:S - 1], ALU.mult,
                                               ALU.add).then_inc(cv_v.sem, 1)
                own("w2")
                v.wait_ge(bank_free[m], g + 4)
                nc.vector.tensor_tensor(y, y, page(C_B + m), ALU.mult).then_inc(cv_v.sem, 1)
                own("b")
                v.wait_ge(bank_free[m], g + 5)
                nc.vector.tensor_tensor(y, y, page(C_Z + m), ALU.mult).then_inc(cv_v.sem, 1)

        mask_in = sem("mask_in")

        def half_cols(p, h):
            return arena[:, p:p + 4, bass.ds(h * HD, HD)]

        sv = arena[:, P_SV:P_SV + 16, :].rearrange("p a n -> p (a n)").rearrange("p (t n) -> p t n", t=TT)
        ln_in = sem("ln_in")
        ln_a = steps("ln_a", "s0 s1 s2 s3 root")
        ln_v = steps("ln_v", "sum mean rec c0 c1 c2 c3 a0 a1 a2 a3")
        sg_p = sem("sg_p")
        sg_v = sem("sg_v")
        u_v = steps("u_v", "m0 m1 m2 m3")

        def act_sgu_values(act):
            act.wait_ge(h_ready, 7 * KT)
            act.wait_ge(new_out, 144)
            act.dma_start(page(S_G, 4), row("ln_g", D)).then_inc(ln_in, 16)
            act.dma_start(page(S_B, 4), row("ln_b", D)).then_inc(ln_in, 16)
            act.dma_start(page(S_BS, 2), row("b_s", 2 * W)).then_inc(ln_in, 16)
            act.dma_start(page(S_WS, 2), ws_d).then_inc(ln_in, 16)
            with act.Fori(0, 4) as n:
                for t in range(TT):
                    full(act, G_SV + n, t)
                    nc.scalar.activation(sv[:, t, bass.ds(n * W, W)], bank[t][:], ACT.Gelu_apprx_tanh,
                                         accum_out=small[:, bass.ds(4 * t + n, 1)]).then_inc(bank_free[t], 1)
            act.wait_ge(ln_v.sem, ln_v.at("mean"))
            for t in range(TT):
                act.wait_ge(ln_a.sem, ln_a.n + t)
                nc.scalar.activation(page(S_TMP, 4), sv[:, t, :], ACT.Square, bias=mean[:, t:t + 1],
                                     accum_out=token_sum[:, t:t + 1]).then_inc(ln_a.sem, 1)
            act.wait_ge(ln_a.sem, ln_a.at("s3"))
            nc.scalar.activation(root, token_sum, ACT.Sqrt, bias=eps[:], scale=1.0 / D).then_inc(ln_a.sem, 1)
            act.wait_ge(ln_a.sem, ln_a.at("root"))

        def dve_sgu_values(v):
            group_written(v, G_SV + 3)
            nc.vector.tensor_reduce(mean, square_sum, AX.X, ALU.add).then_inc(ln_v.sem, 1)
            v.wait_ge(ln_v.sem, ln_v.at("sum"))
            nc.vector.tensor_scalar(mean, mean, -1.0 / D, None, ALU.mult).then_inc(ln_v.sem, 1)
            v.wait_ge(ln_a.sem, ln_a.at("root"))
            nc.vector.reciprocal(rstd, root).then_inc(ln_v.sem, 1)
            v.wait_ge(ln_v.sem, ln_v.at("rec"))
            v.wait_ge(ln_in, 64)
            for t in range(TT):
                nc.vector.scalar_tensor_tensor(sv[:, t, :], sv[:, t, :], mean[:, t:t + 1], page(S_G, 4), ALU.add,
                                               ALU.mult).then_inc(ln_v.sem, 1)
            for t in range(TT):
                v.wait_ge(ln_v.sem, ln_v.at(f"c{t}"))
                nc.vector.scalar_tensor_tensor(sv[:, t, :], sv[:, t, :], rstd[:, t:t + 1], page(S_B, 4), ALU.mult,
                                               ALU.add).then_inc(ln_v.sem, 1)

        def pe_sgu(pe):
            pe.wait_ge(ln_v.sem, ln_v.at("a3"))
            for f in range(KT):
                if f >= 4:
                    pe.wait_ge(sg_v, f - 3)
                for n in range(TT):
                    mm = nc.tensor.matmul(bank[4 + f % 4][:, n * P:(n + 1) * P], sv[:, n, f * P:(f + 1) * P],
                                          page(S_WS, 2)[:, (f // 2) * P:(f // 2 + 1) * P], start=True, stop=True)
                mm.then_inc(sg_p, 1)

        def dve_sgu(v):
            for f in range(KT):
                v.wait_ge(sg_p, f + 1)
                bias = page(S_BS, 2)[:, (f // 2) * P:(f // 2 + 1) * P].rearrange("p (o n) -> p o n", o=1)
                nc.vector.tensor_tensor(page(P_MX + f).rearrange("p (t n) -> p t n", n=P),
                                        bank[4 + f % 4][:].rearrange("p (t n) -> p t n", n=P),
                                        bias.to_broadcast([P, TT, P]), ALU.add).then_inc(sg_v, 1)
            v.wait_ge(sg_v, KT)

        def act_sgu_gate(act, n, func):
            for m in range(4):
                act.wait_ge(u_v.sem, u_v.at(f"m{m}", n, back=1))
                full(act, G_SU + n, m)
                nc.scalar.activation(page(S_TMP + m), bank[m][:], func).then_inc(bank_free[m], 1)

        def dve_sgu_gate(v, n, tile):
            for m in range(4):
                v.wait_ge(bank_free[m], G_SU + n + 2)
                nc.vector.tensor_tensor(page(P_MX + tile + m), page(P_MX + tile + m), page(S_TMP + m),
                                        ALU.mult).then_inc(u_v.sem, 1)

        def mix3(f):
            return P_YA + f if f < HEADS else P_YB + f - HEADS

        def mix4(f):
            return P_MX + f

        cols_in, ident_in = sem("cols_in"), sem("ident_in")
        x_loaded = [sem(f"x_loaded{t}") for t in range(TT)]
        first_square = sem("first_square")
        out_done = sem("out_done")

        def mix1(f):
            return P_GA + f if f < HEADS else P_XL + f - HEADS

        block = ctx.enter_context(nc.Block())

        @block.sync
        def _(sp):
            def weights(g, n, with_mod):
                for c in range(NCH):
                    sp.wait_ge(w_ready, NCH * g + c + 1 + WREADY0 - RAW_SLOTS)
                    sp.dma_start(w_raw[:, c % RAW_SLOTS, :],
                                 wall[bass.ds(g, 1), :, c * CH * W:(c + 1) * CH * W]
                                 .rearrange("a p n -> p (a n)")).then_inc(raw_in[c % RAW_SLOTS], 16)
                    if with_mod:
                        if c < 2:
                            sp.wait_ge(mod_sum.sem, mod_sum.at(f"k{13 + 2 * c}", n, back=1))
                        else:
                            sp.wait_ge(mod_sum.sem, mod_sum.at(f"k{2 * c - 3}", n))
                        sp.dma_start(page(MOD_RING + 2 * (c % 2), 2),
                                     mods[bass.ds(n, 1), :, c * CH * W:(c + 1) * CH * W]
                                     .rearrange("a p n -> p (a n)")).then_inc(mod_in[c % 2], 16)

            groups = {0: 0, 1: G_OUT1 + 4, 2: G_OUT2 + 4, 3: G_OUT3 + 4, 4: GROUPS}[layers]
            for m in range(4):
                sp.sem_inc(bank_free[m], 1)
            with sp.Fori(0, min(MODS, groups)) as g:
                weights(g, g, True)
            if groups > MODS:
                with sp.Fori(MODS, groups) as g:
                    weights(g, 0, False)

        @block.gpsimd
        def _(pool):
            pool.sem_inc(w_ready, WREADY0)
            pool.wait_ge(setup_v.sem, setup_v.at("zero"))
            groups = {0: 0, 1: G_OUT1 + 4, 2: G_OUT2 + 4, 3: G_OUT3 + 4, 4: GROUPS}[layers]
            with pool.Fori(0, groups) as g:
                for c in range(NCH):
                    raw, s = w_raw[:, c % RAW_SLOTS, :], c % SPLIT_SLOTS
                    pool.wait_ge(raw_in[c % RAW_SLOTS], 16 * (2 * g + c // RAW_SLOTS + 1))
                    if c == 1:
                        pool.wait_ge(bank_full, 4 * g + FULL0)
                    else:
                        pool.wait_ge(w_used, (NCH - 1) * g + WUSED0 + (c - 1 if c else 0))
                    nc.gpsimd.tensor_tensor(w_hi[:, s, :], raw, zero[:].to_broadcast([P, CH * W]),
                                            ALU.add).then_inc(w_hi_done, 1)
                    pool.wait_ge(w_hi_done, NCH * g + c + 1)
                    nc.gpsimd.tensor_tensor(w_lo[:, s, :], raw, w_hi[:, s, :].bitcast(F32),
                                            ALU.subtract).then_inc(w_ready, 1)

        @block.vector
        def _(v):
            for st in (mod_sum, norm_v, res_v, final_v, lru_v, att1.kv_v, att1.q_v, att1.s_v, att3.kv_v, att3.q_v,
                       att3.s_v, qk_v, setup_v, gate_v, m_v, o_v, z_v,
                       modc_v, modg_v, cv_v, ln_v, u_v):
                v.sem_inc(st.sem, st.n)
            nc.vector.memset(zero[:], 0.0).then_inc(setup_v.sem, 1)
            nc.vector.memset(one[:], 1.0).then_inc(setup_v.sem, 1)
            nc.vector.memset(eps[:], EPS).then_inc(setup_v.sem, 1)
            nc.vector.memset(small[:], 0.0).then_inc(setup_v.sem, 1)
            nc.vector.memset(ones[:], 1.0).then_inc(setup_v.sem, 1)
            v.wait_ge(setup_a.sem, setup_a.at("ln"))
            low = page(ROWS)[:, 0:2 * LRU_TILES]
            nc.vector.tensor_scalar(low, col("lam", 0, 2 * LRU_TILES), 0.0, None, ALU.min).then_inc(setup_v.sem, 1)
            v.wait_ge(setup_v.sem, setup_v.at("min"))
            nc.vector.tensor_tensor(lru_decay[:], low, lru_decay[:], ALU.subtract).then_inc(setup_v.sem, 1)
            v.wait_ge(setup_v.sem, setup_v.at("sub"))
            nc.vector.tensor_scalar(lru_decay[:], lru_decay[:], LRU_C, None, ALU.mult).then_inc(setup_v.sem, 1)
            v.wait_ge(setup_v.sem, setup_v.at("scale"))

            v.wait_ge(ident_in, 16)
            v.wait_ge(first_square, TT)
            dve_norm(v, 0)
            dve_turn(v, 0, TMP)
            with v.Fori(0, G_Q) as g:
                dve_mod(v, g)
            group_written(v, G_Q - 1)
            with v.Fori(0, LRU_TILES // 2) as i:
                dve_mod(v, G_Q + i)
                dve_lru(v, 2 * i)
                dve_lru(v, 2 * i + 1)
            dve_mod(v, G_KV)
            group_written(v, G_KV)
            dve_qk_stats(v)
            v.wait_ge(rope_in, 32)
            with v.Fori(0, KV_HEADS) as kv:
                att1.dve_kv(v, kv, kv * (HEADS // KV_HEADS), head_cols(qkv, D // 2, kv), head_cols(qkv, D // 2 + KV_HEADS * HD, kv),
                            rs_of(HEADS + kv), gain_of(1))
                with v.Fori(0, HEADS // KV_HEADS) as j:
                    h = kv * (HEADS // KV_HEADS) + j
                    att1.dve_q(v, h, kv, head_cols(qkv, 0, h), rs_of(h), gain_of(0))
                    att1.dve_head(v, h, page(P_GA + h))
            dve_split(v, 1, mix1)
            dve_residual(v, 0, G_OUT1, False)
            if layers == 1:
                return

            v.wait_ge(res_a.sem, res_a.at("q3", 3))
            dve_norm(v, 1)
            dve_turn(v, 2, TMP)
            with v.Fori(G_MQ, G_MO) as g:
                dve_mod(v, g)
            dve_gates(v)
            group_written(v, G_MO - 1)
            v.wait_ge(tri_in, 16)
            with v.Fori(0, M_HEADS) as h:
                dve_mlstm(v, h)
            v.wait_ge(m_a.sem, m_a.at("back", M_HEADS - 1))
            with v.Fori(0, MODS - G_MO) as n:
                dve_mod(v, G_MO + n)
                dve_mo(v, n)
            dve_mo(v, 3)
            v.wait_ge(m_root, 1)
            nc.vector.reciprocal(head_rstd[:, 0:32], head_rstd[:, 0:32]).then_inc(m_rec, 1)
            v.wait_ge(m_rec, 1)
            v.wait_ge(gain_in, 16)
            with v.Fori(0, 4) as n:
                dve_mz(v, n)
            dve_turn(v, 3, TMP)
            dve_residual(v, 1, G_OUT2, False)
            v.wait_ge(res_a.sem, res_a.at("q3", 7))
            dve_norm(v, 2)
            dve_final(v, 0)
            if layers == 2:
                return

            v.wait_ge(final_a.sem, final_a.at("q3", 0))
            dve_norm(v, 3)
            dve_mod_cols(v, 0)
            dve_turn(v, 4, TMP)
            with v.Fori(0, 2) as j:
                dve_conv(v, j)
            v.wait_ge(rope_in, 48)
            v.wait_ge(mask_in, 16)
            with v.Fori(0, 2) as j:
                with v.Fori(0, 4) as i:
                    group_written(v, G_ATT + 4 * j + 3)
                    h = 4 * j + i
                    att3.dve_kv(v, h, h, half_cols(P_KH, i), half_cols(P_VH, i))
                    att3.dve_q(v, h, h, half_cols(P_QH, i))
                    att3.dve_head(v, h, page(P_YA + h))
            dve_split(v, 5, mix3)
            dve_residual(v, 2, G_OUT3, True)
            if layers == 3:
                return

            v.wait_ge(res_a.sem, res_a.at("q3", 11))
            dve_norm(v, 4)
            dve_mod_cols(v, 1)
            dve_turn(v, 6, TMP)
            dve_sgu_values(v)
            dve_sgu(v)
            for first in (0, 4):
                with v.Fori(0, 4) as n:
                    dve_sgu_gate(v, first + n, 4 * n)
            dve_split(v, 7, mix4)
            dve_residual(v, 3, G_OUT4, True)
            v.wait_ge(res_a.sem, res_a.at("q3", 15))
            dve_norm(v, 5)
            dve_final(v, 1)

        @block.scalar
        def _(act):
            for st in (setup_a, norm_a, res_a, final_a, lru_a, att1.kv_a, att1.a, att3.kv_a, att3.a, qk_a, gate_a, m_a, ln_a):
                act.sem_inc(st.sem, st.n)
            act.sem_inc(mod_out, 16)
            act.dma_start(cols[:], cols_d).then_inc(cols_in, 16)
            for t in range(TT):
                act.dma_start(xp[:, t, :], x_in[t * P:(t + 1) * P, :]).then_inc(x_loaded[t], 16)
            act.dma_start(ident[:], ident_d).then_inc(ident_in, 16)
            act.wait_ge(cols_in, 16)
            nc.scalar.activation(c_silu[:], col("c", 0, KT), ACT.Silu).then_inc(setup_a.sem, 1)
            nc.scalar.activation(lru_decay[:], col("lam", 0, 2 * LRU_TILES), ACT.Abs).then_inc(setup_a.sem, 1)
            act.wait_ge(setup_a.sem, setup_a.at("abs"))
            nc.scalar.activation(lru_decay[:], lru_decay[:], ACT.Exp, scale=-1.0).then_inc(setup_a.sem, 1)
            act.wait_ge(setup_a.sem, setup_a.at("exp"))
            act.wait_ge(setup_v.sem, setup_v.at("sums"))
            nc.scalar.activation(lru_decay[:], lru_decay[:], ACT.Ln, bias=one[:]).then_inc(setup_a.sem, 1)

            for t in range(TT):
                act.wait_ge(x_loaded[t], 16)
                if t:
                    act.wait_ge(first_square, t)
                nc.scalar.activation(page(JUNK, 4), xp[:, t, :], ACT.Square,
                                     accum_out=square_sum[:, t, 0:1]).then_inc(first_square, 1)
            act_norm(act, 0)
            act_turn(act, 0, TMP, lambda f: col("norm0", f), lambda f: col("zero", f))
            with act.Fori(0, G_GL) as g:
                act_mod(act, g)
                act_evac(act, g, lambda m: page(P_XL + 4 * g + m))
            with act.Fori(0, G_Q - G_GL) as i:
                act_mod(act, G_GL + i)
                act_evac(act, G_GL + i, lambda m: page(P_GL + 4 * i + m), ACT.Silu)
            with act.Fori(0, G_GA - G_Q) as i:
                act_mod(act, G_Q + i)
                act_lru(act, 2 * i)
                act_lru(act, 2 * i + 1)
                act_evac(act, G_Q + i, lambda m: qkv[:, m, bass.ds(i * W, W)])
            with act.Fori(0, G_KV - G_GA) as i:
                act_mod(act, G_GA + i)
                act_lru(act, 2 * i + 4)
                act_lru(act, 2 * i + 5)
                act_evac(act, G_GA + i, lambda m: page(P_GA + 4 * i + m), ACT.Silu)
            act_mod(act, G_KV)
            act.wait_ge(lru_v.sem, lru_v.at("yg", LRU_TILES - 1))
            act_load_rope(act, 0, att1)
            act.dma_start(gains, rows_d[:, ROW["q_gain"]:ROW["q_gain"] + 2 * HD]).then_inc(rope_in, 16)
            act_evac(act, G_KV, lambda m: qkv[:, m, 2 * W:3 * W])
            act.wait_ge(qk_v.sem, qk_v.at("r3"))
            nc.scalar.activation(head_rstd[:, 0:TT * QK], head_sq[:, 0:TT * QK], ACT.Sqrt, bias=eps[:],
                                 scale=1.0 / HD).then_inc(qk_a.sem, 1)
            with act.Fori(0, KV_HEADS) as kv:
                att1.act_kv(act, kv)
                with act.Fori(0, HEADS // KV_HEADS) as j:
                    att1.act_head(act, kv * (HEADS // KV_HEADS) + j)
            act.wait_ge(att1.s_v.sem, att1.s_v.at("gate", HEADS - 1))
            act_split(act, mix1)
            act_residual(act, 0, G_OUT1, x_in, False, True)
            if layers == 1:
                act.dma_start(out.rearrange("(t p) n -> p t n", p=P), xp).then_inc(out_done, 16)
                act.wait_ge(out_done, 16)
                act.wait_ge(new_out, 64)
                act.wait_ge(mod_out, 16 * (G_OUT1 + 4 + 1))
                return

            act_norm(act, 1)
            act_turn(act, 2, TMP, lambda f: col("norm1", f), lambda f: col("zero", f))
            act.wait_ge(new_out, 64)
            act.dma_start(page(GW), gate_w).then_inc(gate_in, 16)
            act.dma_start(gtok[:, 128:160], row("m_bias", 32)).then_inc(gate_in, 16)
            act.dma_start(page(TRI)[:, 0:2 * P], tri_d).then_inc(tri_in, 16)
            for n, dst, scale in ((0, P_MQ, 1.0), (2, P_MK, HD ** -0.5)):
                with act.Fori(0, 2) as i:
                    act_mod(act, G_MQ + n + i)
                    act_evac(act, G_MQ + n + i, lambda m: page(dst + 4 * i + m), scale=scale)
            with act.Fori(0, 4) as i:
                act_mod(act, G_MV + i)
                act_evac(act, G_MV + i, lambda m: v3[:, m, bass.ds(i * W, W)])
            act_gates(act)
            act.wait_ge(gate_v.sem, gate_v.at("cols"))
            with act.Fori(0, M_HEADS) as h:
                act_mlstm(act, h)
            act.dma_start(page(MZ_GAIN, 4), row("m_gain", D)).then_inc(gain_in, 16)
            with act.Fori(0, MODS - G_MO) as n:
                act_mod(act, G_MO + n)
                act_gate_evac(act, G_MO + n, o_v, "g", n, ACT.Sigmoid)
            act_gate_evac(act, G_MO + 3, o_v, "g", 3, ACT.Sigmoid)
            act.wait_ge(o_v.sem, o_v.at("r3", 3))
            nc.scalar.activation(head_rstd[:, 0:32], head_sq[:, 0:32], ACT.Sqrt, bias=eps[:],
                                 scale=1.0 / M_V).then_inc(m_root, 1)
            with act.Fori(0, 4) as n:
                act_gate_evac(act, G_MZ + n, z_v, "z", n, ACT.Silu)
            act_turn(act, 3, TMP)
            act_residual(act, 1, G_OUT2, x_mid, False, False)
            act_norm(act, 2)
            act_final(act, 0)
            act.dma_start(x_mid.rearrange("(t p) n -> p t n", p=P), xp).then_inc(new_out, 16)
            if layers == 2:
                act.dma_start(out.rearrange("(t p) n -> p t n", p=P), xp).then_inc(out_done, 16)
                act.wait_ge(out_done, 16)
                act.wait_ge(new_out, 80)
                act.wait_ge(mod_out, 16 * (MODS + 1))
                return

            act_load_mod(act, 0)
            act_norm(act, 3)
            act.wait_ge(modc_v.sem, modc_v.at("gain", 0))
            act_load_rope(act, 1, att3)
            act_turn(act, 4, TMP, lambda f: mod_scale[:, f:f + 1], lambda f: mod_shift[:, f:f + 1])
            act.wait_ge(new_out, 80)
            act.dma_start(page(att3.pg["mask"], 4), mask_d).then_inc(mask_in, 16)
            with act.Fori(0, 2) as j:
                act_conv(act, j)
            with act.Fori(0, 2) as j:
                act.wait_ge(cv_v.sem, cv_v.at("z3", 1))
                act.wait_ge(att3.s_v.sem, att3.s_v.at("gate", 4 * j, back=1))
                for n, p in enumerate((P_QH, P_KH, P_VH)):
                    act_evac(act, G_ATT + 4 * j + n, lambda m: page(p + m))
                act_evac(act, G_ATT + 4 * j + 3, lambda m: page(P_YA + 4 * j + m), ACT.Silu)
                with act.Fori(0, 4) as i:
                    att3.act_kv(act, 4 * j + i)
                    att3.act_head(act, 4 * j + i)
            act.wait_ge(att3.s_v.sem, att3.s_v.at("gate", HEADS - 1))
            act_split(act, mix3)
            act_residual(act, 2, G_OUT3, x_mid, True, True)
            if layers == 3:
                act.dma_start(out.rearrange("(t p) n -> p t n", p=P), xp).then_inc(out_done, 16)
                act.wait_ge(out_done, 16)
                act.wait_ge(new_out, 144)
                return

            act_load_mod(act, 1)
            act_norm(act, 4)
            act.wait_ge(modc_v.sem, modc_v.at("gain", 1))
            act_turn(act, 6, TMP, lambda f: mod_scale[:, f:f + 1], lambda f: mod_shift[:, f:f + 1])
            act_sgu_values(act)
            for first, func in ((0, ACT.Gelu_apprx_tanh), (4, ACT.Silu)):
                with act.Fori(0, 4) as n:
                    act_sgu_gate(act, first + n, func)
            act.wait_ge(u_v.sem, u_v.at("m3", 7))
            act_split(act, mix4)
            act_residual(act, 3, G_OUT4, x_mid, True, False)
            act_norm(act, 5)
            for t in range(TT):
                act.wait_ge(final_v.sem, final_v.at(f"r{t}", 1))
                act.dma_start(out[t * P:(t + 1) * P, :], xp[:, t, :]).then_inc(out_done, 16)
            act.wait_ge(out_done, 16 * TT)
            act.wait_ge(new_out, 144)

        @block.tensor
        def _(pe):
            for st in (lru_p, att1.kv_p, att1.p, att3.kv_p, att3.p, gate_p, m_p, modc_p, modg_p):
                pe.sem_inc(st.sem, st.n)
            pe.sem_inc(bank_full, FULL0)
            pe.sem_inc(w_used, WUSED0)

            pe.wait_ge(norm_v.sem, norm_v.at("d3"))
            pe_turn(pe, 0, lambda f, t: xp[:, t, f * P:(f + 1) * P], diag)
            with pe.Fori(0, G_Q) as g:
                pe_group(pe, g, False, 0)
            for g0, i0, tokens_out in ((G_Q, 0, True), (G_GA, 2, False)):
                with pe.Fori(0, 2) as i:
                    pe_chunks(pe, g0 + i, 0, 2, tokens_out, 0)
                    pe_lru(pe, 2 * (i + i0))
                    pe_chunks(pe, g0 + i, 2, 5, tokens_out, 0)
                    pe_lru(pe, 2 * (i + i0) + 1)
                    pe_chunks(pe, g0 + i, 5, NCH, tokens_out, 0)
            pe_group(pe, G_KV, True, 0)
            with pe.Fori(0, KV_HEADS) as kv:
                att1.pe_kv(pe, kv, kv * (HEADS // KV_HEADS))
                with pe.Fori(0, HEADS // KV_HEADS) as j:
                    att1.pe_head(pe, kv * (HEADS // KV_HEADS) + j, kv)
            with pe.Fori(G_OUT1, G_OUT1 + 4) as g:
                pe_group(pe, g, True, KT)
            if layers == 1:
                return

            pe.wait_ge(norm_v.sem, norm_v.at("d3", 1))
            pe_turn(pe, 2, lambda f, t: xp[:, t, f * P:(f + 1) * P], diag)
            with pe.Fori(G_MQ, G_MV) as g:
                pe_group(pe, g, False, 2 * KT)
            with pe.Fori(G_MV, G_MO) as g:
                pe_group(pe, g, True, 2 * KT)
            pe_gates(pe)
            pe_gate_cols(pe)
            with pe.Fori(0, M_HEADS) as h:
                pe_mlstm(pe, h)
            with pe.Fori(G_MO, G_OUT2) as g:
                pe_group(pe, g, True, 2 * KT)
            pe.wait_ge(z_v.sem, z_v.at("z3", 3))
            pe_turn(pe, 3, lambda f, t: v3[:, t, f * P:(f + 1) * P], None)
            with pe.Fori(G_OUT2, G_OUT2 + 4) as g:
                pe_group(pe, g, True, 3 * KT)
            if layers == 2:
                return

            pe_mod_cols(pe, 0)
            pe.wait_ge(norm_v.sem, norm_v.at("d3", 3))
            pe_turn(pe, 4, lambda f, t: xp[:, t, f * P:(f + 1) * P], diag)
            with pe.Fori(G_CONV, G_ATT) as g:
                pe_group(pe, g, False, 4 * KT)
            with pe.Fori(0, 2) as j:
                with pe.Fori(0, 3) as n:
                    pe_group(pe, G_ATT + 4 * j + n, True, 4 * KT)
                pe_group(pe, G_ATT + 4 * j + 3, False, 4 * KT)
                with pe.Fori(0, 4) as i:
                    att3.pe_kv(pe, 4 * j + i, 4 * j + i)
                    att3.pe_head(pe, 4 * j + i, 4 * j + i)
            pe_group(pe, G_OUT3, True, 5 * KT)
            pe_gate(pe, 2)
            with pe.Fori(G_OUT3 + 1, G_OUT3 + 4) as g:
                pe_group(pe, g, True, 5 * KT)
            if layers == 3:
                return

            pe_mod_cols(pe, 1)
            pe.wait_ge(norm_v.sem, norm_v.at("d3", 4))
            pe_turn(pe, 6, lambda f, t: xp[:, t, f * P:(f + 1) * P], diag)
            with pe.Fori(G_SV, G_SU) as g:
                pe_group(pe, g, True, 6 * KT)
            pe_sgu(pe)
            with pe.Fori(G_SU, G_OUT4) as g:
                pe_group(pe, g, False, 6 * KT)
            pe_group(pe, G_OUT4, True, 7 * KT)
            pe_gate(pe, 3)
            with pe.Fori(G_OUT4 + 1, GROUPS) as g:
                pe_group(pe, g, True, 7 * KT)


def _rope_table(angle_lo, angle_hi, part):
    both = []
    for fn, sign in ((np.cos, 1.0), (np.sin, -1.0)):
        pieces = []
        for angle in ((angle_lo, angle_hi) if angle_hi is not None else (angle_lo,)):
            pieces += [np.float32(sign) * fn(angle), fn(angle)]
        both.append(np.concatenate(pieces, axis=1).astype(np.float32))
    return np.stack(both).reshape(2, TT, P, HD).transpose(2, 0, 1, 3)


def kernel(**inputs):
    import concourse.bacc as _bacc
    from concourse.bass_utils import run_bass_kernel_spmd as _run

    LAYERS = 4
    a = {k: np.asarray(v) for k, v in inputs.items()}

    def groups(w, *parts):
        w = np.concatenate([w[:, b:e] for b, e in parts], axis=1) if parts else w
        return w.reshape(KT, P, -1, W).transpose(2, 1, 0, 3).reshape(-1, P, KT * W)

    w1, w3, w5, w7 = a["even_w_in"][0], a["odd_w_in"][0], a["ab_w_in_2"][0], a["sg_w_in_2"][0]
    h = LRU_W
    conv_groups = [(b + 4 * h + j * W, b + 4 * h + (j + 1) * W) for j in range(2) for b in (0, 2 * h, h, 3 * h)]
    att_groups = [(b + j * W, b + (j + 1) * W) for j in range(2) for b in (0, h, 2 * h, 3 * h)]
    kv = 2 * KV_HEADS * HD
    wall = np.concatenate([
        groups(w1, (2 * h + kv, 4 * h + kv), (0, h), (h + kv, 2 * h + kv), (h, h + kv)),
        groups(a["even_w_out"][0]),
        groups(w3, (0, 2 * h + 3 * D)), groups(a["odd_w_out"][0]),
        groups(w5, *conv_groups, *att_groups), groups(a["ab_w_out_2"][0]),
        groups(w7, (D, 2 * D), (0, D), (2 * D, 3 * D)), groups(a["sg_w_out_2"][0])])
    mods = np.concatenate([groups(a["ab_w_mod_2"][0]), groups(a["sg_w_mod_2"][0])])
    b2, b3 = a["ab_b_mod_2"][0], a["sg_b_mod_2"][0]
    columns = {"norm0": a["norm_gain"][0], "norm1": a["norm_gain"][1], "conv_w": a["conv_w"], "conv_b": a["conv_b"],
               "ba": a["lru_ba"], "bx": a["lru_bx"], "lam": a["lru_lambda"], "c": a["c_2"],
               "norm2": a["ab_norm_g_2"], "shift_b2": b2[0:D], "scale_b2": b2[D:2 * D], "conv3_w": a["ab_conv_w_2"],
               "norm3": a["sg_norm_g_2"], "shift_b3": b3[0:D], "scale_b3": b3[D:2 * D],
               "zero": np.zeros(D, np.float32)}
    assert list(columns) == list(COLS)
    cols = np.concatenate([v.reshape(-1, P) for v in columns.values()]).T
    long_rows = {"final0": a["final_gain"], "final1": a["final_norm_g_2"], "gate_b2": b2[2 * D:], "gate_b3": b3[2 * D:],
                 "m_gain": a["odd_norm_gain"], "ln_g": a["sg_ln_g_2"], "ln_b": a["sg_ln_b_2"], "b_s": a["sg_b_s_2"],
                 "q_gain": a["q_norm_gain"], "k_gain": a["k_norm_gain"], "m_bias": a["odd_gate_bias"]}
    assert list(long_rows) == list(ROW)
    rows = np.broadcast_to(np.concatenate([v.reshape(-1) for v in long_rows.values()]), (P, NROWS))
    lru_w = np.stack([a["lru_wa"][0, 0], a["lru_wx"][0, 0], a["lru_wa"][0, 1], a["lru_wx"][0, 1]])
    lru_w = lru_w.transpose(1, 2, 0, 3).reshape(LRU_TILES, P, 4 * P)
    gate_w = w3[:, 2 * h + 3 * D:].reshape(KT, P, 32).transpose(1, 0, 2).reshape(P, KT * 32)

    f32 = np.float32
    inv = f32(10000.0) ** (-np.arange(0, HD // 2, 2, dtype=f32) / f32(HD // 2))
    tok = np.arange(S)
    rope1 = _rope_table((tok // 64).astype(f32)[:, None] * inv, (tok % 64).astype(f32)[:, None] * inv, HD // 4)
    inv3 = f32(10000.0) ** (-np.arange(HD // 2, dtype=f32) / f32(HD // 2))
    rope3 = _rope_table(tok.astype(f32)[:, None] * inv3, None, HD // 2)
    rope = np.stack([rope1, rope3]).reshape(2, P, 2 * TT * HD)
    gap = np.abs(tok[:, None] - tok[None, :])
    count = (gap <= 64).astype(int) + ((gap % 4 == 0) & (gap <= 256)) + (gap % 16 == 0)
    mask = np.where(count > 0, np.log(np.maximum(count, 1)) / SCALE, -1e30).astype(f32)
    mask = mask.reshape(TT, P, S).transpose(1, 0, 2).reshape(P, TT * S)
    i = np.arange(P)
    tri = np.stack([i[:, None] <= i[None, :], i[:, None] >= i[None, :]], axis=1).astype(f32).reshape(P, 2 * P)
    arrays = {"x": a["x"][0], "wall": wall, "mods": mods, "cols": cols, "rows": rows, "lru_w": lru_w,
              "gate_w": gate_w, "ident": np.eye(P, dtype=f32), "rope": rope, "mask": mask, "tri": tri,
              "ws": a["sg_w_s_2"][0].transpose(2, 0, 1).reshape(P, 8 * P)}
    arrays = {k: np.ascontiguousarray(v) for k, v in arrays.items()}

    nc = _bacc.Bacc("TRN2", target_bir_lowering=False, num_devices=1)
    args = [nc.dram_tensor(f"in_{k}", v.shape, F32, kind="ExternalInput").ap() for k, v in arrays.items()]
    x_mid = nc.dram_tensor("x_mid", (S, D), F32, kind="Internal").ap()
    mod_mid = nc.dram_tensor("mod_mid", (MODS, P, W), F32, kind="Internal").ap()
    out = nc.dram_tensor("out_0", (S, D), F32, kind="ExternalOutput").ap()
    build_program(nc, *args, x_mid, mod_mid, out, layers=LAYERS)
    r = _run(nc, [{f"in_{k}": v for k, v in arrays.items()}], core_ids=[0])
    return r.results[0]["out_0"].reshape(1, S, D)
```

```python
from contextlib import ExitStack

import numpy as np
import concourse.bass as bass
from concourse import mybir

F32 = mybir.dt.float32
F32R = mybir.dt.float32r
ALU = mybir.AluOpType
ACT = mybir.ActivationFunctionType
AX = mybir.AxisListType

P = 128
D = 2048
S = 512
KT = D // P
TT = S // P
W = 512
CH = 2
NCH = KT // CH
RAW_SLOTS = 4
SPLIT_SLOTS = 2
EPS = 1e-6
HD = 128
HEADS = 8
KV_HEADS = 2
LRU_W = D // 2
LRU_TILES = LRU_W // P
LRU_C = 8.0
M_HEADS = 8
M_V = D // M_HEADS
SCALE = HD ** -0.5
MOD_BLOCKS = 3 * D // W

G_Q, G_KV, G_XL, G_GL, G_GA, G_OUT1 = 0, 2, 3, 5, 7, 9
G_MQ, G_MK, G_MV, G_MO, G_MZ, G_OUT2 = 13, 15, 17, 21, 25, 29
G_ATT, G_ZA, G_OUT3 = 33, 47, 49
G_SV, G_SU, G_SZ, G_OUT4 = 53, 57, 61, 65
GROUPS = 69
MODS = 2 * MOD_BLOCKS
RIDES = ((G_Q + 1, 2, 2, 0), (G_OUT1, 4, 1, 4), (G_MQ + 1, 3, 2, 8), (G_MO + 1, 3, 1, 14), (G_MZ, 4, 1, 17),
         (G_OUT2 + 1, 3, 1, 21))

PAGES = 54
MOD_RING, MOD_ACC = 49, 53
XP, XR, GATE, MACC, DIAG, TMP, JUNK = 0, 16, 24, 28, 32, 33, 37
ROWS = 41
P_XL, P_GL, P_GA, P_QKV = 0, 8, 16, 24
LW, XC, GR0, GI0, GR1, GI1, TH, EA, HB, GA_TMP = 24, 25, 26, 27, 28, 29, 30, 32, 34, 36
P_MQ, P_MK, P_MV, KCUR, NM, EE, PP, TRI, HCUR, MROW = 0, 8, 16, 32, 33, 35, 37, 44, 45, 47
GTOK, GW = 46, 45
MO_TMP, MO_SQ, MZ_GAIN = 32, 36, 40
P_YB, C_U, P_QH, P_KH, P_VH, P_YA = 0, 8, 12, 16, 20, 24
P_SV, P_MX, S_TMP, S_G, S_B, S_BS, S_WS = 0, 16, 32, 36, 40, 44, 46


COLS = {}


def _columns():
    at = 0
    for name, n in (("norm0", KT), ("norm1", KT), ("conv_w", 4 * LRU_TILES), ("conv_b", LRU_TILES),
                    ("ba", 2 * LRU_TILES), ("bx", 2 * LRU_TILES), ("lam", 2 * LRU_TILES), ("c", KT),
                    ("norm2", KT), ("shift_b2", KT), ("scale_b2", KT), ("conv3_w", 3 * LRU_TILES),
                    ("norm3", KT), ("shift_b3", KT), ("scale_b3", KT), ("zero", KT)):
        COLS[name] = at
        at += n
    return at


NCOLS = _columns()
ROW = {}


def _rows():
    at = 0
    for name, n in (("final0", D), ("final1", D), ("gate_b2", D), ("gate_b3", D), ("m_gain", D),
                    ("ln_g", D), ("ln_b", D), ("b_s", 8 * P), ("q_gain", HD), ("k_gain", HD),
                    ("m_bias", 32)):
        ROW[name] = at
        at += n
    return at


NROWS = _rows()


class Steps:

    def __init__(self, sem, names):
        self.sem, self.names = sem, names.split() if isinstance(names, str) else names
        self.n = len(self.names)

    def at(self, name, task=0, back=0):
        return self.n * (task + 1 - back) + self.names.index(name) + 1


def build_program(nc, x_in, wall, mods, cols_d, rows_d, lru_w, gate_w, ident_d, rope_d, mask_d, tri_d,
                  ws_d, x_mid, mod_mid, out, layers=4):
    with ExitStack() as ctx:
        def sb(name, shape, dt=F32):
            return ctx.enter_context(nc.sbuf_tensor(name, shape, dt))

        def sem(name):
            return ctx.enter_context(nc.semaphore(name))

        def steps(name, names):
            return Steps(sem(name), names)

        h_hi = sb("h_hi", [P, KT, S], F32R)
        h_lo = sb("h_lo", [P, KT, S], F32R)
        w_raw = sb("w_raw", [P, RAW_SLOTS, CH * W])
        w_hi = sb("w_hi", [P, SPLIT_SLOTS, CH * W], F32R)
        w_lo = sb("w_lo", [P, SPLIT_SLOTS, CH * W], F32R)
        arena = sb("arena", [P, PAGES, W])
        cols = sb("cols", [P, NCOLS])
        ident = sb("ident", [P, P])
        zero = sb("zero", [P, 1])
        one = sb("one", [P, 1])
        eps = sb("eps", [P, 1])
        c_silu = sb("c_silu", [P, KT])
        lru_decay = sb("lru_decay", [P, 2 * LRU_TILES])
        lru_half = sb("lru_half", [P, 2 * LRU_TILES])
        small = sb("small", [P, 160])
        ones = sb("ones", [P, P])
        m_cols = sb("m_cols", [P, P])
        bank = [ctx.enter_context(nc.psum_tensor(f"bank{i}", [P, W], F32)) for i in range(8)]

        def page(i, n=1):
            if isinstance(i, int):
                return arena[:, i:i + n, :].rearrange("p a n -> p (a n)")
            return arena[:, bass.ds(i, n), :].rearrange("p a n -> p (a n)")

        def col(name, i=0, n=1):
            return cols[:, bass.ds(COLS[name] + i, n)]

        def row(name, n):
            return rows_d[:, ROW[name]:ROW[name] + n]

        square_sum = small[:, 0:16].rearrange("p (t n) -> p t n", n=4)
        token_sum = small[:, 16:20]
        root = small[:, 20:24]
        rstd = small[:, 24:28]
        head_sq = small[:, 28:68]
        head_rstd = small[:, 68:108]
        row_max = small[:, 108:110]
        row_bias = small[:, 110:112]
        row_sum = small[:, 112:114]
        row_rec = small[:, 114:116]
        den = small[:, 116:124]
        mod_scale = small[:, 124:140]
        mod_shift = small[:, 140:156]
        mean = small[:, 156:160]

        raw_in = [sem(f"raw_in{s}") for s in range(RAW_SLOTS)]
        w_hi_done = sem("w_hi_done")
        w_ready = sem("w_ready")
        w_used = sem("w_used")
        bank_full = sem("bank_full")
        bank_free = [sem(f"bank_free{m}") for m in range(4)]
        pool_turn = sem("pool_turn")
        h_ready = sem("h_ready")
        h_hi_done = sem("h_hi_done")
        loaded = sem("loaded")
        stored = sem("stored")
        mod_in = [sem(f"mod_in{s}") for s in range(2)]
        mod_sum = steps("mod_sum", [f"k{k}" for k in range(KT)])
        mod_out = sem("mod_out")
        setup_a = steps("setup_a", "silu abs exp ln")
        setup_v = steps("setup_v", "zero one eps sums ones min sub half scale")

        FULL0, WREADY0, WUSED0 = 4, NCH, NCH - 1

        def group_written(eng, g):
            for m in range(4):
                eng.wait_ge(bank_free[m], g + 2)

        def pe_chunks(pe, g, first, last, tokens_out, h_tiles):
            for c in range(first, last):
                s = c % SPLIT_SLOTS
                pe.wait_ge(h_ready, h_tiles + CH * (c + 1))
                pe.wait_ge(w_ready, NCH * g + c + 1 + WREADY0)
                for m in range(4):
                    if c == 0:
                        pe.wait_ge(bank_free[m], g + 1)
                    for kk in range(CH):
                        k = CH * c + kk
                        if tokens_out:
                            hs = slice(m * P, (m + 1) * P)
                            ws = slice(kk * W, (kk + 1) * W)
                            pairs = ((h_hi[:, k, hs], w_hi[:, s, ws]), (h_hi[:, k, hs], w_lo[:, s, ws]),
                                     (h_lo[:, k, hs], w_hi[:, s, ws]))
                        else:
                            ws = slice(kk * W + m * P, kk * W + (m + 1) * P)
                            pairs = ((w_hi[:, s, ws], h_hi[:, k, :]), (w_hi[:, s, ws], h_lo[:, k, :]),
                                     (w_lo[:, s, ws], h_hi[:, k, :]))
                        for n, (a, b) in enumerate(pairs):
                            mm = nc.tensor.matmul(bank[m][:], a, b, start=(k == 0 and n == 0),
                                                  stop=(k == KT - 1 and n == 2))
                    if c == NCH - 1:
                        mm.then_inc(bank_full, 1)
                if c < NCH - 1:
                    mm.then_inc(w_used, 1)

        def pe_group(pe, g, tokens_out, h_tiles):
            pe_chunks(pe, g, 0, NCH, tokens_out, h_tiles)

        def full(eng, g, m):
            eng.wait_ge(bank_full, 4 * g + m + 1 + FULL0)

        def act_evac(act, g, dst, func=ACT.Copy, scale=1.0, before=None):
            for m in range(4):
                full(act, g, m)
                nc.scalar.activation(dst(m), bank[m][:], func, scale=scale).then_inc(bank_free[m], 1)

        def dve_mod(v, n):
            v.wait_ge(mod_out, 16 * (n + 1))
            for c in range(NCH):
                v.wait_ge(mod_in[c % 2], 16 * (4 * n + c // 2 + 1))
                for kk in range(CH):
                    k = CH * c + kk
                    slab = page(MOD_RING + 2 * (c % 2) + kk)
                    if k == 0:
                        nc.vector.tensor_scalar(page(MOD_ACC), slab, c_silu[:, 0:1], None,
                                                ALU.mult).then_inc(mod_sum.sem, 1)
                    else:
                        v.wait_ge(mod_sum.sem, mod_sum.at(f"k{k - 1}", n))
                        nc.vector.scalar_tensor_tensor(page(MOD_ACC), slab, c_silu[:, k:k + 1], page(MOD_ACC),
                                                       ALU.mult, ALU.add).then_inc(mod_sum.sem, 1)

        def ride(g0):
            return next(r for r in RIDES if r[0] == g0)

        def dve_mods(v, g0, i=0):
            _, _, per, block0 = ride(g0)
            for b in range(per):
                dve_mod(v, block0 + per * i + b)

        def act_mods(act, g0, i=0):
            _, _, per, block0 = ride(g0)
            for b in range(per):
                act_mod(act, block0 + per * i + b)

        def act_mod(act, n):
            act.wait_ge(mod_sum.sem, mod_sum.at(f"k{KT - 1}", n))
            act.dma_start(mod_mid[bass.ds(n, 1)].rearrange("a p n -> p (a n)"), page(MOD_ACC)).then_inc(mod_out, 16)

        tile_val = sem("tile_val")
        tile_turned = sem("tile_turned")
        turns = {0: 0, 2: 1, 3: 2, 4: 3, 6: 4}

        def pe_turn(pe, r, lhs, diag, first, last):
            q = turns[r]
            for f in range(first, last):
                if f >= 4:
                    pe.wait_ge(tile_val, KT * q + f - 3)
                for t in range(TT):
                    dst = bank[4 + f % 4][:, t * P:(t + 1) * P]
                    if diag is None:
                        mm = nc.tensor.transpose(dst, lhs(f, t), ident[:])
                    else:
                        mm = nc.tensor.matmul(dst, lhs(f, t), diag[:, t, :], start=True, stop=True)
                mm.then_inc(tile_turned, 1)

        def pe_turned_group(pe, g, tokens_out, r, lhs, diag):
            pe_turn(pe, r, lhs, diag, 0, 4)
            for c in range(NCH):
                pe_chunks(pe, g, c, c + 1, tokens_out, KT * r)
                pe_turn(pe, r, lhs, diag, min(4 + 2 * c, KT), min(6 + 2 * c, KT))

        def act_turn(act, r, tmp, gain=None, shift=None):
            q = turns[r]
            for f in range(KT):
                act.wait_ge(tile_turned, KT * q + f + 1)
                if f >= 4:
                    act.wait_ge(h_ready, KT * r + f - 3)
                if gain is None:
                    nc.scalar.copy(page(tmp + f % 4), bank[4 + f % 4][:]).then_inc(tile_val, 1)
                else:
                    nc.scalar.activation(page(tmp + f % 4), bank[4 + f % 4][:], ACT.Identity,
                                         bias=shift(f), scale=gain(f)).then_inc(tile_val, 1)

        def dve_turn(v, r, tmp):
            q = turns[r]
            for f in range(KT):
                v.wait_ge(tile_val, KT * q + f + 1)
                nc.vector.tensor_copy(h_hi[:, f, :], page(tmp + f % 4)).then_inc(h_hi_done, 1)
                v.wait_ge(h_hi_done, KT * r + f + 1)
                nc.vector.tensor_tensor(h_lo[:, f, :], page(tmp + f % 4), h_hi[:, f, :].bitcast(F32),
                                        ALU.subtract).then_inc(h_ready, 1)

        def act_split(act, src):
            for f in range(KT):
                nc.scalar.copy(h_hi[:, f, :], page(src(f))).then_inc(h_hi_done, 1)

        def dve_split(v, r, src):
            for f in range(KT):
                v.wait_ge(h_hi_done, KT * r + f + 1)
                nc.vector.tensor_tensor(h_lo[:, f, :], page(src(f)), h_hi[:, f, :].bitcast(F32),
                                        ALU.subtract).then_inc(h_ready, 1)

        diag = page(DIAG).rearrange("p (t n) -> p t n", n=P)
        xp = arena[:, XP:XP + 16, :].rearrange("p a n -> p (a n)").rearrange("p (t n) -> p t n", n=D)
        norm_a = steps("norm_a", "root")
        norm_v = steps("norm_v", "total rstd d0 d1 d2 d3")

        def act_norm(act, q):
            act.wait_ge(norm_v.sem, norm_v.at("total", q))
            nc.scalar.activation(root, token_sum, ACT.Sqrt, bias=eps[:], scale=1.0 / D).then_inc(norm_a.sem, 1)

        def dve_norm(v, q):
            nc.vector.tensor_reduce(token_sum, square_sum, AX.X, ALU.add).then_inc(norm_v.sem, 1)
            v.wait_ge(norm_a.sem, norm_a.at("root", q))
            nc.vector.reciprocal(rstd, root).then_inc(norm_v.sem, 1)
            v.wait_ge(norm_v.sem, norm_v.at("rstd", q))
            for t in range(TT):
                nc.vector.tensor_scalar(diag[:, t, :], ident[:], rstd[:, t:t + 1], None,
                                        ALU.mult).then_inc(norm_v.sem, 1)

        mod_loaded = sem("mod_loaded")
        modc_p = steps("modc_p", "sum")
        modc_v = steps("modc_v", "shift scale one gain")
        gate_loaded = sem("gate_loaded")
        modg_p = steps("modg_p", "g0 g1 g2 g3")
        modg_v = steps("modg_v", "g0 g1 g2 g3")
        MODC = 16

        def act_load_mod(act, q):
            act.wait_ge(mod_out, 16 * (MODS + 1))
            act.dma_start(arena[:, MODC:MODC + 8, :],
                          mod_mid[q * MOD_BLOCKS:q * MOD_BLOCKS + 8].rearrange("b p n -> p b n")).then_inc(mod_loaded, 16)

        def pe_mod_cols(pe, q):
            pe.wait_ge(mod_loaded, 16 * (q + 1))
            for b in range(8):
                for j in range(W // P):
                    mm = nc.tensor.matmul(bank[4][:, 4 * b + j:4 * b + j + 1], page(MODC + b)[:, j * P:(j + 1) * P],
                                          one[:], start=True, stop=True)
            mm.then_inc(modc_p.sem, 1)
            pe.wait_ge(modc_v.sem, modc_v.at("scale", q))

        def dve_mod_cols(v, q):
            v.wait_ge(modc_p.sem, modc_p.at("sum", q))
            nc.vector.tensor_tensor(mod_shift, bank[4][:, 0:KT], col(f"shift_b{q + 2}", 0, KT),
                                    ALU.add).then_inc(modc_v.sem, 1)
            nc.vector.tensor_tensor(mod_scale, bank[4][:, KT:2 * KT], col(f"scale_b{q + 2}", 0, KT),
                                    ALU.add).then_inc(modc_v.sem, 1)
            v.wait_ge(modc_v.sem, modc_v.at("scale", q))
            nc.vector.tensor_scalar(mod_scale, mod_scale, 1.0, None, ALU.add).then_inc(modc_v.sem, 1)
            v.wait_ge(modc_v.sem, modc_v.at("one", q))
            nc.vector.tensor_tensor(mod_scale, mod_scale, col(f"norm{q + 2}", 0, KT), ALU.mult).then_inc(modc_v.sem, 1)

        def act_load_gate(act, lay):
            q = lay - 2
            act.dma_start(arena[:, MACC:MACC + 4, :],
                          mod_mid[q * MOD_BLOCKS + 8:(q + 1) * MOD_BLOCKS].rearrange("b p n -> p b n")).then_inc(gate_loaded, 16)
            act.dma_start(page(GATE, 4), row(f"gate_b{lay}", D)).then_inc(gate_loaded, 16)

        def pe_gate(pe, lay):
            pe.wait_ge(gate_loaded, 32 * (lay - 1))
            for n in range(4):
                nc.tensor.matmul(bank[4 + n][:], ones[:], page(MACC + n), start=True, stop=True).then_inc(modg_p.sem, 1)

        def dve_gate(v, lay):
            for n in range(4):
                v.wait_ge(modg_p.sem, modg_p.at(f"g{n}", lay - 2))
                nc.vector.tensor_tensor(page(GATE + n), bank[4 + n][:], page(GATE + n), ALU.add).then_inc(modg_v.sem, 1)
            v.wait_ge(modg_v.sem, modg_v.at("g3", lay - 2))

        old_in = sem("old_in")
        res_v = steps("res_v", "s0 s1 s2 s3")
        res_a = steps("res_a", "q0 q1 q2 q3")
        new_out = sem("new_out")
        res_task = {0: 0, 1: 0, 2: 0, 3: 4}

        def cols_of(dram, n):
            return dram.rearrange("(t p) n -> p t n", p=P)[:, :, n * W:(n + 1) * W]

        def act_residual(act, lay, g0, src, gated, store):
            def summed(n, t):
                if gated:
                    act.wait_ge(res_v.sem, res_v.at(f"s{t}", res_task[lay] + n))
                else:
                    act.wait_ge(bank_free[t], g0 + n + 2)

            act.wait_ge(h_ready, KT * (2 * lay + 2))
            act.wait_ge(new_out, (0, 64, 80, 144)[lay])
            if gated:
                act_load_gate(act, lay)
            if lay == 1:
                act_load_final(act, 0)
            if lay == 3:
                act_load_final(act, 1)
            for n in range(4):
                for ahead in ((0, 1) if n == 0 else (n + 1,) if n < 3 else ()):
                    act.dma_start(arena[:, XR + 4 * (ahead % 2):XR + 4 * (ahead % 2) + 4, :],
                                  cols_of(src, ahead)).then_inc(old_in, 16)
                    act.wait_ge(old_in, 16 * (4 * lay + ahead + 1))
                if lay == 0:
                    act_mods(act, G_OUT1, n)
                if lay == 1 and n:
                    act_mods(act, G_OUT2 + 1, n - 1)
                for t in range(TT):
                    summed(n, t)
                    act.wait_ge(res_a.sem, res_a.at(f"q{t - 1}", 4 * lay + n) if t else
                                res_a.at("q3", 4 * lay + n, back=1))
                    nc.scalar.activation(page(JUNK), xp[:, t, n * W:(n + 1) * W], ACT.Square,
                                         accum_out=square_sum[:, t, n:n + 1]).then_inc(res_a.sem, 1)
                if store:
                    act.dma_start(cols_of(x_mid, n), xp[:, :, n * W:(n + 1) * W]).then_inc(new_out, 16)

        def dve_residual(v, lay, g0, gated):
            if gated:
                dve_gate(v, lay)
            for n in range(4):
                if lay == 0:
                    dve_mods(v, G_OUT1, n)
                if lay == 1 and n:
                    dve_mods(v, G_OUT2 + 1, n - 1)
                v.wait_ge(old_in, 16 * (4 * lay + n + 1))
                for t in range(TT):
                    new = xp[:, t, n * W:(n + 1) * W]
                    old = page(XR + 4 * (n % 2) + t)
                    full(v, g0 + n, t)
                    if gated:
                        v.wait_ge(res_v.sem, res_v.at(f"s{t}", res_task[lay] + n, back=1))
                        nc.vector.tensor_tensor(page(TMP + t), bank[t][:], page(GATE + n),
                                                ALU.mult).then_inc(bank_free[t], 1)
                    else:
                        nc.vector.tensor_tensor(new, bank[t][:], old, ALU.add).then_inc(bank_free[t], 1)
                if gated:
                    for t in range(TT):
                        v.wait_ge(bank_free[t], g0 + n + 2)
                        nc.vector.tensor_tensor(xp[:, t, n * W:(n + 1) * W], page(TMP + t),
                                                page(XR + 4 * (n % 2) + t), ALU.add).then_inc(res_v.sem, 1)

        final_in = sem("final_in")
        final_v = steps("final_v", "clear r0 r1 r2 r3")
        final_a = steps("final_a", "q0 q1 q2 q3")

        def act_load_final(act, q):
            act.dma_start(page(ROWS, 4), row(f"final{q}", D)).then_inc(final_in, 16)

        def dve_final(v, q):
            v.wait_ge(norm_v.sem, norm_v.at("total", 2 + 3 * q))
            nc.vector.memset(small[:, 0:16], 0.0).then_inc(final_v.sem, 1)
            v.wait_ge(final_in, 16 * (q + 1))
            for t in range(TT):
                nc.vector.scalar_tensor_tensor(xp[:, t, :], xp[:, t, :], rstd[:, t:t + 1], page(ROWS, 4),
                                               ALU.mult, ALU.mult).then_inc(final_v.sem, 1)

        def act_final(act, q):
            act.wait_ge(final_v.sem, final_v.at("clear", q))
            for t in range(TT):
                act.wait_ge(final_v.sem, final_v.at(f"r{t}", q))
                act.wait_ge(final_a.sem, final_a.at(f"q{t - 1}", q) if t else final_a.at("q3", q, back=1))
                nc.scalar.activation(page(JUNK, 4), xp[:, t, :], ACT.Square,
                                     accum_out=square_sum[:, t, 0:1]).then_inc(final_a.sem, 1)

        lru_in = sem("lru_in")
        lru_p = steps("lru_p", "a0 x0 a1 x1")
        lru_a = steps("lru_a", "sr0 si0 sr1 si1 tanh0 exp0 tanh1 exp1 sqrt0 sqrt1")
        lru_v = steps("lru_v", "c2 c0 c1 c3 ix0 ix1 q0 q1 u0 u1 h0 h1 y yg")

        def pe_lru(pe, j):
            pe.wait_ge(lru_in, 16 * (j + 1))
            pe.wait_ge(lru_v.sem, lru_v.at("c3", j))
            pe.wait_ge(lru_a.sem, lru_a.at("si1", j, back=1))
            for n in range(4):
                nc.tensor.matmul(bank[4 + n][:], page(LW)[:, n * P:(n + 1) * P], page(XC),
                                 start=True, stop=True).then_inc(lru_p.sem, 1)

        def act_lru(act, j):
            act.wait_ge(lru_p.sem, lru_p.at("x1", j, back=1))
            act.dma_start(page(LW), lru_w[bass.ds(j, 1)].rearrange("a p n -> p (a n)")).then_inc(lru_in, 16)
            act.wait_ge(lru_v.sem, lru_v.at("yg", j, back=1))
            for n, (bias, dst) in enumerate((("ba", GR0), ("bx", GI0), ("ba", GR1), ("bx", GI1))):
                act.wait_ge(lru_p.sem, lru_p.at(("a0", "x0", "a1", "x1")[n], j))
                nc.scalar.activation(page(dst), bank[4 + n][:], ACT.Sigmoid,
                                     bias=col(bias, LRU_TILES * (n // 2) + j)).then_inc(lru_a.sem, 1)
            for d, gr in ((0, GR0), (1, GR1)):
                decay = [x[:, bass.ds(LRU_TILES * d + j, 1)] for x in (lru_half, lru_decay)]
                act.wait_ge(lru_a.sem, lru_a.at(f"sr{d}", j))
                nc.scalar.activation(page(TH + d), page(gr), ACT.Tanh, scale=decay[0]).then_inc(lru_a.sem, 1)
                nc.scalar.activation(page(EA + d), page(gr), ACT.Exp, scale=decay[1]).then_inc(lru_a.sem, 1)
            for d in range(2):
                act.wait_ge(lru_a.sem, lru_a.at(f"tanh{d}", j))
                nc.scalar.activation(page(TH + d), page(TH + d), ACT.Sqrt, scale=-1.0).then_inc(lru_a.sem, 1)

        def dve_lru(v, j):
            own = lambda name: v.wait_ge(lru_v.sem, lru_v.at(name, j))
            from_act = lambda name: v.wait_ge(lru_a.sem, lru_a.at(name, j))
            x, xc = page(P_XL + j), page(XC)
            cw = lambda w: col("conv_w", LRU_TILES * w + j)
            nc.vector.tensor_scalar(xc, x, cw(2), col("conv_b", j), ALU.mult, ALU.add).then_inc(lru_v.sem, 1)
            own("c2")
            nc.vector.scalar_tensor_tensor(xc[:, 2:S], arena_cols(P_XL + j, 0, S - 2), cw(0), xc[:, 2:S],
                                           ALU.mult, ALU.add).then_inc(lru_v.sem, 1)
            own("c0")
            nc.vector.scalar_tensor_tensor(xc[:, 1:S], arena_cols(P_XL + j, 0, S - 1), cw(1), xc[:, 1:S],
                                           ALU.mult, ALU.add).then_inc(lru_v.sem, 1)
            own("c1")
            nc.vector.scalar_tensor_tensor(xc[:, 0:S - 1], arena_cols(P_XL + j, 1, S), cw(3), xc[:, 0:S - 1],
                                           ALU.mult, ALU.add).then_inc(lru_v.sem, 1)
            own("c3")
            for d, gi in ((0, GI0), (1, GI1)):
                from_act(f"si{d}")
                nc.vector.tensor_tensor(page(gi), page(gi), xc, ALU.mult).then_inc(lru_v.sem, 1)
            for d, gi in ((0, GI0), (1, GI1)):
                from_act(f"exp{d}")
                own(f"ix{d}")
                nc.vector.scalar_tensor_tensor(page(gi), page(EA + d), 1.0, page(gi), ALU.add,
                                               ALU.mult).then_inc(lru_v.sem, 1)
            for d, gi in ((0, GI0), (1, GI1)):
                from_act(f"sqrt{d}")
                own(f"q{d}")
                nc.vector.tensor_tensor(page(gi), page(gi), page(TH + d), ALU.mult).then_inc(lru_v.sem, 1)
            for d, gr, gi in ((0, GR0, GI0), (1, GR1, GI1)):
                own(f"u{d}")
                turn = slice(None, None, -1) if d else slice(None)
                nc.vector.tensor_tensor_scan(page(HB + d)[:, turn], page(EA + d)[:, turn], page(gi)[:, turn], 0.0,
                                             ALU.mult, ALU.add).then_inc(lru_v.sem, 1)
            own("h1")
            nc.vector.tensor_tensor(page(HB), page(HB), page(HB + 1), ALU.add).then_inc(lru_v.sem, 1)
            own("y")
            nc.vector.tensor_tensor(page(P_XL + j), page(HB), page(P_GL + j), ALU.mult).then_inc(lru_v.sem, 1)

        def arena_cols(pg, a, b):
            if isinstance(pg, int):
                return arena[:, pg, a:b]
            return arena[:, bass.ds(pg, 1), a:b].rearrange("p a n -> p (a n)")

        class Attention:

            def __init__(self, tag, normed, masked, lo, hi, pages):
                self.normed, self.masked, self.lo, self.hi, self.pg = normed, masked, lo, hi, pages
                rot = "n g A Bl Bh r" if normed else "A Bl Bh r"
                self.kv_v = steps(tag + "_kv_v", rot + " vc")
                self.kv_p = steps(tag + "_kv_p", "turned")
                self.kv_a = steps(tag + "_kv_a", "kT")
                self.q_v = steps(tag + "_q_v", rot)
                score = ["add{0}", "max{0}", "bias{0}"] if masked else ["max{0}", "bias{0}"]
                names = []
                for pair in ((0, 1), (2, 3)):
                    names += [x.format(t) for t in pair for x in score]
                    names += [f"{x}{t}" for t in pair for x in ("rec", "norm")]
                self.s_v = steps(tag + "_s_v", names + ["out"])
                self.p = steps(tag + "_p", "q s0 s1 t0 t1 s2 s3 t2 t3 o")
                self.a = steps(tag + "_a", "qT e0 e1 T0 T1 e2 e3 T2 T3")

            def rotate(self, v, st, task, src, dst, rs, gain):
                pg = self.pg
                tok = lambda p: page(p).rearrange("p (t n) -> p t n", n=HD)
                x = src
                if self.normed:
                    nc.vector.tensor_tensor(tok(pg["X"]), x, rs, ALU.mult).then_inc(st.sem, 1)
                    v.wait_ge(st.sem, st.at("n", task))
                    nc.vector.tensor_tensor(tok(pg["X"]), tok(pg["X"]), gain, ALU.mult).then_inc(st.sem, 1)
                    v.wait_ge(st.sem, st.at("g", task))
                    x = tok(pg["X"])
                nc.vector.tensor_tensor(tok(pg["A"]), x, tok(pg["C"]), ALU.mult).then_inc(st.sem, 1)
                lo, hi = self.lo, self.hi
                nc.vector.tensor_tensor(lo(tok(pg["B"])), hi(x), lo(tok(pg["S"])), ALU.mult).then_inc(st.sem, 1)
                nc.vector.tensor_tensor(hi(tok(pg["B"])), lo(x), hi(tok(pg["S"])), ALU.mult).then_inc(st.sem, 1)
                v.wait_ge(st.sem, st.at("Bh", task))
                nc.vector.tensor_tensor(page(dst), page(pg["A"]), page(pg["B"]), ALU.add).then_inc(st.sem, 1)

            def dve_kv(self, v, i, head, k, val, rs=None, gain=None):
                v.wait_ge(self.s_v.sem, self.s_v.at("out", head, back=1))
                v.wait_ge(self.kv_p.sem, self.kv_p.at("turned", i, back=1))
                self.rotate(v, self.kv_v, i, k, self.pg["kcur"], rs, gain)
                nc.vector.tensor_copy(page(self.pg["vcur"]).rearrange("p (t n) -> p t n", n=HD),
                                      val).then_inc(self.kv_v.sem, 1)

            def dve_q(self, v, i, kv, q, rs=None, gain=None):
                v.wait_ge(self.kv_v.sem, self.kv_v.at("vc", kv))
                v.wait_ge(self.p.sem, self.p.at("q", i, back=1))
                self.rotate(v, self.q_v, i, q, self.pg["qcur"], rs, gain)

            def pe_kv(self, pe, i, head):
                pe.wait_ge(self.kv_v.sem, self.kv_v.at("r", i))
                pe.wait_ge(self.s_v.sem, self.s_v.at("out", head, back=1))
                for t in range(TT):
                    mm = nc.tensor.transpose(bank[6][:, t * P:(t + 1) * P],
                                             page(self.pg["kcur"])[:, t * P:(t + 1) * P], ident[:])
                mm.then_inc(self.kv_p.sem, 1)

            def act_kv(self, act, i):
                act.wait_ge(self.kv_p.sem, self.kv_p.at("turned", i))
                nc.scalar.copy(page(self.pg["kT"]), bank[6][:]).then_inc(self.kv_a.sem, 1)

            def pe_queries(self, pe, i):
                pe.wait_ge(self.q_v.sem, self.q_v.at("r", i))
                pe.wait_ge(self.s_v.sem, self.s_v.at("out", i, back=1))
                for t in range(TT):
                    mm = nc.tensor.transpose(bank[4][:, t * P:(t + 1) * P],
                                             page(self.pg["qcur"])[:, t * P:(t + 1) * P], ident[:])
                mm.then_inc(self.p.sem, 1)

            def pe_scores(self, pe, i, kv, pair):
                pe.wait_ge(self.kv_a.sem, self.kv_a.at("kT", kv))
                pe.wait_ge(self.a.sem, self.a.at("qT", i))
                for t in pair:
                    if t >= 2:
                        pe.wait_ge(self.a.sem, self.a.at(f"e{t - 2}", i))
                        if self.masked:
                            pe.wait_ge(self.s_v.sem, self.s_v.at(f"add{t - 2}", i))
                    nc.tensor.matmul(bank[5 + t % 2][:], page(self.pg["qT"])[:, t * P:(t + 1) * P],
                                     page(self.pg["kT"]), start=True, stop=True).then_inc(self.p.sem, 1)

            def turn_bank(self, t):
                return bank[4 if t % 2 else 7]

            def pe_turn_probs(self, pe, i, pair):
                for t in pair:
                    pe.wait_ge(self.s_v.sem, self.s_v.at(f"norm{t}", i))
                    if t >= 2:
                        pe.wait_ge(self.a.sem, self.a.at(f"T{t - 2}", i))
                    for k in range(TT):
                        mm = nc.tensor.transpose(self.turn_bank(t)[:, k * P:(k + 1) * P],
                                                 page(self.pg["P"] + t % 2)[:, k * P:(k + 1) * P], ident[:])
                    mm.then_inc(self.p.sem, 1)

            def pe_values(self, pe, i, kv):
                pe.wait_ge(self.a.sem, self.a.at("T3", i))
                pe.wait_ge(self.kv_v.sem, self.kv_v.at("vc", kv))
                for k in range(TT):
                    mm = nc.tensor.matmul(bank[4][:], page(self.pg["vcur"])[:, k * P:(k + 1) * P],
                                          page(self.pg["PT"] + k), start=(k == 0), stop=(k == TT - 1))
                mm.then_inc(self.p.sem, 1)

            def act_head(self, act, i):
                pg, p, sv = self.pg, self.p, self.s_v
                act.wait_ge(p.sem, p.at("q", i))
                nc.scalar.copy(page(pg["qT"]), bank[4][:]).then_inc(self.a.sem, 1)
                for pair in ((0, 1), (2, 3)):
                    for t in pair:
                        act.wait_ge(sv.sem, sv.at(f"bias{t}", i))
                        src = page(pg["A"] + t % 2) if self.masked else bank[5 + t % 2][:]
                        nc.scalar.activation(page(pg["P"] + t % 2), src, ACT.Exp, bias=row_bias[:, t % 2:t % 2 + 1],
                                             scale=SCALE, accum_out=row_sum[:, t % 2:t % 2 + 1]).then_inc(self.a.sem, 1)
                    for t in pair:
                        act.wait_ge(p.sem, p.at(f"t{t}", i))
                        nc.scalar.copy(arena[:, pg["PT"]:pg["PT"] + TT, t * P:(t + 1) * P],
                                       self.turn_bank(t)[:].rearrange("p (k n) -> p k n", n=P)).then_inc(self.a.sem, 1)

            def dve_head(self, v, i, out):
                pg, p, sv = self.pg, self.p, self.s_v
                for pair in ((0, 1), (2, 3)):
                    for t in pair:
                        b = t % 2
                        v.wait_ge(p.sem, p.at(f"s{t}", i))
                        src = bank[5 + b][:]
                        if self.masked:
                            nc.vector.tensor_tensor(page(pg["A"] + b), src, page(pg["mask"] + t),
                                                    ALU.add).then_inc(sv.sem, 1)
                            v.wait_ge(sv.sem, sv.at(f"add{t}", i))
                            src = page(pg["A"] + b)
                        nc.vector.tensor_reduce(row_max[:, b:b + 1], src, AX.X, ALU.max).then_inc(sv.sem, 1)
                        v.wait_ge(sv.sem, sv.at(f"max{t}", i))
                        nc.vector.tensor_scalar(row_bias[:, b:b + 1], row_max[:, b:b + 1], -SCALE, None,
                                                ALU.mult).then_inc(sv.sem, 1)
                    for t in pair:
                        b = t % 2
                        v.wait_ge(self.a.sem, self.a.at(f"e{t}", i))
                        nc.vector.reciprocal(row_rec[:, b:b + 1], row_sum[:, b:b + 1]).then_inc(sv.sem, 1)
                        v.wait_ge(sv.sem, sv.at(f"rec{t}", i))
                        nc.vector.tensor_scalar(page(pg["P"] + b), page(pg["P"] + b), row_rec[:, b:b + 1], None,
                                                ALU.mult).then_inc(sv.sem, 1)
                v.wait_ge(p.sem, p.at("o", i))
                nc.vector.tensor_copy(out, bank[4][:]).then_inc(sv.sem, 1)

        def halves(n, first):
            def pick(ap):
                if 2 * n == HD:
                    return ap[:, :, 0:n] if first else ap[:, :, n:]
                v4 = ap.rearrange("p t (b h e) -> p t b h e", h=2, e=n)
                return v4[:, :, :, 0 if first else 1, :]
            return pick

        att1 = Attention("att1", True, False, halves(HD // 4, True), halves(HD // 4, False),
                         dict(C=36, S=37, A=38, B=39, qcur=40, kcur=41, vcur=42, qT=43, kT=44, P=45, X=47, PT=P_GL + 4))
        att3 = Attention("att3", False, True, halves(HD // 2, True), halves(HD // 2, False),
                         dict(C=32, S=33, A=34, B=35, qcur=36, kcur=37, vcur=38, qT=39, kT=40, P=41, PT=43, mask=47))

        QK = HEADS + KV_HEADS
        qkv = arena[:, P_QKV:P_QKV + 12, :].rearrange("p a n -> p (a n)").rearrange("p (t n) -> p t n", t=TT)
        gains = page(48)[:, 0:2 * HD]
        qk_v = steps("qk_v", "q0 r0 q1 r1 q2 r2 q3 r3 rec")
        qk_a = steps("qk_a", "root")
        rope_in = sem("rope_in")
        head_sq3 = head_sq[:, 0:TT * QK].rearrange("p (t n) -> p t n", t=TT)
        head_rs3 = head_rstd[:, 0:TT * QK].rearrange("p (t n) -> p t n", t=TT)

        def act_load_rope(act, lay, att):
            act.dma_start(page(att.pg["C"], 2), rope_d[lay]).then_inc(rope_in, 16)

        def dve_qk_stats(v):
            for t in range(TT):
                sq = page(P_XL, 3)[:, 0:QK * HD]
                if t:
                    v.wait_ge(qk_v.sem, qk_v.at(f"r{t - 1}"))
                nc.vector.tensor_tensor(sq, qkv[:, t, 0:QK * HD], qkv[:, t, 0:QK * HD], ALU.mult).then_inc(qk_v.sem, 1)
                v.wait_ge(qk_v.sem, qk_v.at(f"q{t}"))
                nc.vector.tensor_reduce(head_sq3[:, t, :], sq.rearrange("p (h n) -> p h n", n=HD), AX.X,
                                        ALU.add).then_inc(qk_v.sem, 1)
            v.wait_ge(qk_a.sem, qk_a.at("root"))
            nc.vector.reciprocal(head_rstd[:, 0:TT * QK], head_rstd[:, 0:TT * QK]).then_inc(qk_v.sem, 1)
            v.wait_ge(qk_v.sem, qk_v.at("rec"))

        def head_cols(x, base, h):
            return x[:, :, bass.ds(base + h * HD, HD)]

        def rs_of(h):
            return head_rs3[:, :, bass.ds(h, 1)].to_broadcast([P, TT, HD])

        def gain_of(n):
            g = gains[:, n * HD:(n + 1) * HD]
            return g.rearrange("p (o n) -> p o n", o=1).to_broadcast([P, TT, HD])

        v3 = arena[:, P_MV:P_MV + 16, :].rearrange("p a n -> p (a n)").rearrange("p (t n) -> p t n", t=TT)
        gate_in = sem("gate_in")
        tri_in = sem("tri_in")
        gain_in = sem("gain_in")
        gate_p = steps("gate_p", "tok rows cols")
        gate_a = steps("gate_a", "i f abs exp ln em")
        gate_v = steps("gate_v", "bias lf Ff Fb g Mf Mb m cols")
        m_p = steps("m_p", "Mf Mb s0 s1 s2 s3 den n0 n1 n2 n3")
        m_a = steps("m_a", "k nf nb xf0 xb0 xf1 xb1 xf2 xb2 xf3 xb3 c0 c1 c2 c3 back")
        m_v = steps("m_v", ["Mh"] + [f"{x}{i}" for i in range(TT) for x in ("ef", "eb", "pf", "pb", "mf", "mb")]
                    + "dcopy dabs dmax drec n0 n1 n2 n3".split())
        o_v = steps("o_v", [f"{x}{t}" for t in range(TT) for x in "gsr"])
        z_v = steps("z_v", [f"{x}{t}" for t in range(TT) for x in "nwz"])
        m_root = sem("m_root")
        m_rec = sem("m_rec")
        gtok = page(GTOK)
        rows8 = lambda p: arena[0:8, p:p + 2, :].rearrange("p a n -> p (a n)")
        row8 = lambda p: arena[0:8, p, :]
        R_I, R_F, R_L, R_S, R_G = 33, 35, 37, 39, 41
        back = slice(None, None, -1)

        def pe_gates(pe):
            pe.wait_ge(gate_in, 32)
            pe.wait_ge(h_ready, 3 * KT)
            for t in range(TT):
                for part in (h_hi, h_lo):
                    for k in range(KT):
                        mm = nc.tensor.matmul(bank[4][:, t * 32:(t + 1) * 32],
                                              part[:, k, t * P:(t + 1) * P].bitcast(F32),
                                              page(GW)[:, k * 32:(k + 1) * 32],
                                              start=(k == 0 and part is h_hi), stop=(k == KT - 1 and part is h_lo))
            mm.then_inc(gate_p.sem, 1)

        def pe_gate_rows(pe):
            pe.wait_ge(gate_v.sem, gate_v.at("bias"))
            for n in range(4):
                for t in range(TT):
                    mm = nc.tensor.transpose(bank[4 + n][0:8, t * P:(t + 1) * P],
                                             gtok[:, t * 32 + 8 * n:t * 32 + 8 * n + 8], ident[:])
            mm.then_inc(gate_p.sem, 1)

        def pe_gate_cols(pe):
            pe.wait_ge(gate_v.sem, gate_v.at("Mb"))
            pe.wait_ge(gate_a.sem, gate_a.at("em"))
            for n, src in enumerate((R_G, R_G + 1, R_L, R_L + 1)):
                for t in range(TT):
                    mm = nc.tensor.transpose(bank[4][:, n * 32 + t * 8:n * 32 + t * 8 + 8],
                                             row8(src)[:, t * P:(t + 1) * P], ident[0:8, 0:8])
            mm.then_inc(gate_p.sem, 1)

        def act_gates(act):
            act.wait_ge(gate_p.sem, gate_p.at("rows"))
            for n, dst in enumerate((R_I, R_F)):
                nc.scalar.copy(row8(dst), bank[4 + 2 * n][0:8, :])
                nc.scalar.copy(row8(dst + 1), bank[5 + 2 * n][0:8, :]).then_inc(gate_a.sem, 1)
            act.wait_ge(gate_a.sem, gate_a.at("f"))
            nc.scalar.activation(rows8(R_L), rows8(R_F), ACT.Abs).then_inc(gate_a.sem, 1)
            act.wait_ge(gate_a.sem, gate_a.at("abs"))
            nc.scalar.activation(rows8(R_L), rows8(R_L), ACT.Exp, scale=-1.0).then_inc(gate_a.sem, 1)
            act.wait_ge(gate_a.sem, gate_a.at("exp"))
            nc.scalar.activation(rows8(R_L), rows8(R_L), ACT.Ln, bias=one[0:8]).then_inc(gate_a.sem, 1)
            act.wait_ge(gate_v.sem, gate_v.at("m"))
            nc.scalar.activation(rows8(R_L), rows8(R_S), ACT.Exp, scale=-1.0).then_inc(gate_a.sem, 1)

        def dve_gates(v):
            v.wait_ge(gate_p.sem, gate_p.at("tok"))
            bias = gtok[:, 128:160].rearrange("p (o n) -> p o n", o=1).to_broadcast([P, TT, 32])
            nc.vector.tensor_tensor(gtok[:, 0:128].rearrange("p (t n) -> p t n", n=32),
                                    bank[4][:, 0:128].rearrange("p (t n) -> p t n", n=32), bias,
                                    ALU.add).then_inc(gate_v.sem, 1)
            v.wait_ge(gate_a.sem, gate_a.at("ln"))
            nc.vector.scalar_tensor_tensor(rows8(R_F), rows8(R_F), 0.0, rows8(R_L), ALU.min,
                                           ALU.subtract).then_inc(gate_v.sem, 1)
            v.wait_ge(gate_v.sem, gate_v.at("lf"))
            for n, turn in ((0, slice(None)), (1, back)):
                nc.vector.tensor_tensor_scan(row8(R_S + n)[:, turn], one[0:8].to_broadcast([8, S]),
                                             row8(R_F + n)[:, turn], 0.0, ALU.mult, ALU.add).then_inc(gate_v.sem, 1)
            v.wait_ge(gate_v.sem, gate_v.at("Fb"))
            nc.vector.tensor_tensor(rows8(R_G), rows8(R_I), rows8(R_S), ALU.subtract).then_inc(gate_v.sem, 1)
            v.wait_ge(gate_v.sem, gate_v.at("g"))
            for n, turn in ((0, slice(None)), (1, back)):
                nc.vector.tensor_tensor_scan(row8(MROW + n)[:, turn], row8(R_G + n)[:, turn],
                                             row8(R_G + n)[:, turn], 0.0, ALU.max, ALU.max).then_inc(gate_v.sem, 1)
            v.wait_ge(gate_v.sem, gate_v.at("Mb"))
            nc.vector.tensor_tensor(rows8(R_S), rows8(R_S), rows8(MROW), ALU.add).then_inc(gate_v.sem, 1)
            v.wait_ge(gate_p.sem, gate_p.at("cols"))
            nc.vector.tensor_copy(m_cols[:], bank[4][:, 0:P]).then_inc(gate_v.sem, 1)
            v.wait_ge(gate_v.sem, gate_v.at("cols"))

        def fwd(p, i):
            return arena[:, p, i * P:S]

        def bwd(p, i):
            return arena[:, p, 0:(i + 1) * P]

        def pe_m_max(pe, h):
            pe.wait_ge(m_v.sem, m_v.at("Mh", h))
            for n in range(2):
                nc.tensor.matmul(bank[4 + n][:], ones[0:8, :], row8(HCUR + n), start=True,
                                 stop=True).then_inc(m_p.sem, 1)

        def pe_m_scores(pe, h, pair):
            pe.wait_ge(m_a.sem, m_a.at("k", h))
            for i in pair:
                st, name = ((m_a, "nf"), (m_a, "nb"), (m_v, "pb0"), (m_v, "pb1"))[i]
                pe.wait_ge(st.sem, st.at(name, h))
                nc.tensor.matmul(bank[4 + i % 2][:], page(KCUR)[:, i * P:(i + 1) * P], page(P_MQ + h),
                                 start=True, stop=True).then_inc(m_p.sem, 1)

        def pe_m_values(pe, h):
            pe.wait_ge(m_v.sem, m_v.at("mb3", h))
            tiles = lambda d, j: [i for i in range(TT) if (i <= j if d == 0 else i >= j)]
            for j in range(TT):
                for d in range(2):
                    for i in tiles(d, j):
                        mm = nc.tensor.matmul(bank[4][:, 4 * d + j:4 * d + j + 1],
                                              arena[:, PP + i + d, j * P:(j + 1) * P], one[:],
                                              start=(i == tiles(d, j)[0]), stop=(i == tiles(d, j)[-1]))
            mm.then_inc(m_p.sem, 1)
            for j in range(TT):
                if j >= 2:
                    pe.wait_ge(m_v.sem, m_v.at(f"n{j - 2}", h))
                for d in range(2):
                    for i in tiles(d, j):
                        mm = nc.tensor.matmul(bank[6 + j % 2][:, d * M_V:(d + 1) * M_V],
                                              arena[:, PP + i + d, j * P:(j + 1) * P],
                                              v3[:, i, bass.ds(h * M_V, M_V)],
                                              start=(i == tiles(d, j)[0]), stop=(i == tiles(d, j)[-1]))
                mm.then_inc(m_p.sem, 1)

        def pe_m_group(pe, g, h0):
            for n in range(2):
                h = h0 + n
                pe_m_max(pe, h)
                pe_chunks(pe, g, 4 * n, 4 * n + 1, True, 2 * KT)
                pe_m_scores(pe, h, (0, 1))
                pe_chunks(pe, g, 4 * n + 1, 4 * n + 2, True, 2 * KT)
                pe_m_scores(pe, h, (2, 3))
                pe_chunks(pe, g, 4 * n + 2, 4 * n + 3, True, 2 * KT)
                pe_m_values(pe, h)
                pe_chunks(pe, g, 4 * n + 3, 4 * n + 4, True, 2 * KT)

        hcur = arena[:, HCUR:HCUR + 2, :].rearrange("p a n -> p (a n)").rearrange("p (t n) -> p t n", t=TT)

        def act_mlstm(act, h):
            at = lambda st, name, back=0: act.wait_ge(st.sem, st.at(name, h, back))
            at(m_p, "s3", 1)
            nc.scalar.copy(page(KCUR), page(P_MK + h)).then_inc(m_a.sem, 1)
            for n, name in enumerate(("Mf", "Mb")):
                at(m_p, name)
                nc.scalar.copy(page(NM + n), bank[4 + n][:]).then_inc(m_a.sem, 1)
            for i in range(TT):
                for n, (name, part) in enumerate((("ef", fwd), ("eb", bwd))):
                    at(m_v, f"{name}{i}")
                    nc.scalar.activation(part(EE + n, i), part(EE + n, i), ACT.Exp).then_inc(m_a.sem, 1)
            at(m_v, "drec")
            for j in range(TT):
                at(m_p, f"n{j}")
                nc.scalar.activation(hcur[:, j, :], bank[6 + j % 2][:, 0:M_V], ACT.Copy,
                                     scale=den[:, j:j + 1]).then_inc(m_a.sem, 1)
            at(m_v, "n3")
            nc.scalar.copy(v3[:, :, bass.ds(h * M_V, M_V)], hcur).then_inc(m_a.sem, 1)

        def dve_mlstm(v, h):
            at = lambda st, name, back=0: v.wait_ge(st.sem, st.at(name, h, back))
            at(m_a, "back", 1)
            nc.vector.tensor_scalar(rows8(HCUR), rows8(MROW), ident[0:8, bass.ds(h, 1)], -1.0, ALU.mult,
                                    ALU.mult).then_inc(m_v.sem, 1)
            for i in range(TT):
                if i:
                    at(m_v, f"mb{i - 1}")
                for n, part in enumerate((fwd, bwd)):
                    at(m_a, "nf" if n == 0 else "nb")
                    nc.vector.tensor_scalar(part(EE + n, i), part(NM + n, i),
                                            m_cols[:, bass.ds(n * 32 + i * 8 + h, 1)], 0.0, ALU.add,
                                            ALU.min).then_inc(m_v.sem, 1)
                at(m_p, f"s{i}")
                for n, part in enumerate((fwd, bwd)):
                    at(m_a, ("xf" if n == 0 else "xb") + str(i))
                    scores = bank[4 + i % 2][:, i * P:S] if n == 0 else bank[4 + i % 2][:, 0:(i + 1) * P]
                    nc.vector.tensor_tensor(part(PP + i + n, i), scores, part(EE + n, i),
                                            ALU.mult).then_inc(m_v.sem, 1)
                for n in range(2):
                    at(m_v, ("pf" if n == 0 else "pb") + str(i))
                    own = arena[:, PP + i + n, i * P:(i + 1) * P]
                    nc.vector.tensor_tensor(own, own, page(TRI)[:, n * P:(n + 1) * P], ALU.mult).then_inc(m_v.sem, 1)
            at(m_p, "den")
            nc.vector.tensor_copy(den, bank[4][:, 0:8]).then_inc(m_v.sem, 1)
            at(m_v, "dcopy")
            nc.vector.scalar_tensor_tensor(den, den, -1.0, den, ALU.mult, ALU.max).then_inc(m_v.sem, 1)
            at(m_v, "dabs")
            floor = m_cols[:, 64:P].rearrange("p (n h) -> p n h", h=8)[:, :, bass.ds(h, 1)].rearrange("p n h -> p (n h)")
            nc.vector.tensor_tensor(den, den, floor, ALU.max).then_inc(m_v.sem, 1)
            at(m_v, "dmax")
            nc.vector.reciprocal(den, den).then_inc(m_v.sem, 1)
            at(m_v, "drec")
            for j in range(TT):
                at(m_a, f"c{j}")
                nc.vector.scalar_tensor_tensor(hcur[:, j, :], bank[6 + j % 2][:, M_V:2 * M_V], den[:, 4 + j:5 + j],
                                               hcur[:, j, :], ALU.mult, ALU.add).then_inc(m_v.sem, 1)

        def act_gate_evac(act, g, st, name, task, func):
            for t in range(TT):
                act.wait_ge(st.sem, st.at(f"{name}{t}", task, back=1))
                full(act, g, t)
                nc.scalar.activation(page(MO_TMP + t), bank[t][:], func).then_inc(bank_free[t], 1)

        def dve_mo(v, n):
            for t in range(TT):
                x, sq = v3[:, t, bass.ds(n * W, W)], page(MO_SQ + t)
                v.wait_ge(bank_free[t], G_MO + n + 2)
                nc.vector.tensor_tensor(x, x, page(MO_TMP + t), ALU.mult).then_inc(o_v.sem, 1)
                v.wait_ge(o_v.sem, o_v.at(f"g{t}", n))
                v.wait_ge(o_v.sem, o_v.at(f"r{t}", n, back=1))
                nc.vector.tensor_tensor(sq, x, x, ALU.mult).then_inc(o_v.sem, 1)
                v.wait_ge(o_v.sem, o_v.at(f"s{t}", n))
                nc.vector.tensor_reduce(head_sq[:, bass.ds(t * M_HEADS + 2 * n, 2)], sq.rearrange("p (h n) -> p h n", n=M_V),
                                        AX.X, ALU.add).then_inc(o_v.sem, 1)

        def dve_mz(v, n):
            for t in range(TT):
                x = v3[:, t, bass.ds(n * W, W)]
                by_head = x.rearrange("p (h n) -> p h n", n=M_V)
                rs = head_rstd[:, bass.ds(t * M_HEADS + 2 * n, 2)].rearrange("p (h o) -> p h o", o=1)
                nc.vector.tensor_tensor(by_head, by_head, rs.to_broadcast([P, 2, M_V]), ALU.mult).then_inc(z_v.sem, 1)
                v.wait_ge(z_v.sem, z_v.at(f"n{t}", n))
                nc.vector.tensor_tensor(x, x, page(MZ_GAIN, 4)[:, bass.ds(n * W, W)], ALU.mult).then_inc(z_v.sem, 1)
                v.wait_ge(z_v.sem, z_v.at(f"w{t}", n))
                v.wait_ge(bank_free[t], G_MZ + n + 2)
                nc.vector.tensor_tensor(x, x, page(MO_TMP + t), ALU.mult).then_inc(z_v.sem, 1)

        cv_v = steps("cv_v", [f"{x}{m}" for x in ("w1", "w0", "w2") for m in range(4)] + [f"z{m}" for m in range(4)])

        def act_conv_u(act, j, g):
            act.wait_ge(cv_v.sem, cv_v.at("z3", j, back=1))
            act_evac(act, g, lambda m: page(C_U + m))

        def dve_conv_c(v, j, g):
            for m in range(4):
                v.wait_ge(bank_free[m], g + 1)
                full(v, g, m)
                nc.vector.tensor_tensor(page(C_U + m), bank[m][:], page(C_U + m), ALU.mult).then_inc(bank_free[m], 1)
            cw = lambda w, m: col("conv3_w", LRU_TILES * w + 4 * j + m)
            y = lambda m: page(P_YB + 4 * j + m)
            for m in range(4):
                v.wait_ge(bank_free[m], g + 2)
                nc.vector.tensor_scalar(y(m), page(C_U + m), cw(1, m), None, ALU.mult).then_inc(cv_v.sem, 1)
            for m in range(4):
                v.wait_ge(cv_v.sem, cv_v.at(f"w1{m}", j))
                nc.vector.scalar_tensor_tensor(y(m)[:, 1:S], page(C_U + m)[:, 0:S - 1], cw(0, m), y(m)[:, 1:S],
                                               ALU.mult, ALU.add).then_inc(cv_v.sem, 1)
            for m in range(4):
                v.wait_ge(cv_v.sem, cv_v.at(f"w0{m}", j))
                nc.vector.scalar_tensor_tensor(y(m)[:, 0:S - 1], page(C_U + m)[:, 1:S], cw(2, m), y(m)[:, 0:S - 1],
                                               ALU.mult, ALU.add).then_inc(cv_v.sem, 1)

        def dve_conv_b(v, j, g):
            for m in range(4):
                v.wait_ge(cv_v.sem, cv_v.at(f"w2{m}", j))
                full(v, g, m)
                nc.vector.tensor_tensor(page(P_YB + 4 * j + m), bank[m][:], page(P_YB + 4 * j + m),
                                        ALU.mult).then_inc(bank_free[m], 1)

        def act_conv_z(act, j, g):
            act.wait_ge(cv_v.sem, cv_v.at("w23", j))
            act_evac(act, g, lambda m: page(C_U + m), ACT.Silu)

        def dve_conv_z(v, j, g):
            for m in range(4):
                v.wait_ge(bank_free[m], g + 2)
                nc.vector.tensor_tensor(page(P_YB + 4 * j + m), page(P_YB + 4 * j + m), page(C_U + m),
                                        ALU.mult).then_inc(cv_v.sem, 1)

        mask_in = sem("mask_in")

        def half_cols(p, h):
            return arena[:, p:p + 4, bass.ds(h * HD, HD)]

        sv = arena[:, P_SV:P_SV + 16, :].rearrange("p a n -> p (a n)").rearrange("p (t n) -> p t n", t=TT)
        ln_in = sem("ln_in")
        ln_a = steps("ln_a", "s0 s1 s2 s3 root")
        ln_v = steps("ln_v", "sum mean rec c0 c1 c2 c3 a0 a1 a2 a3")
        sg_p = sem("sg_p")
        sg_v = sem("sg_v")
        u_v = steps("u_v", "m0 m1 m2 m3")

        def act_sgu_values(act):
            act.wait_ge(h_ready, 7 * KT)
            act.wait_ge(new_out, 144)
            act.dma_start(page(S_G, 4), row("ln_g", D)).then_inc(ln_in, 16)
            act.dma_start(page(S_B, 4), row("ln_b", D)).then_inc(ln_in, 16)
            act.dma_start(page(S_BS, 2), row("b_s", 2 * W)).then_inc(ln_in, 16)
            act.dma_start(page(S_WS, 2), ws_d).then_inc(ln_in, 16)
            with act.Fori(0, 4) as n:
                for t in range(TT):
                    full(act, G_SV + n, t)
                    nc.scalar.activation(sv[:, t, bass.ds(n * W, W)], bank[t][:], ACT.Gelu_apprx_tanh,
                                         accum_out=small[:, bass.ds(4 * t + n, 1)]).then_inc(bank_free[t], 1)
            act.wait_ge(ln_v.sem, ln_v.at("mean"))
            for t in range(TT):
                act.wait_ge(ln_a.sem, ln_a.n + t)
                nc.scalar.activation(page(S_TMP, 4), sv[:, t, :], ACT.Square, bias=mean[:, t:t + 1],
                                     accum_out=token_sum[:, t:t + 1]).then_inc(ln_a.sem, 1)
            act.wait_ge(ln_a.sem, ln_a.at("s3"))
            nc.scalar.activation(root, token_sum, ACT.Sqrt, bias=eps[:], scale=1.0 / D).then_inc(ln_a.sem, 1)
            act.wait_ge(ln_a.sem, ln_a.at("root"))

        def dve_sgu_values(v):
            group_written(v, G_SV + 3)
            nc.vector.tensor_reduce(mean, square_sum, AX.X, ALU.add).then_inc(ln_v.sem, 1)
            v.wait_ge(ln_v.sem, ln_v.at("sum"))
            nc.vector.tensor_scalar(mean, mean, -1.0 / D, None, ALU.mult).then_inc(ln_v.sem, 1)
            v.wait_ge(ln_a.sem, ln_a.at("root"))
            nc.vector.reciprocal(rstd, root).then_inc(ln_v.sem, 1)
            v.wait_ge(ln_v.sem, ln_v.at("rec"))
            v.wait_ge(ln_in, 64)
            for t in range(TT):
                nc.vector.scalar_tensor_tensor(sv[:, t, :], sv[:, t, :], mean[:, t:t + 1], page(S_G, 4), ALU.add,
                                               ALU.mult).then_inc(ln_v.sem, 1)
            for t in range(TT):
                v.wait_ge(ln_v.sem, ln_v.at(f"c{t}"))
                nc.vector.scalar_tensor_tensor(sv[:, t, :], sv[:, t, :], rstd[:, t:t + 1], page(S_B, 4), ALU.mult,
                                               ALU.add).then_inc(ln_v.sem, 1)

        def pe_sgu(pe, first, last):
            pe.wait_ge(ln_v.sem, ln_v.at("a3"))
            for f in range(first, last):
                if f >= 4:
                    pe.wait_ge(sg_v, f - 3)
                for n in range(TT):
                    mm = nc.tensor.matmul(bank[4 + f % 4][:, n * P:(n + 1) * P], sv[:, n, f * P:(f + 1) * P],
                                          page(S_WS, 2)[:, (f // 2) * P:(f // 2 + 1) * P], start=True, stop=True)
                mm.then_inc(sg_p, 1)

        def dve_sgu(v):
            for f in range(KT):
                v.wait_ge(sg_p, f + 1)
                bias = page(S_BS, 2)[:, (f // 2) * P:(f // 2 + 1) * P].rearrange("p (o n) -> p o n", o=1)
                nc.vector.tensor_tensor(page(P_MX + f).rearrange("p (t n) -> p t n", n=P),
                                        bank[4 + f % 4][:].rearrange("p (t n) -> p t n", n=P),
                                        bias.to_broadcast([P, TT, P]), ALU.add).then_inc(sg_v, 1)
            v.wait_ge(sg_v, KT)

        def act_sgu_gate(act, n, func):
            for m in range(4):
                act.wait_ge(u_v.sem, u_v.at(f"m{m}", n, back=1))
                full(act, G_SU + n, m)
                nc.scalar.activation(page(S_TMP + m), bank[m][:], func).then_inc(bank_free[m], 1)

        def dve_sgu_gate(v, n, tile):
            for m in range(4):
                v.wait_ge(bank_free[m], G_SU + n + 2)
                nc.vector.tensor_tensor(page(P_MX + tile + m), page(P_MX + tile + m), page(S_TMP + m),
                                        ALU.mult).then_inc(u_v.sem, 1)

        def mix3(f):
            return P_YA + f if f < HEADS else P_YB + f - HEADS

        def mix4(f):
            return P_MX + f

        ga_v = steps("ga_v", "m0 m1 m2 m3")

        def act_attn_gate(act, g0, task, n, tmp):
            for m in range(4):
                act.wait_ge(ga_v.sem, ga_v.at(f"m{m}", task + n, back=1))
                full(act, g0 + n, m)
                nc.scalar.activation(page(tmp + m), bank[m][:], ACT.Silu).then_inc(bank_free[m], 1)

        def dve_attn_gate(v, g0, task, n, tmp, ya):
            for m in range(4):
                v.wait_ge(bank_free[m], g0 + n + 2)
                nc.vector.tensor_tensor(page(ya + 4 * n + m), page(ya + 4 * n + m), page(tmp + m),
                                        ALU.mult).then_inc(ga_v.sem, 1)

        cols_in, ident_in = sem("cols_in"), sem("ident_in")
        x_loaded = [sem(f"x_loaded{t}") for t in range(TT)]
        first_square = sem("first_square")
        out_done = sem("out_done")

        def mix1(f):
            return P_GA + f if f < HEADS else P_XL + f - HEADS

        block = ctx.enter_context(nc.Block())

        @block.sync
        def _(sp):
            def weights(g, per=0, block=0):
                for c in range(NCH):
                    sp.wait_ge(w_ready, NCH * g + c + 1 + WREADY0 - RAW_SLOTS)
                    sp.dma_start(w_raw[:, c % RAW_SLOTS, :],
                                 wall[bass.ds(g, 1), :, c * CH * W:(c + 1) * CH * W]
                                 .rearrange("a p n -> p (a n)")).then_inc(raw_in[c % RAW_SLOTS], 16)
                    for i in range(c * per, (c + 1) * per):
                        b, mc = block + i // NCH, i % NCH
                        if mc < 2:
                            sp.wait_ge(mod_sum.sem, mod_sum.at(f"k{13 + 2 * mc}", b, back=1))
                        else:
                            sp.wait_ge(mod_sum.sem, mod_sum.at(f"k{2 * mc - 3}", b))
                        sp.dma_start(page(MOD_RING + 2 * (mc % 2), 2),
                                     mods[bass.ds(b, 1), :, mc * CH * W:(mc + 1) * CH * W]
                                     .rearrange("a p n -> p (a n)")).then_inc(mod_in[mc % 2], 16)

            groups = {0: 0, 1: G_OUT1 + 4, 2: G_OUT2 + 4, 3: G_OUT3 + 4, 4: GROUPS}[layers]
            for m in range(4):
                sp.sem_inc(bank_free[m], 1)
            at = 0
            for first, n, per, block in RIDES:
                if first >= groups:
                    break
                if at < first:
                    with sp.Fori(at, first) as g:
                        weights(g)
                with sp.Fori(0, n) as i:
                    weights(first + i, per, block + per * i)
                at = first + n
            if at < groups:
                with sp.Fori(at, groups) as g:
                    weights(g)

        @block.gpsimd
        def _(pool):
            pool.sem_inc(w_ready, WREADY0)
            pool.wait_ge(setup_v.sem, setup_v.at("zero"))
            groups = {0: 0, 1: G_OUT1 + 4, 2: G_OUT2 + 4, 3: G_OUT3 + 4, 4: GROUPS}[layers]
            with pool.Fori(0, groups) as g:
                for c in range(NCH):
                    raw, s = w_raw[:, c % RAW_SLOTS, :], c % SPLIT_SLOTS
                    pool.wait_ge(raw_in[c % RAW_SLOTS], 16 * (2 * g + c // RAW_SLOTS + 1))
                    if c == 1:
                        pool.wait_ge(bank_full, 4 * g + FULL0)
                    else:
                        pool.wait_ge(w_used, (NCH - 1) * g + WUSED0 + (c - 1 if c else 0))
                    nc.gpsimd.tensor_tensor(w_hi[:, s, :], raw, zero[:].to_broadcast([P, CH * W]),
                                            ALU.add).then_inc(w_hi_done, 1)
                    pool.wait_ge(w_hi_done, NCH * g + c + 1)
                    nc.gpsimd.tensor_tensor(w_lo[:, s, :], raw, w_hi[:, s, :].bitcast(F32),
                                            ALU.subtract).then_inc(w_ready, 1)

        @block.vector
        def _(v):
            for st in (mod_sum, norm_v, res_v, final_v, lru_v, att1.kv_v, att1.q_v, att1.s_v, att3.kv_v, att3.q_v,
                       att3.s_v, qk_v, setup_v, gate_v, m_v, o_v, z_v,
                       modc_v, modg_v, cv_v, ln_v, u_v, ga_v):
                v.sem_inc(st.sem, st.n)
            nc.vector.memset(zero[:], 0.0).then_inc(setup_v.sem, 1)
            nc.vector.memset(one[:], 1.0).then_inc(setup_v.sem, 1)
            nc.vector.memset(eps[:], EPS).then_inc(setup_v.sem, 1)
            nc.vector.memset(small[:], 0.0).then_inc(setup_v.sem, 1)
            nc.vector.memset(ones[:], 1.0).then_inc(setup_v.sem, 1)
            v.wait_ge(setup_a.sem, setup_a.at("ln"))
            low = page(ROWS)[:, 0:2 * LRU_TILES]
            nc.vector.tensor_scalar(low, col("lam", 0, 2 * LRU_TILES), 0.0, None, ALU.min).then_inc(setup_v.sem, 1)
            v.wait_ge(setup_v.sem, setup_v.at("min"))
            nc.vector.tensor_tensor(lru_decay[:], low, lru_decay[:], ALU.subtract).then_inc(setup_v.sem, 1)
            v.wait_ge(setup_v.sem, setup_v.at("sub"))
            nc.vector.tensor_scalar(lru_half[:], lru_decay[:], LRU_C / 2, None, ALU.mult).then_inc(setup_v.sem, 1)
            v.wait_ge(setup_v.sem, setup_v.at("half"))
            nc.vector.tensor_scalar(lru_decay[:], lru_decay[:], LRU_C, None, ALU.mult).then_inc(setup_v.sem, 1)
            v.wait_ge(setup_v.sem, setup_v.at("scale"))

            v.wait_ge(ident_in, 16)
            v.wait_ge(first_square, TT)
            dve_norm(v, 0)
            dve_turn(v, 0, TMP)
            for i in range(2):
                dve_mods(v, G_Q + 1, i)
            group_written(v, G_KV)
            dve_qk_stats(v)
            v.wait_ge(rope_in, 32)
            for kv in range(KV_HEADS):
                att1.dve_kv(v, kv, kv * (HEADS // KV_HEADS), head_cols(qkv, D // 2, kv),
                            head_cols(qkv, D // 2 + KV_HEADS * HD, kv), rs_of(HEADS + kv), gain_of(1))
                with v.Fori(0, 2) as i:
                    for n in range(2):
                        h = kv * (HEADS // KV_HEADS) + 2 * i + n
                        att1.dve_q(v, h, kv, head_cols(qkv, 0, h), rs_of(h), gain_of(0))
                        att1.dve_head(v, h, page(P_GA + h))
            with v.Fori(0, 2) as i:
                for n in range(4):
                    group_written(v, G_GL + 1)
                    dve_lru(v, 4 * i + n)
                dve_attn_gate(v, G_GA, 0, i, GA_TMP, P_GA)
            dve_split(v, 1, mix1)
            dve_residual(v, 0, G_OUT1, False)
            if layers == 1:
                return

            v.wait_ge(res_a.sem, res_a.at("q3", 3))
            dve_norm(v, 1)
            dve_turn(v, 2, TMP)
            with v.Fori(0, 3) as i:
                dve_mods(v, G_MQ + 1, i)
            dve_gates(v)
            with v.Fori(0, M_HEADS // 2) as i:
                for k in range(2):
                    group_written(v, G_MV + i)
                    v.wait_ge(tri_in, 16)
                    dve_mlstm(v, 2 * i + k)
            v.wait_ge(m_a.sem, m_a.at("back", M_HEADS - 1))
            dve_mo(v, 0)
            with v.Fori(0, 3) as n:
                dve_mods(v, G_MO + 1, n)
                dve_mo(v, n + 1)
            v.wait_ge(m_root, 1)
            nc.vector.reciprocal(head_rstd[:, 0:32], head_rstd[:, 0:32]).then_inc(m_rec, 1)
            v.wait_ge(m_rec, 1)
            v.wait_ge(gain_in, 16)
            with v.Fori(0, 4) as n:
                dve_mods(v, G_MZ, n)
                dve_mz(v, n)
            dve_turn(v, 3, TMP)
            dve_residual(v, 1, G_OUT2, False)
            v.wait_ge(res_a.sem, res_a.at("q3", 7))
            dve_norm(v, 2)
            dve_final(v, 0)
            if layers == 2:
                return

            v.wait_ge(final_a.sem, final_a.at("q3", 0))
            dve_norm(v, 3)
            dve_mod_cols(v, 0)
            dve_turn(v, 4, TMP)
            v.wait_ge(rope_in, 48)
            v.wait_ge(mask_in, 16)
            with v.Fori(0, 2) as j:
                g = G_ATT + 7 * j
                for i in range(4):
                    h = 4 * j + i
                    group_written(v, g + 2)
                    att3.dve_kv(v, h, h, half_cols(P_KH, i), half_cols(P_VH, i))
                    att3.dve_q(v, h, h, half_cols(P_QH, i))
                    att3.dve_head(v, h, page(P_YA + h))
                    if i:
                        (dve_conv_c, dve_conv_b, dve_conv_z)[i - 1](v, j, g + 3 + i)
            with v.Fori(0, 2) as n:
                dve_attn_gate(v, G_ZA, 2, n, C_U, P_YA)
            dve_split(v, 5, mix3)
            dve_residual(v, 2, G_OUT3, True)
            if layers == 3:
                return

            v.wait_ge(res_a.sem, res_a.at("q3", 11))
            dve_norm(v, 4)
            dve_mod_cols(v, 1)
            dve_turn(v, 6, TMP)
            dve_sgu_values(v)
            dve_sgu(v)
            for first in (0, 4):
                with v.Fori(0, 4) as n:
                    dve_sgu_gate(v, first + n, 4 * n)
            dve_split(v, 7, mix4)
            dve_residual(v, 3, G_OUT4, True)
            v.wait_ge(res_a.sem, res_a.at("q3", 15))
            dve_norm(v, 5)
            dve_final(v, 1)

        @block.scalar
        def _(act):
            for st in (setup_a, norm_a, res_a, final_a, lru_a, att1.kv_a, att1.a, att3.kv_a, att3.a, qk_a, gate_a, m_a, ln_a):
                act.sem_inc(st.sem, st.n)
            act.sem_inc(mod_out, 16)
            act.dma_start(cols[:], cols_d).then_inc(cols_in, 16)
            for t in range(TT):
                act.dma_start(xp[:, t, :], x_in[t * P:(t + 1) * P, :]).then_inc(x_loaded[t], 16)
            act.dma_start(ident[:], ident_d).then_inc(ident_in, 16)
            act.wait_ge(cols_in, 16)
            nc.scalar.activation(c_silu[:], col("c", 0, KT), ACT.Silu).then_inc(setup_a.sem, 1)
            nc.scalar.activation(lru_decay[:], col("lam", 0, 2 * LRU_TILES), ACT.Abs).then_inc(setup_a.sem, 1)
            act.wait_ge(setup_a.sem, setup_a.at("abs"))
            nc.scalar.activation(lru_decay[:], lru_decay[:], ACT.Exp, scale=-1.0).then_inc(setup_a.sem, 1)
            act.wait_ge(setup_a.sem, setup_a.at("exp"))
            act.wait_ge(setup_v.sem, setup_v.at("sums"))
            nc.scalar.activation(lru_decay[:], lru_decay[:], ACT.Ln, bias=one[:]).then_inc(setup_a.sem, 1)

            for t in range(TT):
                act.wait_ge(x_loaded[t], 16)
                if t:
                    act.wait_ge(first_square, t)
                nc.scalar.activation(page(JUNK, 4), xp[:, t, :], ACT.Square,
                                     accum_out=square_sum[:, t, 0:1]).then_inc(first_square, 1)
            act_norm(act, 0)
            act_turn(act, 0, TMP, lambda f: col("norm0", f), lambda f: col("zero", f))
            act.wait_ge(h_ready, KT)
            act_load_rope(act, 0, att1)
            act.dma_start(gains, rows_d[:, ROW["q_gain"]:ROW["q_gain"] + 2 * HD]).then_inc(rope_in, 16)
            for g in range(G_XL):
                if g:
                    act_mods(act, G_Q + 1, g - 1)
                act_evac(act, g, lambda m: qkv[:, m, bass.ds(g * W, W)])
            act.wait_ge(qk_v.sem, qk_v.at("r3"))
            nc.scalar.activation(head_rstd[:, 0:TT * QK], head_sq[:, 0:TT * QK], ACT.Sqrt, bias=eps[:],
                                 scale=1.0 / HD).then_inc(qk_a.sem, 1)
            for kv, dst, func in ((0, P_XL, ACT.Copy), (1, P_GL, ACT.Silu)):
                att1.act_kv(act, kv)
                with act.Fori(0, 2) as i:
                    for n in range(2):
                        att1.act_head(act, kv * (HEADS // KV_HEADS) + 2 * i + n)
                    act.wait_ge(att1.p.sem, att1.p.at("o", kv * (HEADS // KV_HEADS) + 2 * i + 1))
                    act_evac(act, G_XL + 2 * kv + i, lambda m: page(dst + 4 * i + m), func)
            with act.Fori(0, 2) as i:
                for n in range(4):
                    act_lru(act, 4 * i + n)
                act_attn_gate(act, G_GA, 0, i, GA_TMP)
            act.wait_ge(ga_v.sem, ga_v.at("m3", 1))
            act_split(act, mix1)
            act_residual(act, 0, G_OUT1, x_in, False, True)
            if layers == 1:
                act.dma_start(out.rearrange("(t p) n -> p t n", p=P), xp).then_inc(out_done, 16)
                act.wait_ge(out_done, 16)
                act.wait_ge(new_out, 64)
                act.wait_ge(mod_out, 16 * 9)
                return

            act_norm(act, 1)
            act_turn(act, 2, TMP, lambda f: col("norm1", f), lambda f: col("zero", f))
            act.wait_ge(new_out, 64)
            act.dma_start(page(GW), gate_w).then_inc(gate_in, 16)
            act.dma_start(gtok[:, 128:160], row("m_bias", 32)).then_inc(gate_in, 16)
            act.dma_start(page(TRI)[:, 0:2 * P], tri_d).then_inc(tri_in, 16)
            for n, dst, scale in ((0, P_MQ, 1.0), (2, P_MK, HD ** -0.5)):
                for i in range(2):
                    if n + i:
                        act_mods(act, G_MQ + 1, n + i - 1)
                    act_evac(act, G_MQ + n + i, lambda m: page(dst + 4 * i + m), scale=scale)
            act_gates(act)
            act_evac(act, G_MV, lambda m: v3[:, m, 0:W])
            with act.Fori(0, 3) as i:
                for k in range(2):
                    act_mlstm(act, 2 * i + k)
                act_evac(act, G_MV + 1 + i, lambda m: v3[:, m, bass.ds((i + 1) * W, W)])
            for h in range(M_HEADS - 2, M_HEADS):
                act_mlstm(act, h)
            act.wait_ge(m_a.sem, m_a.at("back", M_HEADS - 1))
            act_gate_evac(act, G_MO, o_v, "g", 0, ACT.Sigmoid)
            act.dma_start(page(MZ_GAIN, 4), row("m_gain", D)).then_inc(gain_in, 16)
            with act.Fori(0, 3) as n:
                act_mods(act, G_MO + 1, n)
                act_gate_evac(act, G_MO + 1 + n, o_v, "g", n + 1, ACT.Sigmoid)
            act.wait_ge(o_v.sem, o_v.at("r3", 3))
            nc.scalar.activation(head_rstd[:, 0:32], head_sq[:, 0:32], ACT.Sqrt, bias=eps[:],
                                 scale=1.0 / M_V).then_inc(m_root, 1)
            with act.Fori(0, 4) as n:
                act_mods(act, G_MZ, n)
                act_gate_evac(act, G_MZ + n, z_v, "z", n, ACT.Silu)
            act_turn(act, 3, TMP)
            act_residual(act, 1, G_OUT2, x_mid, False, False)
            act_norm(act, 2)
            act_final(act, 0)
            act.dma_start(x_mid.rearrange("(t p) n -> p t n", p=P), xp).then_inc(new_out, 16)
            if layers == 2:
                act.dma_start(out.rearrange("(t p) n -> p t n", p=P), xp).then_inc(out_done, 16)
                act.wait_ge(out_done, 16)
                act.wait_ge(new_out, 80)
                act.wait_ge(mod_out, 16 * (MODS + 1))
                return

            act_load_mod(act, 0)
            act_norm(act, 3)
            act.wait_ge(modc_v.sem, modc_v.at("gain", 0))
            act_turn(act, 4, TMP, lambda f: mod_scale[:, f:f + 1], lambda f: mod_shift[:, f:f + 1])
            act.wait_ge(new_out, 80)
            act.wait_ge(h_ready, 5 * KT)
            act_load_rope(act, 1, att3)
            act.dma_start(page(att3.pg["mask"], 4), mask_d).then_inc(mask_in, 16)
            with act.Fori(0, 2) as j:
                g = G_ATT + 7 * j
                act.wait_ge(att3.s_v.sem, att3.s_v.at("out", 4 * j, back=1))
                for n, p in enumerate((P_QH, P_KH, P_VH)):
                    act_evac(act, g + n, lambda m: page(p + m))
                for i in range(4):
                    att3.act_kv(act, 4 * j + i)
                    att3.act_head(act, 4 * j + i)
                    if i == 0:
                        act_conv_u(act, j, g + 3)
                    if i == 3:
                        act_conv_z(act, j, g + 6)
            act.wait_ge(cv_v.sem, cv_v.at("z3", 1))
            with act.Fori(0, 2) as n:
                act_attn_gate(act, G_ZA, 2, n, C_U)
            act.wait_ge(ga_v.sem, ga_v.at("m3", 3))
            act_split(act, mix3)
            act_residual(act, 2, G_OUT3, x_mid, True, True)
            if layers == 3:
                act.dma_start(out.rearrange("(t p) n -> p t n", p=P), xp).then_inc(out_done, 16)
                act.wait_ge(out_done, 16)
                act.wait_ge(new_out, 144)
                return

            act_load_mod(act, 1)
            act_norm(act, 4)
            act.wait_ge(modc_v.sem, modc_v.at("gain", 1))
            act_turn(act, 6, TMP, lambda f: mod_scale[:, f:f + 1], lambda f: mod_shift[:, f:f + 1])
            act_sgu_values(act)
            for first, func in ((0, ACT.Gelu_apprx_tanh), (4, ACT.Silu)):
                with act.Fori(0, 4) as n:
                    act_sgu_gate(act, first + n, func)
            act.wait_ge(u_v.sem, u_v.at("m3", 7))
            act_split(act, mix4)
            act_residual(act, 3, G_OUT4, x_mid, True, False)
            act_norm(act, 5)
            for t in range(TT):
                act.wait_ge(final_v.sem, final_v.at(f"r{t}", 1))
                act.dma_start(out[t * P:(t + 1) * P, :], xp[:, t, :]).then_inc(out_done, 16)
            act.wait_ge(out_done, 16 * TT)
            act.wait_ge(new_out, 144)

        @block.tensor
        def _(pe):
            for st in (lru_p, att1.kv_p, att1.p, att3.kv_p, att3.p, gate_p, m_p, modc_p, modg_p):
                pe.sem_inc(st.sem, st.n)
            pe.sem_inc(bank_full, FULL0)
            pe.sem_inc(w_used, WUSED0)

            pe.wait_ge(norm_v.sem, norm_v.at("d3"))
            x_tile = lambda f, t: xp[:, t, f * P:(f + 1) * P]
            pe_turned_group(pe, G_Q, True, 0, x_tile, diag)
            with pe.Fori(G_Q + 1, G_XL) as g:
                pe_group(pe, g, True, 0)
            for kv in range(KV_HEADS):
                att1.pe_kv(pe, kv, kv * (HEADS // KV_HEADS))
                with pe.Fori(0, 2) as i:
                    for n in range(2):
                        h, g = kv * (HEADS // KV_HEADS) + 2 * i + n, G_XL + 2 * kv + i
                        att1.pe_queries(pe, h)
                        pe_chunks(pe, g, 4 * n, 4 * n + 1, False, 0)
                        att1.pe_scores(pe, h, kv, (0, 1))
                        pe_chunks(pe, g, 4 * n + 1, 4 * n + 2, False, 0)
                        att1.pe_turn_probs(pe, h, (0, 1))
                        att1.pe_scores(pe, h, kv, (2, 3))
                        pe_chunks(pe, g, 4 * n + 2, 4 * n + 3, False, 0)
                        att1.pe_turn_probs(pe, h, (2, 3))
                        att1.pe_values(pe, h, kv)
                        pe_chunks(pe, g, 4 * n + 3, 4 * n + 4, False, 0)
            with pe.Fori(0, 2) as i:
                for n in range(4):
                    pe_chunks(pe, G_GA + i, 2 * n, 2 * n + 1, False, 0)
                    pe_lru(pe, 4 * i + n)
                    pe_chunks(pe, G_GA + i, 2 * n + 1, 2 * n + 2, False, 0)
            with pe.Fori(G_OUT1, G_OUT1 + 4) as g:
                pe_group(pe, g, True, KT)
            if layers == 1:
                return

            pe.wait_ge(norm_v.sem, norm_v.at("d3", 1))
            pe_turned_group(pe, G_MQ, False, 2, x_tile, diag)
            with pe.Fori(G_MQ + 1, G_MV) as g:
                pe_group(pe, g, False, 2 * KT)
            pe_gates(pe)
            pe_chunks(pe, G_MV, 0, 1, True, 2 * KT)
            pe_gate_rows(pe)
            pe_chunks(pe, G_MV, 1, 6, True, 2 * KT)
            pe_gate_cols(pe)
            pe_chunks(pe, G_MV, 6, NCH, True, 2 * KT)
            with pe.Fori(0, M_HEADS // 2) as i:
                pe_m_group(pe, G_MV + 1 + i, 2 * i)
            with pe.Fori(G_MO + 1, G_OUT2) as g:
                pe_group(pe, g, True, 2 * KT)
            pe.wait_ge(z_v.sem, z_v.at("z3", 3))
            pe_turned_group(pe, G_OUT2, True, 3, lambda f, t: v3[:, t, f * P:(f + 1) * P], None)
            with pe.Fori(G_OUT2 + 1, G_OUT2 + 4) as g:
                pe_group(pe, g, True, 3 * KT)
            if layers == 2:
                return

            pe_mod_cols(pe, 0)
            pe.wait_ge(norm_v.sem, norm_v.at("d3", 3))
            pe_turned_group(pe, G_ATT, True, 4, x_tile, diag)
            for j in range(2):
                g = G_ATT + 7 * j
                with pe.Fori(1 - j, 3) as n:
                    pe_group(pe, g + n, True, 4 * KT)
                with pe.Fori(0, 4) as i:
                    h = 4 * j + i
                    att3.pe_kv(pe, h, h)
                    att3.pe_queries(pe, h)
                    pe_chunks(pe, g + 3 + i, 0, 2, False, 4 * KT)
                    att3.pe_scores(pe, h, h, (0, 1))
                    pe_chunks(pe, g + 3 + i, 2, 3, False, 4 * KT)
                    att3.pe_turn_probs(pe, h, (0, 1))
                    att3.pe_scores(pe, h, h, (2, 3))
                    pe_chunks(pe, g + 3 + i, 3, 4, False, 4 * KT)
                    att3.pe_turn_probs(pe, h, (2, 3))
                    att3.pe_values(pe, h, h)
                    pe_chunks(pe, g + 3 + i, 4, NCH, False, 4 * KT)
            with pe.Fori(G_ZA, G_OUT3) as g:
                pe_group(pe, g, False, 4 * KT)
            pe_group(pe, G_OUT3, True, 5 * KT)
            pe_gate(pe, 2)
            with pe.Fori(G_OUT3 + 1, G_OUT3 + 4) as g:
                pe_group(pe, g, True, 5 * KT)
            if layers == 3:
                return

            pe_mod_cols(pe, 1)
            pe.wait_ge(norm_v.sem, norm_v.at("d3", 4))
            pe_turned_group(pe, G_SV, True, 6, x_tile, diag)
            with pe.Fori(G_SV + 1, G_SU) as g:
                pe_group(pe, g, True, 6 * KT)
            pe_chunks(pe, G_SU, 0, 6, False, 6 * KT)
            for n in range(2):
                pe_sgu(pe, 8 * n, 8 * n + 8)
                pe_chunks(pe, G_SU, 6 + n, 7 + n, False, 6 * KT)
            with pe.Fori(G_SU + 1, G_OUT4) as g:
                pe_group(pe, g, False, 6 * KT)
            pe_group(pe, G_OUT4, True, 7 * KT)
            pe_gate(pe, 3)
            with pe.Fori(G_OUT4 + 1, GROUPS) as g:
                pe_group(pe, g, True, 7 * KT)


def _rope_table(angle_lo, angle_hi, part):
    both = []
    for fn, sign in ((np.cos, 1.0), (np.sin, -1.0)):
        pieces = []
        for angle in ((angle_lo, angle_hi) if angle_hi is not None else (angle_lo,)):
            pieces += [np.float32(sign) * fn(angle), fn(angle)]
        both.append(np.concatenate(pieces, axis=1).astype(np.float32))
    return np.stack(both).reshape(2, TT, P, HD).transpose(2, 0, 1, 3)


def kernel(**inputs):
    import concourse.bacc as _bacc
    from concourse.bass_utils import run_bass_kernel_spmd as _run

    LAYERS = 4
    a = {k: np.asarray(v) for k, v in inputs.items()}

    def groups(w, *parts):
        w = np.concatenate([w[:, b:e] for b, e in parts], axis=1) if parts else w
        return w.reshape(KT, P, -1, W).transpose(2, 1, 0, 3).reshape(-1, P, KT * W)

    w1, w3, w5, w7 = a["even_w_in"][0], a["odd_w_in"][0], a["ab_w_in_2"][0], a["sg_w_in_2"][0]
    h = LRU_W
    half = lambda b, j: (b * h + j * W, b * h + (j + 1) * W)
    ab_groups = [half(b, j) for j in range(2) for b in (0, 1, 2, 4, 6, 5, 7)] + [half(3, 0), half(3, 1)]
    kv = 2 * KV_HEADS * HD
    wall = np.concatenate([
        groups(w1, (0, h + kv), (2 * h + kv, 4 * h + kv), (h + kv, 2 * h + kv)),
        groups(a["even_w_out"][0]),
        groups(w3, (0, 2 * h + 3 * D)), groups(a["odd_w_out"][0]),
        groups(w5, *ab_groups), groups(a["ab_w_out_2"][0]),
        groups(w7, (D, 2 * D), (0, D), (2 * D, 3 * D)), groups(a["sg_w_out_2"][0])])
    mods = np.concatenate([groups(a["ab_w_mod_2"][0]), groups(a["sg_w_mod_2"][0])])
    b2, b3 = a["ab_b_mod_2"][0], a["sg_b_mod_2"][0]
    columns = {"norm0": a["norm_gain"][0], "norm1": a["norm_gain"][1], "conv_w": a["conv_w"], "conv_b": a["conv_b"],
               "ba": a["lru_ba"], "bx": a["lru_bx"], "lam": a["lru_lambda"], "c": a["c_2"],
               "norm2": a["ab_norm_g_2"], "shift_b2": b2[0:D], "scale_b2": b2[D:2 * D], "conv3_w": a["ab_conv_w_2"],
               "norm3": a["sg_norm_g_2"], "shift_b3": b3[0:D], "scale_b3": b3[D:2 * D],
               "zero": np.zeros(D, np.float32)}
    assert list(columns) == list(COLS)
    cols = np.concatenate([v.reshape(-1, P) for v in columns.values()]).T
    long_rows = {"final0": a["final_gain"], "final1": a["final_norm_g_2"], "gate_b2": b2[2 * D:], "gate_b3": b3[2 * D:],
                 "m_gain": a["odd_norm_gain"], "ln_g": a["sg_ln_g_2"], "ln_b": a["sg_ln_b_2"], "b_s": a["sg_b_s_2"],
                 "q_gain": a["q_norm_gain"], "k_gain": a["k_norm_gain"], "m_bias": a["odd_gate_bias"]}
    assert list(long_rows) == list(ROW)
    rows = np.broadcast_to(np.concatenate([v.reshape(-1) for v in long_rows.values()]), (P, NROWS))
    lru_w = np.stack([a["lru_wa"][0, 0], a["lru_wx"][0, 0], a["lru_wa"][0, 1], a["lru_wx"][0, 1]])
    lru_w = lru_w.transpose(1, 2, 0, 3).reshape(LRU_TILES, P, 4 * P)
    gate_w = w3[:, 2 * h + 3 * D:].reshape(KT, P, 32).transpose(1, 0, 2).reshape(P, KT * 32)

    f32 = np.float32
    inv = f32(10000.0) ** (-np.arange(0, HD // 2, 2, dtype=f32) / f32(HD // 2))
    tok = np.arange(S)
    rope1 = _rope_table((tok // 64).astype(f32)[:, None] * inv, (tok % 64).astype(f32)[:, None] * inv, HD // 4)
    inv3 = f32(10000.0) ** (-np.arange(HD // 2, dtype=f32) / f32(HD // 2))
    rope3 = _rope_table(tok.astype(f32)[:, None] * inv3, None, HD // 2)
    rope = np.stack([rope1, rope3]).reshape(2, P, 2 * TT * HD)
    gap = np.abs(tok[:, None] - tok[None, :])
    count = (gap <= 64).astype(int) + ((gap % 4 == 0) & (gap <= 256)) + (gap % 16 == 0)
    mask = np.where(count > 0, np.log(np.maximum(count, 1)) / SCALE, -1e30).astype(f32)
    mask = mask.reshape(TT, P, S).transpose(1, 0, 2).reshape(P, TT * S)
    i = np.arange(P)
    tri = np.stack([i[:, None] <= i[None, :], i[:, None] >= i[None, :]], axis=1).astype(f32).reshape(P, 2 * P)
    arrays = {"x": a["x"][0], "wall": wall, "mods": mods, "cols": cols, "rows": rows, "lru_w": lru_w,
              "gate_w": gate_w, "ident": np.eye(P, dtype=f32), "rope": rope, "mask": mask, "tri": tri,
              "ws": a["sg_w_s_2"][0].transpose(2, 0, 1).reshape(P, 8 * P)}
    arrays = {k: np.ascontiguousarray(v) for k, v in arrays.items()}

    nc = _bacc.Bacc("TRN2", target_bir_lowering=False, num_devices=1)
    args = [nc.dram_tensor(f"in_{k}", v.shape, F32, kind="ExternalInput").ap() for k, v in arrays.items()]
    x_mid = nc.dram_tensor("x_mid", (S, D), F32, kind="Internal").ap()
    mod_mid = nc.dram_tensor("mod_mid", (MODS, P, W), F32, kind="Internal").ap()
    out = nc.dram_tensor("out_0", (S, D), F32, kind="ExternalOutput").ap()
    build_program(nc, *args, x_mid, mod_mid, out, layers=LAYERS)
    r = _run(nc, [{f"in_{k}": v for k, v in arrays.items()}], core_ids=[0])
    return r.results[0]["out_0"].reshape(1, S, D)
```

```python
from contextlib import ExitStack

import numpy as np
import concourse.bass as bass
from concourse import mybir

F32 = mybir.dt.float32
F32R = mybir.dt.float32r
ALU = mybir.AluOpType
ACT = mybir.ActivationFunctionType
AX = mybir.AxisListType

P = 128
D = 2048
S = 512
KT = D // P
TT = S // P
W = 512
CH = 2
NCH = KT // CH
RAW_SLOTS = 4
SPLIT_SLOTS = 2
EPS = 1e-6
HD = 128
HEADS = 8
KV_HEADS = 2
LRU_W = D // 2
LRU_TILES = LRU_W // P
LRU_C = 8.0
M_HEADS = 8
M_V = D // M_HEADS
SCALE = HD ** -0.5
MOD_BLOCKS = 3 * D // W

G_KV, G_Q, G_XL, G_GL, G_GA, G_OUT1 = 0, 1, 3, 5, 7, 9
G_MQ, G_MK, G_MV, G_MO, G_MZ, G_OUT2 = 13, 15, 17, 21, 25, 29
G_ATT, G_ZA, G_OUT3 = 33, 47, 49
G_SV, G_SU, G_SZ, G_OUT4 = 53, 57, 61, 65
GROUPS = 69
MODS = 2 * MOD_BLOCKS
RIDES = ((G_Q, 2, 1, 0), (G_OUT1, 4, 1, 2), (G_MQ + 1, 3, 2, 6), (G_MO + 1, 3, 1, 12), (G_MZ, 4, 1, 15),
         (G_OUT2 + 1, 3, 1, 19), (G_ZA, 2, 1, 22))

PAGES = 54
MOD_RING, MOD_ACC = 49, 53
XP, XR, GATE, MACC, DIAG, TMP, JUNK = 0, 16, 24, 28, 32, 33, 37
ROWS = 41
P_XL, P_GL, P_GA, P_QKV = 0, 8, 16, 24
LRU_SET, GA_TMP = (24, 34), 44
LW, XC, GR0, GI0, GR1, GI1, TH, EA = 0, 1, 2, 3, 4, 5, 6, 8
P_MQ, P_MK, P_MV, KCUR, NM, EE, PP, MHEAD, TRI, MROW = 0, 8, 16, 32, 33, 35, 37, 42, 44, 47
GATES, GW = 43, 24
MO_TMP, MO_SQ, MZ_GAIN = 32, 36, 40
P_YB, C_U, P_QH, P_KH, P_VH, P_YA = 0, 8, 12, 16, 20, 24
P_SV, P_MX, S_TMP, S_G, S_B, S_BS, S_WS = 0, 16, 32, 36, 40, 44, 46


COLS = {}


def _columns():
    at = 0
    for name, n in (("norm0", KT), ("norm1", KT), ("conv_w", 4 * LRU_TILES), ("conv_b", LRU_TILES),
                    ("ba", 2 * LRU_TILES), ("bx", 2 * LRU_TILES), ("lam", 2 * LRU_TILES), ("c", KT),
                    ("norm2", KT), ("shift_b2", KT), ("scale_b2", KT), ("conv3_w", 3 * LRU_TILES),
                    ("norm3", KT), ("m_bias", 1), ("shift_b3", KT), ("scale_b3", KT), ("zero", KT)):
        COLS[name] = at
        at += n
    return at


NCOLS = _columns()
ROW = {}


def _rows():
    at = 0
    for name, n in (("final0", D), ("final1", D), ("gate_b2", D), ("gate_b3", D), ("m_gain", D),
                    ("ln_g", D), ("ln_b", D), ("b_s", 8 * P), ("q_gain", HD), ("k_gain", HD)):
        ROW[name] = at
        at += n
    return at


NROWS = _rows()


class Steps:

    def __init__(self, sem, names, before=1):
        self.sem, self.names, self.before = sem, names.split() if isinstance(names, str) else names, before
        self.n = len(self.names)
        self.start = self.n * before

    def at(self, name, task=0, back=0):
        return self.n * (task + self.before - back) + self.names.index(name) + 1


def build_program(nc, x_in, wall, mods, cols_d, rows_d, lru_w, gate_w, ident_d, rope_d, mask_d, tri_d,
                  ws_d, x_mid, mod_mid, out):
    with ExitStack() as ctx:
        def sb(name, shape, dt=F32):
            return ctx.enter_context(nc.sbuf_tensor(name, shape, dt))

        def sem(name):
            return ctx.enter_context(nc.semaphore(name))

        def steps(name, names, before=1):
            return Steps(sem(name), names, before)

        h_hi = sb("h_hi", [P, KT, S], F32R)
        h_lo = sb("h_lo", [P, KT, S], F32R)
        w_raw = sb("w_raw", [P, RAW_SLOTS, CH * W])
        w_hi = sb("w_hi", [P, SPLIT_SLOTS, CH * W], F32R)
        w_lo = sb("w_lo", [P, SPLIT_SLOTS, CH * W], F32R)
        arena = sb("arena", [P, PAGES, W])
        cols = sb("cols", [P, NCOLS])
        ident = sb("ident", [P, P])
        zero = sb("zero", [P, 1])
        one = sb("one", [P, 1])
        eps = sb("eps", [P, 1])
        c_silu = sb("c_silu", [P, KT])
        lru_decay = sb("lru_decay", [P, 2 * LRU_TILES])
        lru_half = sb("lru_half", [P, 2 * LRU_TILES])
        small = sb("small", [P, 160])
        ones = sb("ones", [P, P])
        bank = [ctx.enter_context(nc.psum_tensor(f"bank{i}", [P, W], F32)) for i in range(8)]

        def page(i, n=1):
            if isinstance(i, int):
                return arena[:, i:i + n, :].rearrange("p a n -> p (a n)")
            return arena[:, bass.ds(i, n), :].rearrange("p a n -> p (a n)")

        def col(name, i=0, n=1):
            return cols[:, bass.ds(COLS[name] + i, n)]

        def row(name, n):
            return rows_d[:, ROW[name]:ROW[name] + n]

        square_sum = small[:, 0:16].rearrange("p (t n) -> p t n", n=4)
        token_sum = small[:, 16:20]
        root = small[:, 20:24]
        rstd = small[:, 24:28]
        head_sq = small[:, 28:68]
        head_rstd = small[:, 68:108]
        row_max = small[:, 108:110]
        row_bias = small[:, 110:112]
        row_sum = small[:, 112:114]
        row_rec = small[:, 114:116]
        den = small[:, 116:124]
        mod_scale = small[:, 124:140]
        mod_shift = small[:, 140:156]
        mean = small[:, 156:160]

        raw_in = [sem(f"raw_in{s}") for s in range(RAW_SLOTS)]
        w_hi_done = sem("w_hi_done")
        w_ready = sem("w_ready")
        w_used = sem("w_used")
        bank_full = sem("bank_full")
        bank_free = [sem(f"bank_free{m}") for m in range(4)]
        h_ready = sem("h_ready")
        h_hi_done = sem("h_hi_done")
        mod_in = [sem(f"mod_in{s}") for s in range(2)]
        mod_sum = steps("mod_sum", [f"k{k}" for k in range(KT)])
        mod_out = sem("mod_out")
        setup_a = steps("setup_a", "silu abs exp ln")
        setup_v = steps("setup_v", "zero one eps sums ones min sub half scale")

        slot_shift = {"pe": 0}
        FULL0, WREADY0, WUSED0 = 4, NCH, NCH - 1

        def group_written(eng, g):
            for m in range(4):
                eng.wait_ge(bank_free[m], g + 2)

        def pe_chunks(pe, g, first, last, tokens_out, h_tiles):
            for c in range(first, last):
                s = (c + slot_shift["pe"]) % SPLIT_SLOTS
                pe.wait_ge(h_ready, h_tiles + CH * (c + 1))
                pe.wait_ge(w_ready, NCH * g + c + 1 + WREADY0)
                for m in range(4):
                    if c == 0:
                        pe.wait_ge(bank_free[m], g + 1)
                    for kk in range(CH):
                        k = CH * c + kk
                        if tokens_out:
                            hs = slice(m * P, (m + 1) * P)
                            ws = slice(kk * W, (kk + 1) * W)
                            pairs = ((h_hi[:, k, hs], w_hi[:, s, ws]), (h_hi[:, k, hs], w_lo[:, s, ws]),
                                     (h_lo[:, k, hs], w_hi[:, s, ws]))
                        else:
                            ws = slice(kk * W + m * P, kk * W + (m + 1) * P)
                            pairs = ((w_hi[:, s, ws], h_hi[:, k, :]), (w_hi[:, s, ws], h_lo[:, k, :]),
                                     (w_lo[:, s, ws], h_hi[:, k, :]))
                        for n, (a, b) in enumerate(pairs):
                            mm = nc.tensor.matmul(bank[m][:], a, b, start=(k == 0 and n == 0),
                                                  stop=(k == KT - 1 and n == 2))
                    if c == NCH - 1:
                        mm.then_inc(bank_full, 1)
                if c < NCH - 1:
                    mm.then_inc(w_used, 1)

        def pe_group(pe, g, tokens_out, h_tiles):
            pe_chunks(pe, g, 0, NCH, tokens_out, h_tiles)

        def full(eng, g, m):
            eng.wait_ge(bank_full, 4 * g + m + 1 + FULL0)

        def act_evac(act, g, dst, func=ACT.Copy, scale=1.0):
            for m in range(4):
                full(act, g, m)
                nc.scalar.activation(dst(m), bank[m][:], func, scale=scale).then_inc(bank_free[m], 1)

        def dve_mod(v, n):
            v.wait_ge(mod_out, 16 * (n + 1))
            for c in range(NCH):
                v.wait_ge(mod_in[c % 2], 16 * (4 * n + c // 2 + 1))
                for kk in range(CH):
                    k = CH * c + kk
                    slab = page(MOD_RING + 2 * (c % 2) + kk)
                    if k == 0:
                        nc.vector.tensor_scalar(page(MOD_ACC), slab, c_silu[:, 0:1], None,
                                                ALU.mult).then_inc(mod_sum.sem, 1)
                    else:
                        v.wait_ge(mod_sum.sem, mod_sum.at(f"k{k - 1}", n))
                        nc.vector.scalar_tensor_tensor(page(MOD_ACC), slab, c_silu[:, k:k + 1], page(MOD_ACC),
                                                       ALU.mult, ALU.add).then_inc(mod_sum.sem, 1)

        def ride(g0):
            return next(r for r in RIDES if r[0] == g0)

        def dve_mods(v, g0, i=0):
            _, _, per, block0 = ride(g0)
            for b in range(per):
                dve_mod(v, block0 + per * i + b)

        def act_mods(act, g0, i=0):
            _, _, per, block0 = ride(g0)
            for b in range(per):
                act_mod(act, block0 + per * i + b)

        def act_mod(act, n):
            act.wait_ge(mod_sum.sem, mod_sum.at(f"k{KT - 1}", n))
            act.dma_start(mod_mid[bass.ds(n, 1)].rearrange("a p n -> p (a n)"), page(MOD_ACC)).then_inc(mod_out, 16)

        tile_val = sem("tile_val")
        tile_turned = sem("tile_turned")
        turns = {0: 0, 2: 1, 3: 2, 4: 3, 6: 4}

        def pe_turn(pe, r, lhs, diag, first, last):
            q = turns[r]
            for f in range(first, last):
                if f >= 4:
                    pe.wait_ge(tile_val, KT * q + f - 3)
                for t in range(TT):
                    dst = bank[4 + f % 4][:, t * P:(t + 1) * P]
                    if diag is None:
                        mm = nc.tensor.transpose(dst, lhs(f, t), ident[:])
                    else:
                        mm = nc.tensor.matmul(dst, lhs(f, t), diag[:, t, :], start=True, stop=True)
                mm.then_inc(tile_turned, 1)

        def pe_turned_group(pe, g, tokens_out, r, lhs, diag):
            pe_turn(pe, r, lhs, diag, 0, 4)
            for c in range(NCH):
                pe_chunks(pe, g, c, c + 1, tokens_out, KT * r)
                pe_turn(pe, r, lhs, diag, min(4 + 2 * c, KT), min(6 + 2 * c, KT))

        def act_turn(act, r, tmp, gain=None, shift=None):
            q = turns[r]
            for f in range(KT):
                act.wait_ge(tile_turned, KT * q + f + 1)
                if f >= 4:
                    act.wait_ge(h_ready, KT * r + f - 3)
                if gain is None:
                    nc.scalar.copy(page(tmp + f % 4), bank[4 + f % 4][:]).then_inc(tile_val, 1)
                else:
                    nc.scalar.activation(page(tmp + f % 4), bank[4 + f % 4][:], ACT.Identity,
                                         bias=shift(f), scale=gain(f)).then_inc(tile_val, 1)

        def dve_turn(v, r, tmp):
            q = turns[r]
            for f in range(KT):
                v.wait_ge(tile_val, KT * q + f + 1)
                nc.vector.tensor_copy(h_hi[:, f, :], page(tmp + f % 4)).then_inc(h_hi_done, 1)
                v.wait_ge(h_hi_done, KT * r + f + 1)
                nc.vector.tensor_tensor(h_lo[:, f, :], page(tmp + f % 4), h_hi[:, f, :].bitcast(F32),
                                        ALU.subtract).then_inc(h_ready, 1)

        def act_split(act, src, first, last, ready):
            for f in range(first, last):
                st, name, task = ready(f)
                act.wait_ge(st.sem, st.at(name, task))
                nc.scalar.copy(h_hi[:, f, :], page(src(f))).then_inc(h_hi_done, 1)

        def dve_split(v, r, src, first, last):
            for f in range(first, last):
                v.wait_ge(h_hi_done, KT * r + f + 1)
                nc.vector.tensor_tensor(h_lo[:, f, :], page(src(f)), h_hi[:, f, :].bitcast(F32),
                                        ALU.subtract).then_inc(h_ready, 1)

        diag = page(DIAG).rearrange("p (t n) -> p t n", n=P)
        xp = arena[:, XP:XP + 16, :].rearrange("p a n -> p (a n)").rearrange("p (t n) -> p t n", n=D)
        norm_a = steps("norm_a", "root")
        norm_v = steps("norm_v", "total rstd d0 d1 d2 d3")

        def act_norm(act, q):
            act.wait_ge(norm_v.sem, norm_v.at("total", q))
            nc.scalar.activation(root, token_sum, ACT.Sqrt, bias=eps[:], scale=1.0 / D).then_inc(norm_a.sem, 1)

        def dve_norm(v, q):
            nc.vector.tensor_reduce(token_sum, square_sum, AX.X, ALU.add).then_inc(norm_v.sem, 1)
            v.wait_ge(norm_a.sem, norm_a.at("root", q))
            nc.vector.reciprocal(rstd, root).then_inc(norm_v.sem, 1)
            v.wait_ge(norm_v.sem, norm_v.at("rstd", q))
            for t in range(TT):
                nc.vector.tensor_scalar(diag[:, t, :], ident[:], rstd[:, t:t + 1], None,
                                        ALU.mult).then_inc(norm_v.sem, 1)

        mod_loaded = sem("mod_loaded")
        modc_p = steps("modc_p", "sum")
        modc_v = steps("modc_v", "shift scale one gain")
        gate_loaded = sem("gate_loaded")
        modg_p = steps("modg_p", "g0 g1 g2 g3")
        modg_v = steps("modg_v", "g0 g1 g2 g3")
        MODC = {0: GATE, 1: ROWS}

        def act_load_mod(act, q):
            act.wait_ge(mod_out, 16 * (MOD_BLOCKS * (q + 1) + 1))
            act.dma_start(arena[:, MODC[q]:MODC[q] + 8, :],
                          mod_mid[q * MOD_BLOCKS:q * MOD_BLOCKS + 8].rearrange("b p n -> p b n")).then_inc(mod_loaded, 16)

        def pe_mod_cols(pe, q):
            pe.wait_ge(mod_loaded, 16 * (q + 1))
            for b in range(8):
                for j in range(W // P):
                    mm = nc.tensor.matmul(bank[4][:, 4 * b + j:4 * b + j + 1], page(MODC[q] + b)[:, j * P:(j + 1) * P],
                                          one[:], start=True, stop=True)
            mm.then_inc(modc_p.sem, 1)
            pe.wait_ge(modc_v.sem, modc_v.at("scale", q))

        def dve_mod_cols(v, q):
            v.wait_ge(modc_p.sem, modc_p.at("sum", q))
            nc.vector.tensor_tensor(mod_shift, bank[4][:, 0:KT], col(f"shift_b{q + 2}", 0, KT),
                                    ALU.add).then_inc(modc_v.sem, 1)
            nc.vector.tensor_tensor(mod_scale, bank[4][:, KT:2 * KT], col(f"scale_b{q + 2}", 0, KT),
                                    ALU.add).then_inc(modc_v.sem, 1)
            v.wait_ge(modc_v.sem, modc_v.at("scale", q))
            nc.vector.tensor_scalar(mod_scale, mod_scale, 1.0, None, ALU.add).then_inc(modc_v.sem, 1)
            v.wait_ge(modc_v.sem, modc_v.at("one", q))
            nc.vector.tensor_tensor(mod_scale, mod_scale, col(f"norm{q + 2}", 0, KT), ALU.mult).then_inc(modc_v.sem, 1)

        def act_load_gate(act, lay):
            q = lay - 2
            act.dma_start(arena[:, MACC:MACC + 4, :],
                          mod_mid[q * MOD_BLOCKS + 8:(q + 1) * MOD_BLOCKS].rearrange("b p n -> p b n")).then_inc(gate_loaded, 16)
            act.dma_start(page(GATE, 4), row(f"gate_b{lay}", D)).then_inc(gate_loaded, 16)

        def pe_gate(pe, lay):
            pe.wait_ge(gate_loaded, 32 * (lay - 1))
            for n in range(4):
                nc.tensor.matmul(bank[4 + n][:], ones[:], page(MACC + n), start=True, stop=True).then_inc(modg_p.sem, 1)

        def dve_gate(v, lay):
            for n in range(4):
                v.wait_ge(modg_p.sem, modg_p.at(f"g{n}", lay - 2))
                nc.vector.tensor_tensor(page(GATE + n), bank[4 + n][:], page(GATE + n), ALU.add).then_inc(modg_v.sem, 1)
            v.wait_ge(modg_v.sem, modg_v.at("g3", lay - 2))

        old_in = sem("old_in")
        res_v = steps("res_v", "s0 s1 s2 s3")
        res_a = steps("res_a", "q0 q1 q2 q3")
        new_out = sem("new_out")
        res_task = {0: 0, 1: 0, 2: 0, 3: 4}

        def cols_of(dram, n):
            return dram.rearrange("(t p) n -> p t n", p=P)[:, :, n * W:(n + 1) * W]

        def act_residual(act, lay, g0, src, gated, store):
            def summed(n, t):
                if gated:
                    act.wait_ge(res_v.sem, res_v.at(f"s{t}", res_task[lay] + n))
                else:
                    act.wait_ge(bank_free[t], g0 + n + 2)

            act.wait_ge(h_ready, KT * (2 * lay + 2))
            if lay in (1, 2):
                act_load_mod(act, lay - 1)
            act.wait_ge(new_out, (0, 64, 80, 144)[lay])
            if gated:
                act_load_gate(act, lay)
            if lay == 1:
                act_load_final(act, 0)
            if lay == 3:
                act_load_final(act, 1)
            for n in range(4):
                for ahead in ((0, 1) if n == 0 else (n + 1,) if n < 3 else ()):
                    act.dma_start(arena[:, XR + 4 * (ahead % 2):XR + 4 * (ahead % 2) + 4, :],
                                  cols_of(src, ahead)).then_inc(old_in, 16)
                    act.wait_ge(old_in, 16 * (4 * lay + ahead + 1))
                if lay == 0:
                    act_mods(act, G_OUT1, n)
                if lay == 1 and n:
                    act_mods(act, G_OUT2 + 1, n - 1)
                for t in range(TT):
                    summed(n, t)
                    act.wait_ge(res_a.sem, res_a.at(f"q{t - 1}", 4 * lay + n) if t else
                                res_a.at("q3", 4 * lay + n, back=1))
                    nc.scalar.activation(page(JUNK), xp[:, t, n * W:(n + 1) * W], ACT.Square,
                                         accum_out=square_sum[:, t, n:n + 1]).then_inc(res_a.sem, 1)
                if store:
                    act.dma_start(cols_of(x_mid, n), xp[:, :, n * W:(n + 1) * W]).then_inc(new_out, 16)

        def dve_residual(v, lay, g0, gated):
            if gated:
                dve_gate(v, lay)
            for n in range(4):
                if n == 3 and lay in (1, 2):
                    dve_mod_cols(v, lay - 1)
                if lay == 0:
                    dve_mods(v, G_OUT1, n)
                if lay == 1 and n:
                    dve_mods(v, G_OUT2 + 1, n - 1)
                v.wait_ge(old_in, 16 * (4 * lay + n + 1))
                for t in range(TT):
                    new = xp[:, t, n * W:(n + 1) * W]
                    old = page(XR + 4 * (n % 2) + t)
                    full(v, g0 + n, t)
                    if gated:
                        v.wait_ge(res_v.sem, res_v.at(f"s{t}", res_task[lay] + n, back=1))
                        nc.vector.tensor_tensor(page(TMP + t), bank[t][:], page(GATE + n),
                                                ALU.mult).then_inc(bank_free[t], 1)
                    else:
                        nc.vector.tensor_tensor(new, bank[t][:], old, ALU.add).then_inc(bank_free[t], 1)
                if gated:
                    for t in range(TT):
                        v.wait_ge(bank_free[t], g0 + n + 2)
                        nc.vector.tensor_tensor(xp[:, t, n * W:(n + 1) * W], page(TMP + t),
                                                page(XR + 4 * (n % 2) + t), ALU.add).then_inc(res_v.sem, 1)

        final_in = sem("final_in")
        final_v = steps("final_v", "clear r0 r1 r2 r3")
        final_a = steps("final_a", "q0 q1 q2 q3")

        def act_load_final(act, q):
            act.dma_start(page(ROWS, 4), row(f"final{q}", D)).then_inc(final_in, 16)

        def dve_final(v, q):
            v.wait_ge(norm_v.sem, norm_v.at("total", 2 + 3 * q))
            nc.vector.memset(small[:, 0:16], 0.0).then_inc(final_v.sem, 1)
            v.wait_ge(final_in, 16 * (q + 1))
            for t in range(TT):
                nc.vector.scalar_tensor_tensor(xp[:, t, :], xp[:, t, :], rstd[:, t:t + 1], page(ROWS, 4),
                                               ALU.mult, ALU.mult).then_inc(final_v.sem, 1)

        def act_final(act, q):
            act.wait_ge(final_v.sem, final_v.at("clear", q))
            for t in range(TT):
                act.wait_ge(final_v.sem, final_v.at(f"r{t}", q))
                act.wait_ge(final_a.sem, final_a.at(f"q{t - 1}", q) if t else final_a.at("q3", q, back=1))
                nc.scalar.activation(page(JUNK, 4), xp[:, t, :], ACT.Square,
                                     accum_out=square_sum[:, t, 0:1]).then_inc(final_a.sem, 1)

        lru_in = [sem(f"lru_in{n}") for n in range(2)]
        lru_p = steps("lru_p", "a0 x0 a1 x1", before=2)
        lru_a = steps("lru_a", "sr0 si0 sr1 si1 tanh0 exp0 tanh1 exp1 sqrt0 sqrt1")
        lru_c = steps("lru_c", "c2 c0 c1 c3")
        lru_v = steps("lru_v", "ix0 ix1 q0 q1 u0 u1 h0 h1 y yg", before=2)

        def lru_page(which, odd, n=1):
            return page(LRU_SET[odd] + which, n)

        def pe_lru(pe, k, odd):
            j = 2 * k + odd
            pe.wait_ge(lru_in[odd], 16 * (k + 1))
            pe.wait_ge(lru_c.sem, lru_c.at("c3", j))
            pe.wait_ge(lru_a.sem, lru_a.at("si1", j, back=1))
            for n in range(4):
                nc.tensor.matmul(bank[4 + n][:], lru_page(LW, odd)[:, n * P:(n + 1) * P], lru_page(XC, odd),
                                 start=True, stop=True).then_inc(lru_p.sem, 1)

        def act_lru_load(act, j, odd):
            act.wait_ge(lru_p.sem, lru_p.at("x1", j, back=2))
            act.dma_start(lru_page(LW, odd), lru_w[bass.ds(j, 1)].rearrange("a p n -> p (a n)")).then_inc(lru_in[odd], 16)

        def act_lru(act, j, odd):
            act.wait_ge(lru_v.sem, lru_v.at("yg", j, back=2))
            for n, (bias, dst) in enumerate((("ba", GR0), ("bx", GI0), ("ba", GR1), ("bx", GI1))):
                act.wait_ge(lru_p.sem, lru_p.at(("a0", "x0", "a1", "x1")[n], j))
                nc.scalar.activation(lru_page(dst, odd), bank[4 + n][:], ACT.Sigmoid,
                                     bias=col(bias, LRU_TILES * (n // 2) + j)).then_inc(lru_a.sem, 1)
            for d, gr in ((0, GR0), (1, GR1)):
                decay = [x[:, bass.ds(LRU_TILES * d + j, 1)] for x in (lru_half, lru_decay)]
                act.wait_ge(lru_a.sem, lru_a.at(f"sr{d}", j))
                nc.scalar.activation(lru_page(TH + d, odd), lru_page(gr, odd), ACT.Tanh,
                                     scale=decay[0]).then_inc(lru_a.sem, 1)
                nc.scalar.activation(lru_page(EA + d, odd), lru_page(gr, odd), ACT.Exp,
                                     scale=decay[1]).then_inc(lru_a.sem, 1)
            for d in range(2):
                act.wait_ge(lru_a.sem, lru_a.at(f"tanh{d}", j))
                nc.scalar.activation(lru_page(TH + d, odd), lru_page(TH + d, odd), ACT.Sqrt,
                                     scale=-1.0).then_inc(lru_a.sem, 1)

        def dve_lru_conv(v, j, odd):
            v.wait_ge(lru_p.sem, lru_p.at("x1", j, back=2))
            v.wait_ge(lru_v.sem, lru_v.at("ix1", j, back=2))
            own = lambda name: v.wait_ge(lru_c.sem, lru_c.at(name, j))
            x, xc = page(P_XL + j), lru_page(XC, odd)
            cw = lambda w: col("conv_w", LRU_TILES * w + j)
            nc.vector.tensor_scalar(xc, x, cw(2), col("conv_b", j), ALU.mult, ALU.add).then_inc(lru_c.sem, 1)
            own("c2")
            nc.vector.scalar_tensor_tensor(xc[:, 2:S], arena_cols(P_XL + j, 0, S - 2), cw(0), xc[:, 2:S],
                                           ALU.mult, ALU.add).then_inc(lru_c.sem, 1)
            own("c0")
            nc.vector.scalar_tensor_tensor(xc[:, 1:S], arena_cols(P_XL + j, 0, S - 1), cw(1), xc[:, 1:S],
                                           ALU.mult, ALU.add).then_inc(lru_c.sem, 1)
            own("c1")
            nc.vector.scalar_tensor_tensor(xc[:, 0:S - 1], arena_cols(P_XL + j, 1, S), cw(3), xc[:, 0:S - 1],
                                           ALU.mult, ALU.add).then_inc(lru_c.sem, 1)

        def dve_lru(v, j, odd):
            own = lambda name: v.wait_ge(lru_v.sem, lru_v.at(name, j))
            from_act = lambda name: v.wait_ge(lru_a.sem, lru_a.at(name, j))
            pg = lambda which: lru_page(which, odd)
            v.wait_ge(lru_c.sem, lru_c.at("c3", j))
            for d, gi in ((0, GI0), (1, GI1)):
                from_act(f"si{d}")
                nc.vector.tensor_tensor(pg(gi), pg(gi), pg(XC), ALU.mult).then_inc(lru_v.sem, 1)
            for d, gi in ((0, GI0), (1, GI1)):
                from_act(f"exp{d}")
                own(f"ix{d}")
                nc.vector.scalar_tensor_tensor(pg(gi), pg(EA + d), 1.0, pg(gi), ALU.add,
                                               ALU.mult).then_inc(lru_v.sem, 1)
            for d, gi in ((0, GI0), (1, GI1)):
                from_act(f"sqrt{d}")
                own(f"q{d}")
                nc.vector.tensor_tensor(pg(gi), pg(gi), pg(TH + d), ALU.mult).then_inc(lru_v.sem, 1)
            for d, gi in ((0, GI0), (1, GI1)):
                own(f"u{d}")
                turn = slice(None, None, -1) if d else slice(None)
                nc.vector.tensor_tensor_scan(pg(TH + d)[:, turn], pg(EA + d)[:, turn], pg(gi)[:, turn], 0.0,
                                             ALU.mult, ALU.add).then_inc(lru_v.sem, 1)
            own("h1")
            nc.vector.tensor_tensor(pg(TH), pg(TH), pg(TH + 1), ALU.add).then_inc(lru_v.sem, 1)
            own("y")
            nc.vector.tensor_tensor(page(P_XL + j), pg(TH), page(P_GL + j), ALU.mult).then_inc(lru_v.sem, 1)

        def arena_cols(pg, a, b):
            if isinstance(pg, int):
                return arena[:, pg, a:b]
            return arena[:, bass.ds(pg, 1), a:b].rearrange("p a n -> p (a n)")

        class Attention:

            def __init__(self, tag, normed, masked, lo, hi, keys_turn, query_turn, pages):
                self.normed, self.masked, self.lo, self.hi, self.pg = normed, masked, lo, hi, pages
                rot = "n g A Bl Bh r" if normed else "A Bl Bh r"
                self.keys_turn, self.query_turn = keys_turn, query_turn
                self.rot_v = steps(tag + "_rot_v", rot)
                self.val_v = steps(tag + "_val_v", "vc")
                self.kv_p = steps(tag + "_kv_p", "turned")
                self.kv_a = steps(tag + "_kv_a", "kT")
                score = ["add{0}", "max{0}", "bias{0}"] if masked else ["max{0}", "bias{0}"]
                names = []
                for pair in ((0, 1), (2, 3)):
                    names += [x.format(t) for t in pair for x in score]
                    names += [f"{x}{t}" for t in pair for x in ("rec", "norm")]
                self.s_v = steps(tag + "_s_v", names + ["out"])
                self.p = steps(tag + "_p", "q s0 s1 t0 t1 s2 s3 t2 t3 o")
                self.a = steps(tag + "_a", "qT e0 e1 T0 T1 e2 e3 T2 T3")

            def rotate(self, v, task, src, dst, rs, gain):
                st = self.rot_v
                v.wait_ge(st.sem, st.at("r", task, back=1))
                pg = self.pg
                tok = lambda p: page(p).rearrange("p (t n) -> p t n", n=HD)
                x = src
                if self.normed:
                    nc.vector.tensor_tensor(tok(pg["X"]), x, rs, ALU.mult).then_inc(st.sem, 1)
                    v.wait_ge(st.sem, st.at("n", task))
                    nc.vector.tensor_tensor(tok(pg["X"]), tok(pg["X"]), gain, ALU.mult).then_inc(st.sem, 1)
                    v.wait_ge(st.sem, st.at("g", task))
                    x = tok(pg["X"])
                nc.vector.tensor_tensor(tok(pg["A"]), x, tok(pg["C"]), ALU.mult).then_inc(st.sem, 1)
                lo, hi = self.lo, self.hi
                nc.vector.tensor_tensor(lo(tok(pg["B"])), hi(x), lo(tok(pg["S"])), ALU.mult).then_inc(st.sem, 1)
                nc.vector.tensor_tensor(hi(tok(pg["B"])), lo(x), hi(tok(pg["S"])), ALU.mult).then_inc(st.sem, 1)
                v.wait_ge(st.sem, st.at("Bh", task))
                nc.vector.tensor_tensor(page(dst), page(pg["A"]), page(pg["B"]), ALU.add).then_inc(st.sem, 1)

            def dve_keys(self, v, i, k, rs=None, gain=None):
                v.wait_ge(self.kv_p.sem, self.kv_p.at("turned", i, back=1))
                self.rotate(v, self.keys_turn(i), k, self.pg["kcur"], rs, gain)

            def dve_vals(self, v, i, head, val):
                v.wait_ge(self.s_v.sem, self.s_v.at("out", head, back=1))
                nc.vector.tensor_copy(page(self.pg["vcur"]).rearrange("p (t n) -> p t n", n=HD),
                                      val).then_inc(self.val_v.sem, 1)

            def dve_q(self, v, i, kv, q, rs=None, gain=None):
                v.wait_ge(self.p.sem, self.p.at("q", i, back=1))
                self.rotate(v, self.query_turn(i, kv), q, self.pg["qcur"], rs, gain)

            def pe_kv(self, pe, i, head):
                pe.wait_ge(self.rot_v.sem, self.rot_v.at("r", self.keys_turn(i)))
                pe.wait_ge(self.s_v.sem, self.s_v.at("out", head, back=1))
                for t in range(TT):
                    mm = nc.tensor.transpose(bank[6][:, t * P:(t + 1) * P],
                                             page(self.pg["kcur"])[:, t * P:(t + 1) * P], ident[:])
                mm.then_inc(self.kv_p.sem, 1)

            def act_kv(self, act, i):
                act.wait_ge(self.kv_p.sem, self.kv_p.at("turned", i))
                nc.scalar.copy(page(self.pg["kT"]), bank[6][:]).then_inc(self.kv_a.sem, 1)

            def pe_queries(self, pe, i, kv):
                pe.wait_ge(self.rot_v.sem, self.rot_v.at("r", self.query_turn(i, kv)))
                pe.wait_ge(self.s_v.sem, self.s_v.at("out", i, back=1))
                for t in range(TT):
                    mm = nc.tensor.transpose(bank[4][:, t * P:(t + 1) * P],
                                             page(self.pg["qcur"])[:, t * P:(t + 1) * P], ident[:])
                mm.then_inc(self.p.sem, 1)

            def pe_scores(self, pe, i, kv, pair):
                pe.wait_ge(self.kv_a.sem, self.kv_a.at("kT", kv))
                pe.wait_ge(self.a.sem, self.a.at("qT", i))
                for t in pair:
                    if t >= 2:
                        pe.wait_ge(self.a.sem, self.a.at(f"e{t - 2}", i))
                        if self.masked:
                            pe.wait_ge(self.s_v.sem, self.s_v.at(f"add{t - 2}", i))
                    nc.tensor.matmul(bank[5 + t % 2][:], page(self.pg["qT"])[:, t * P:(t + 1) * P],
                                     page(self.pg["kT"]), start=True, stop=True).then_inc(self.p.sem, 1)

            def turn_bank(self, t):
                return bank[4 if t % 2 else 7]

            def pe_turn_probs(self, pe, i, pair):
                for t in pair:
                    pe.wait_ge(self.s_v.sem, self.s_v.at(f"norm{t}", i))
                    if t >= 2:
                        pe.wait_ge(self.a.sem, self.a.at(f"T{t - 2}", i))
                    for k in range(TT):
                        mm = nc.tensor.transpose(self.turn_bank(t)[:, k * P:(k + 1) * P],
                                                 page(self.pg["P"] + t % 2)[:, k * P:(k + 1) * P], ident[:])
                    mm.then_inc(self.p.sem, 1)

            def pe_values(self, pe, i, kv):
                pe.wait_ge(self.a.sem, self.a.at("T3", i))
                pe.wait_ge(self.val_v.sem, self.val_v.at("vc", kv))
                for k in range(TT):
                    mm = nc.tensor.matmul(bank[4][:], page(self.pg["vcur"])[:, k * P:(k + 1) * P],
                                          page(self.pg["PT"] + k), start=(k == 0), stop=(k == TT - 1))
                mm.then_inc(self.p.sem, 1)

            def act_head(self, act, i):
                pg, p, sv = self.pg, self.p, self.s_v
                act.wait_ge(p.sem, p.at("q", i))
                nc.scalar.copy(page(pg["qT"]), bank[4][:]).then_inc(self.a.sem, 1)
                for pair in ((0, 1), (2, 3)):
                    for t in pair:
                        act.wait_ge(sv.sem, sv.at(f"bias{t}", i))
                        src = page(pg["A"] + t % 2) if self.masked else bank[5 + t % 2][:]
                        nc.scalar.activation(page(pg["P"] + t % 2), src, ACT.Exp, bias=row_bias[:, t % 2:t % 2 + 1],
                                             scale=SCALE, accum_out=row_sum[:, t % 2:t % 2 + 1]).then_inc(self.a.sem, 1)
                    for t in pair:
                        act.wait_ge(p.sem, p.at(f"t{t}", i))
                        nc.scalar.copy(arena[:, pg["PT"]:pg["PT"] + TT, t * P:(t + 1) * P],
                                       self.turn_bank(t)[:].rearrange("p (k n) -> p k n", n=P)).then_inc(self.a.sem, 1)

            def dve_head(self, v, i, out, ahead=None):
                pg, p, sv = self.pg, self.p, self.s_v
                for pair in ((0, 1), (2, 3)):
                    for t in pair:
                        b = t % 2
                        v.wait_ge(p.sem, p.at(f"s{t}", i))
                        src = bank[5 + b][:]
                        if self.masked:
                            nc.vector.tensor_tensor(page(pg["A"] + b), src, page(pg["mask"] + t),
                                                    ALU.add).then_inc(sv.sem, 1)
                            v.wait_ge(sv.sem, sv.at(f"add{t}", i))
                            src = page(pg["A"] + b)
                        nc.vector.tensor_reduce(row_max[:, b:b + 1], src, AX.X, ALU.max).then_inc(sv.sem, 1)
                        v.wait_ge(sv.sem, sv.at(f"max{t}", i))
                        nc.vector.tensor_scalar(row_bias[:, b:b + 1], row_max[:, b:b + 1], -SCALE, None,
                                                ALU.mult).then_inc(sv.sem, 1)
                    for t in pair:
                        b = t % 2
                        v.wait_ge(self.a.sem, self.a.at(f"e{t}", i))
                        nc.vector.reciprocal(row_rec[:, b:b + 1], row_sum[:, b:b + 1]).then_inc(sv.sem, 1)
                        v.wait_ge(sv.sem, sv.at(f"rec{t}", i))
                        nc.vector.tensor_scalar(page(pg["P"] + b), page(pg["P"] + b), row_rec[:, b:b + 1], None,
                                                ALU.mult).then_inc(sv.sem, 1)
                if ahead:
                    ahead()
                v.wait_ge(p.sem, p.at("o", i))
                nc.vector.tensor_copy(out, bank[4][:]).then_inc(sv.sem, 1)

        def halves(n, first):
            def pick(ap):
                if 2 * n == HD:
                    return ap[:, :, 0:n] if first else ap[:, :, n:]
                v4 = ap.rearrange("p t (b h e) -> p t b h e", h=2, e=n)
                return v4[:, :, :, 0 if first else 1, :]
            return pick

        att1 = Attention("att1", True, False, halves(HD // 4, True), halves(HD // 4, False),
                         lambda kv: (HEADS // KV_HEADS + 1) * kv, lambda h, kv: h + kv + 1,
                         dict(C=36, S=37, A=38, B=39, qcur=40, kcur=41, vcur=42, qT=43, kT=44, P=45, X=47, PT=P_GL + 4))
        att3 = Attention("att3", False, True, halves(HD // 2, True), halves(HD // 2, False),
                         lambda h: 2 * h, lambda h, kv: 2 * h + 1,
                         dict(C=32, S=33, A=34, B=35, qcur=36, kcur=37, vcur=38, qT=39, kT=40, P=41, PT=43, mask=47))

        QK = HEADS + KV_HEADS
        qkv = arena[:, P_QKV:P_QKV + 12, :].rearrange("p a n -> p (a n)").rearrange("p (t n) -> p t n", t=TT)
        gains = page(48)[:, 0:2 * HD]
        QK_PARTS = ((0, KV_HEADS * HD, 0, KV_HEADS), (W, 2 * W, KV_HEADS, KV_HEADS + 4), (2 * W, 3 * W, KV_HEADS + 4, QK))
        qk_v = steps("qk_v", "q0 r0 q1 r1 q2 r2 q3 r3 rec")
        qk_a = steps("qk_a", "root")
        rope_in = sem("rope_in")
        head_sq3 = head_sq[:, 0:TT * QK].rearrange("p (t n) -> p t n", t=TT)
        head_rs3 = head_rstd[:, 0:TT * QK].rearrange("p (t n) -> p t n", t=TT)

        def act_load_rope(act, lay, att):
            act.dma_start(page(att.pg["C"], 2), rope_d[lay]).then_inc(rope_in, 16)

        def dve_qk_stats(v, part):
            c0, c1, h0, h1 = QK_PARTS[part]
            group_written(v, part)
            for t in range(TT):
                sq = page(P_XL)[:, 0:c1 - c0]
                v.wait_ge(qk_v.sem, qk_v.at(f"r{t - 1}", part) if t else qk_v.at("rec", part, back=1))
                nc.vector.tensor_tensor(sq, qkv[:, t, c0:c1], qkv[:, t, c0:c1], ALU.mult).then_inc(qk_v.sem, 1)
                v.wait_ge(qk_v.sem, qk_v.at(f"q{t}", part))
                nc.vector.tensor_reduce(head_sq3[:, t, h0:h1], sq.rearrange("p (h n) -> p h n", n=HD), AX.X,
                                        ALU.add).then_inc(qk_v.sem, 1)
            v.wait_ge(qk_a.sem, qk_a.at("root", part))
            nc.vector.reciprocal(head_rs3[:, :, h0:h1], head_rs3[:, :, h0:h1]).then_inc(qk_v.sem, 1)
            v.wait_ge(qk_v.sem, qk_v.at("rec", part))

        def act_qk_root(act, part):
            _, _, h0, h1 = QK_PARTS[part]
            act.wait_ge(qk_v.sem, qk_v.at("r3", part))
            nc.scalar.activation(head_rs3[:, :, h0:h1], head_sq3[:, :, h0:h1], ACT.Sqrt, bias=eps[:],
                                 scale=1.0 / HD).then_inc(qk_a.sem, 1)

        def head_cols(x, base, h):
            return x[:, :, bass.ds(base + h * HD, HD)]

        def rs_of(h):
            return head_rs3[:, :, bass.ds(h, 1)].to_broadcast([P, TT, HD])

        def gain_of(n):
            g = gains[:, n * HD:(n + 1) * HD]
            return g.rearrange("p (o n) -> p o n", o=1).to_broadcast([P, TT, HD])

        v3 = arena[:, P_MV:P_MV + 16, :].rearrange("p a n -> p (a n)").rearrange("p (t n) -> p t n", t=TT)
        gate_in = sem("gate_in")
        gate_split = sem("gate_split")
        rows_in = sem("rows_in")
        tri_in = sem("tri_in")
        gain_in = sem("gain_in")
        gate_p = steps("gate_p", "rows cols")
        gate_a = steps("gate_a", "abs exp ln em")
        gate_v = steps("gate_v", "ones bias lf Ff Fb g Mf Mb m cols")
        m_p = steps("m_p", "Mf Mb s0 s1 s2 s3 n0 n1 n2 n3")
        m_a = steps("m_a", "k v nf nb xf0 xb0 xf1 xb1 xf2 xb2 xf3 xb3 c0 c1 c2 c3")
        m_v = steps("m_v", ["Mh"] + [f"{x}{i}" for i in range(TT) for x in ("ef", "eb", "pf", "pb", "mf", "mb")]
                    + "df0 db0 mf_0 mb_0 rec0 df1 db1 mf_1 mb_1 rec1 n0 df2 db2 mf_2 mb_2 rec2 n1 df3 db3 mf_3 mb_3 rec3 n2 n3".split())
        o_v = steps("o_v", [f"{x}{t}" for t in range(TT) for x in "gsr"])
        z_v = steps("z_v", [f"{x}{t}" for t in range(TT) for x in "nwz"])
        m_root = sem("m_root")
        m_rec = sem("m_rec")
        M_V1 = M_V + 1
        m_cols = page(TRI + 2)[:, W - P:W]
        vcur = page(TRI, 3)[:, 2 * P:2 * P + TT * M_V1].rearrange("p (t n) -> p t n", n=M_V1)
        rows8 = lambda p: arena[0:8, p:p + 2, :].rearrange("p a n -> p (a n)")
        row8 = lambda p: arena[0:8, p, :]
        R_I, R_F, R_L, R_S, R_G = 33, 35, 37, 39, 41
        back = slice(None, None, -1)

        def pe_gates(pe):
            pe.wait_ge(gate_split, 2)
            pe.wait_ge(h_ready, 3 * KT)
            for k in range(KT):
                ws = slice(k * 32, (k + 1) * 32)
                for n, (a, b) in enumerate(((w_hi[:, 0, ws], h_hi[:, k, :]), (w_hi[:, 0, ws], h_lo[:, k, :]),
                                            (w_lo[:, 0, ws], h_hi[:, k, :]))):
                    mm = nc.tensor.matmul(bank[4][0:32, :], a, b, start=(k == 0 and n == 0), stop=(k == KT - 1 and n == 2))
            mm.then_inc(gate_p.sem, 1)

        def pe_gate_cols(pe):
            pe.wait_ge(gate_v.sem, gate_v.at("Mb"))
            pe.wait_ge(gate_a.sem, gate_a.at("em"))
            for n, src in enumerate((R_G, R_G + 1, R_L, R_L + 1)):
                for t in range(TT):
                    mm = nc.tensor.transpose(bank[4][:, n * 32 + t * 8:n * 32 + t * 8 + 8],
                                             row8(src)[:, t * P:(t + 1) * P], ident[0:8, 0:8])
            mm.then_inc(gate_p.sem, 1)

        def act_gates(act):
            act.wait_ge(gate_v.sem, gate_v.at("bias"))
            for n, dst in enumerate((R_I, R_I + 1, R_F, R_F + 1)):
                act.dma_start(row8(dst), arena[8 * n:8 * n + 8, GATES, :]).then_inc(rows_in, 16)
            act.wait_ge(rows_in, 64)
            nc.scalar.activation(rows8(R_L), rows8(R_F), ACT.Abs).then_inc(gate_a.sem, 1)
            act.wait_ge(gate_a.sem, gate_a.at("abs"))
            nc.scalar.activation(rows8(R_L), rows8(R_L), ACT.Exp, scale=-1.0).then_inc(gate_a.sem, 1)
            act.wait_ge(gate_a.sem, gate_a.at("exp"))
            nc.scalar.activation(rows8(R_L), rows8(R_L), ACT.Ln, bias=one[0:8]).then_inc(gate_a.sem, 1)
            act.wait_ge(gate_v.sem, gate_v.at("m"))
            nc.scalar.activation(rows8(R_L), rows8(R_S), ACT.Exp, scale=-1.0).then_inc(gate_a.sem, 1)

        def dve_gates(v):
            nc.vector.memset(vcur[:, :, M_V:M_V1], 1.0).then_inc(gate_v.sem, 1)
            v.wait_ge(gate_p.sem, gate_p.at("rows"))
            nc.vector.tensor_scalar(arena[0:32, GATES, :], bank[4][0:32, :], col("m_bias")[0:32], None, ALU.add).then_inc(gate_v.sem, 1)
            v.wait_ge(rows_in, 64)
            v.wait_ge(gate_a.sem, gate_a.at("ln"))
            nc.vector.scalar_tensor_tensor(rows8(R_F), rows8(R_F), 0.0, rows8(R_L), ALU.min,
                                           ALU.subtract).then_inc(gate_v.sem, 1)
            v.wait_ge(gate_v.sem, gate_v.at("lf"))
            for n, turn in ((0, slice(None)), (1, back)):
                nc.vector.tensor_tensor_scan(row8(R_S + n)[:, turn], one[0:8].to_broadcast([8, S]),
                                             row8(R_F + n)[:, turn], 0.0, ALU.mult, ALU.add).then_inc(gate_v.sem, 1)
            v.wait_ge(gate_v.sem, gate_v.at("Fb"))
            nc.vector.tensor_tensor(rows8(R_G), rows8(R_I), rows8(R_S), ALU.subtract).then_inc(gate_v.sem, 1)
            v.wait_ge(gate_v.sem, gate_v.at("g"))
            for n, turn in ((0, slice(None)), (1, back)):
                nc.vector.tensor_tensor_scan(row8(MROW + n)[:, turn], row8(R_G + n)[:, turn],
                                             row8(R_G + n)[:, turn], 0.0, ALU.max, ALU.max).then_inc(gate_v.sem, 1)
            v.wait_ge(gate_v.sem, gate_v.at("Mb"))
            nc.vector.tensor_tensor(rows8(R_S), rows8(R_S), rows8(MROW), ALU.add).then_inc(gate_v.sem, 1)
            v.wait_ge(gate_p.sem, gate_p.at("cols"))
            nc.vector.tensor_copy(m_cols[:], bank[4][:, 0:P]).then_inc(gate_v.sem, 1)
            v.wait_ge(gate_v.sem, gate_v.at("cols"))

        def fwd(p, i):
            return arena[:, p, i * P:S]

        def bwd(p, i):
            return arena[:, p, 0:(i + 1) * P]

        def pe_m_max(pe, h):
            pe.wait_ge(m_v.sem, m_v.at("Mh", h))
            for n in range(2):
                nc.tensor.matmul(bank[4 + n][:], ones[0:8, :], row8(MHEAD + n), start=True,
                                 stop=True).then_inc(m_p.sem, 1)

        def pe_m_scores(pe, h, pair):
            pe.wait_ge(m_a.sem, m_a.at("k", h))
            for i in pair:
                st, name = ((m_a, "nf"), (m_a, "nb"), (m_v, "pb0"), (m_v, "pb1"))[i]
                pe.wait_ge(st.sem, st.at(name, h))
                nc.tensor.matmul(bank[4 + i % 2][:], page(KCUR)[:, i * P:(i + 1) * P], page(P_MQ + h),
                                 start=True, stop=True).then_inc(m_p.sem, 1)

        def m_bank(j, d):
            return bank[(6, 4)[j % 2] + d]

        def pe_m_values(pe, h):
            pe.wait_ge(m_v.sem, m_v.at("mb3", h))
            pe.wait_ge(m_a.sem, m_a.at("v", h))
            for j in range(TT):
                if j >= 2:
                    pe.wait_ge(m_v.sem, m_v.at(f"n{j - 2}", h))
                for d in range(2):
                    tiles = [i for i in range(TT) if (i <= j if d == 0 else i >= j)]
                    for i in tiles:
                        mm = nc.tensor.matmul(m_bank(j, d)[:, 0:M_V1], arena[:, PP + i + d, j * P:(j + 1) * P],
                                              vcur[:, i, :], start=(i == tiles[0]), stop=(i == tiles[-1]))
                mm.then_inc(m_p.sem, 1)

        def pe_m_group(pe, g, h0):
            for n in range(2):
                h = h0 + n
                pe_m_max(pe, h)
                pe_chunks(pe, g, 4 * n, 4 * n + 1, True, 2 * KT)
                pe_m_scores(pe, h, (0, 1))
                pe_chunks(pe, g, 4 * n + 1, 4 * n + 2, True, 2 * KT)
                pe_m_scores(pe, h, (2, 3))
                pe_chunks(pe, g, 4 * n + 2, 4 * n + 3, True, 2 * KT)
                pe_m_values(pe, h)
                pe_chunks(pe, g, 4 * n + 3, 4 * n + 4, True, 2 * KT)

        def m_fwd(j):
            return page(NM + j % 2)[:, 0:M_V]

        def m_out(j, h):
            return v3[:, j, bass.ds(h * M_V, M_V)]

        def act_mlstm(act, h):
            at = lambda st, name, back=0: act.wait_ge(st.sem, st.at(name, h, back))
            at(m_p, "s3", 1)
            nc.scalar.copy(page(KCUR), page(P_MK + h)).then_inc(m_a.sem, 1)
            at(m_p, "n3", 1)
            nc.scalar.copy(vcur[:, :, 0:M_V], v3[:, :, bass.ds(h * M_V, M_V)]).then_inc(m_a.sem, 1)
            for n, name in enumerate(("Mf", "Mb")):
                at(m_p, name)
                nc.scalar.copy(page(NM + n), bank[4 + n][:]).then_inc(m_a.sem, 1)
            for i in range(TT):
                for n, (name, part) in enumerate((("ef", fwd), ("eb", bwd))):
                    at(m_v, f"{name}{i}")
                    nc.scalar.activation(part(EE + n, i), part(EE + n, i), ACT.Exp).then_inc(m_a.sem, 1)
            for j in range(TT):
                at(m_v, f"rec{j}")
                nc.scalar.activation(m_fwd(j), m_bank(j, 0)[:, 0:M_V], ACT.Copy,
                                     scale=den[:, 2 * j:2 * j + 1]).then_inc(m_a.sem, 1)

        def dve_mlstm(v, h):
            at = lambda st, name, back=0: v.wait_ge(st.sem, st.at(name, h, back))
            at(m_p, "Mb", 1)
            nc.vector.tensor_scalar(rows8(MHEAD), rows8(MROW), ident[0:8, bass.ds(h, 1)], -1.0, ALU.mult,
                                    ALU.mult).then_inc(m_v.sem, 1)
            for i in range(TT):
                if i:
                    at(m_v, f"mb{i - 1}")
                for n, part in enumerate((fwd, bwd)):
                    at(m_a, "nf" if n == 0 else "nb")
                    nc.vector.tensor_scalar(part(EE + n, i), part(NM + n, i),
                                            m_cols[:, bass.ds(n * 32 + i * 8 + h, 1)], 0.0, ALU.add,
                                            ALU.min).then_inc(m_v.sem, 1)
                at(m_p, f"s{i}")
                for n, part in enumerate((fwd, bwd)):
                    at(m_a, ("xf" if n == 0 else "xb") + str(i))
                    scores = bank[4 + i % 2][:, i * P:S] if n == 0 else bank[4 + i % 2][:, 0:(i + 1) * P]
                    nc.vector.tensor_tensor(part(PP + i + n, i), scores, part(EE + n, i),
                                            ALU.mult).then_inc(m_v.sem, 1)
                for n in range(2):
                    at(m_v, ("pf" if n == 0 else "pb") + str(i))
                    own = arena[:, PP + i + n, i * P:(i + 1) * P]
                    nc.vector.tensor_tensor(own, own, page(TRI)[:, n * P:(n + 1) * P], ALU.mult).then_inc(m_v.sem, 1)
            def add_back(j):
                at(m_a, f"c{j}")
                nc.vector.scalar_tensor_tensor(m_out(j, h), m_bank(j, 1)[:, 0:M_V], den[:, 2 * j + 1:2 * j + 2],
                                               m_fwd(j), ALU.mult, ALU.add).then_inc(m_v.sem, 1)

            for j in range(TT):
                at(m_p, f"n{j}")
                pair = den[:, 2 * j:2 * j + 2]
                for d in range(2):
                    nc.vector.tensor_scalar(pair[:, d:d + 1], m_bank(j, d)[:, M_V:M_V1], -1.0,
                                            m_cols[:, bass.ds((2 + d) * 32 + j * 8 + h, 1)], ALU.mult,
                                            ALU.max).then_inc(m_v.sem, 1)
                at(m_v, f"db{j}")
                for d in range(2):
                    nc.vector.scalar_tensor_tensor(pair[:, d:d + 1], m_bank(j, d)[:, M_V:M_V1], 1.0, pair[:, d:d + 1],
                                                   ALU.mult, ALU.max).then_inc(m_v.sem, 1)
                at(m_v, f"mb_{j}")
                nc.vector.reciprocal(pair, pair).then_inc(m_v.sem, 1)
                if j:
                    add_back(j - 1)
            add_back(TT - 1)

        def act_gate_evac(act, g, st, name, task, func):
            for t in range(TT):
                act.wait_ge(st.sem, st.at(f"{name}{t}", task, back=1))
                full(act, g, t)
                nc.scalar.activation(page(MO_TMP + t), bank[t][:], func).then_inc(bank_free[t], 1)

        def dve_mo(v, n):
            for t in range(TT):
                x, sq = v3[:, t, bass.ds(n * W, W)], page(MO_SQ + t)
                v.wait_ge(bank_free[t], G_MO + n + 2)
                nc.vector.tensor_tensor(x, x, page(MO_TMP + t), ALU.mult).then_inc(o_v.sem, 1)
                v.wait_ge(o_v.sem, o_v.at(f"g{t}", n))
                v.wait_ge(o_v.sem, o_v.at(f"r{t}", n, back=1))
                nc.vector.tensor_tensor(sq, x, x, ALU.mult).then_inc(o_v.sem, 1)
                v.wait_ge(o_v.sem, o_v.at(f"s{t}", n))
                nc.vector.tensor_reduce(head_sq[:, bass.ds(t * M_HEADS + 2 * n, 2)], sq.rearrange("p (h n) -> p h n", n=M_V),
                                        AX.X, ALU.add).then_inc(o_v.sem, 1)

        def dve_mz(v, n):
            for t in range(TT):
                x = v3[:, t, bass.ds(n * W, W)]
                by_head = x.rearrange("p (h n) -> p h n", n=M_V)
                rs = head_rstd[:, bass.ds(t * M_HEADS + 2 * n, 2)].rearrange("p (h o) -> p h o", o=1)
                nc.vector.tensor_tensor(by_head, by_head, rs.to_broadcast([P, 2, M_V]), ALU.mult).then_inc(z_v.sem, 1)
                v.wait_ge(z_v.sem, z_v.at(f"n{t}", n))
                nc.vector.tensor_tensor(x, x, page(MZ_GAIN, 4)[:, bass.ds(n * W, W)], ALU.mult).then_inc(z_v.sem, 1)
                v.wait_ge(z_v.sem, z_v.at(f"w{t}", n))
                v.wait_ge(bank_free[t], G_MZ + n + 2)
                nc.vector.tensor_tensor(x, x, page(MO_TMP + t), ALU.mult).then_inc(z_v.sem, 1)

        cv_v = steps("cv_v", [f"{x}{m}" for x in ("w1", "w0", "w2") for m in range(4)] + [f"z{m}" for m in range(4)])

        def act_conv_u(act, j, g):
            act.wait_ge(cv_v.sem, cv_v.at("z3", j, back=1))
            act_evac(act, g, lambda m: page(C_U + m))

        def dve_conv_c(v, j, g):
            for m in range(4):
                v.wait_ge(bank_free[m], g + 1)
                full(v, g, m)
                nc.vector.tensor_tensor(page(C_U + m), bank[m][:], page(C_U + m), ALU.mult).then_inc(bank_free[m], 1)
            cw = lambda w, m: col("conv3_w", LRU_TILES * w + 4 * j + m)
            y = lambda m: page(P_YB + 4 * j + m)
            for m in range(4):
                v.wait_ge(bank_free[m], g + 2)
                nc.vector.tensor_scalar(y(m), page(C_U + m), cw(1, m), None, ALU.mult).then_inc(cv_v.sem, 1)
            for m in range(4):
                v.wait_ge(cv_v.sem, cv_v.at(f"w1{m}", j))
                nc.vector.scalar_tensor_tensor(y(m)[:, 1:S], page(C_U + m)[:, 0:S - 1], cw(0, m), y(m)[:, 1:S],
                                               ALU.mult, ALU.add).then_inc(cv_v.sem, 1)
            for m in range(4):
                v.wait_ge(cv_v.sem, cv_v.at(f"w0{m}", j))
                nc.vector.scalar_tensor_tensor(y(m)[:, 0:S - 1], page(C_U + m)[:, 1:S], cw(2, m), y(m)[:, 0:S - 1],
                                               ALU.mult, ALU.add).then_inc(cv_v.sem, 1)

        def dve_conv_b(v, j, g):
            for m in range(4):
                v.wait_ge(cv_v.sem, cv_v.at(f"w2{m}", j))
                full(v, g, m)
                nc.vector.tensor_tensor(page(P_YB + 4 * j + m), bank[m][:], page(P_YB + 4 * j + m),
                                        ALU.mult).then_inc(bank_free[m], 1)

        def act_conv_z(act, j, g):
            act.wait_ge(cv_v.sem, cv_v.at("w23", j))
            act_evac(act, g, lambda m: page(C_U + m), ACT.Silu)

        def dve_conv_z(v, j, g):
            for m in range(4):
                v.wait_ge(bank_free[m], g + 2)
                nc.vector.tensor_tensor(page(P_YB + 4 * j + m), page(P_YB + 4 * j + m), page(C_U + m),
                                        ALU.mult).then_inc(cv_v.sem, 1)

        mask_in = sem("mask_in")

        def half_cols(p, h):
            return arena[:, p:p + 4, bass.ds(h * HD, HD)]

        sv = arena[:, P_SV:P_SV + 16, :].rearrange("p a n -> p (a n)").rearrange("p (t n) -> p t n", t=TT)
        ln_in = sem("ln_in")
        ln_a = steps("ln_a", "s0 s1 s2 s3 root")
        ln_v = steps("ln_v", "sum mean rec c0 c1 c2 c3 a0 a1 a2 a3")
        sg_p = sem("sg_p")
        sg_v = sem("sg_v")
        u_v = steps("u_v", "m0 m1 m2 m3")

        def act_sgu_values(act):
            act.wait_ge(h_ready, 7 * KT)
            act.wait_ge(new_out, 144)
            act.dma_start(page(S_G, 4), row("ln_g", D)).then_inc(ln_in, 16)
            act.dma_start(page(S_B, 4), row("ln_b", D)).then_inc(ln_in, 16)
            act.dma_start(page(S_BS, 2), row("b_s", 2 * W)).then_inc(ln_in, 16)
            act.dma_start(page(S_WS, 2), ws_d).then_inc(ln_in, 16)
            with act.Fori(0, 4) as n:
                for t in range(TT):
                    full(act, G_SV + n, t)
                    nc.scalar.activation(sv[:, t, bass.ds(n * W, W)], bank[t][:], ACT.Gelu_apprx_tanh,
                                         accum_out=small[:, bass.ds(4 * t + n, 1)]).then_inc(bank_free[t], 1)
            act.wait_ge(ln_v.sem, ln_v.at("mean"))
            for t in range(TT):
                act.wait_ge(ln_a.sem, ln_a.n + t)
                nc.scalar.activation(page(S_TMP, 4), sv[:, t, :], ACT.Square, bias=mean[:, t:t + 1],
                                     accum_out=token_sum[:, t:t + 1]).then_inc(ln_a.sem, 1)
            act.wait_ge(ln_a.sem, ln_a.at("s3"))
            nc.scalar.activation(root, token_sum, ACT.Sqrt, bias=eps[:], scale=1.0 / D).then_inc(ln_a.sem, 1)
            act.wait_ge(ln_a.sem, ln_a.at("root"))

        def dve_sgu_values(v):
            group_written(v, G_SV + 3)
            nc.vector.tensor_reduce(mean, square_sum, AX.X, ALU.add).then_inc(ln_v.sem, 1)
            v.wait_ge(ln_v.sem, ln_v.at("sum"))
            nc.vector.tensor_scalar(mean, mean, -1.0 / D, None, ALU.mult).then_inc(ln_v.sem, 1)
            v.wait_ge(ln_a.sem, ln_a.at("root"))
            nc.vector.reciprocal(rstd, root).then_inc(ln_v.sem, 1)
            v.wait_ge(ln_v.sem, ln_v.at("rec"))
            v.wait_ge(ln_in, 64)
            for t in range(TT):
                nc.vector.scalar_tensor_tensor(sv[:, t, :], sv[:, t, :], mean[:, t:t + 1], page(S_G, 4), ALU.add,
                                               ALU.mult).then_inc(ln_v.sem, 1)
            for t in range(TT):
                v.wait_ge(ln_v.sem, ln_v.at(f"c{t}"))
                nc.vector.scalar_tensor_tensor(sv[:, t, :], sv[:, t, :], rstd[:, t:t + 1], page(S_B, 4), ALU.mult,
                                               ALU.add).then_inc(ln_v.sem, 1)

        def pe_sgu(pe, first, last):
            pe.wait_ge(ln_v.sem, ln_v.at("a3"))
            for f in range(first, last):
                if f >= 4:
                    pe.wait_ge(sg_v, f - 3)
                for n in range(TT):
                    mm = nc.tensor.matmul(bank[4 + f % 4][:, n * P:(n + 1) * P], sv[:, n, f * P:(f + 1) * P],
                                          page(S_WS, 2)[:, (f // 2) * P:(f // 2 + 1) * P], start=True, stop=True)
                mm.then_inc(sg_p, 1)

        def dve_sgu(v):
            for f in range(KT):
                v.wait_ge(sg_p, f + 1)
                bias = page(S_BS, 2)[:, (f // 2) * P:(f // 2 + 1) * P].rearrange("p (o n) -> p o n", o=1)
                nc.vector.tensor_tensor(page(P_MX + f).rearrange("p (t n) -> p t n", n=P),
                                        bank[4 + f % 4][:].rearrange("p (t n) -> p t n", n=P),
                                        bias.to_broadcast([P, TT, P]), ALU.add).then_inc(sg_v, 1)
            v.wait_ge(sg_v, KT)

        def act_sgu_gate(act, n, func):
            for m in range(4):
                act.wait_ge(u_v.sem, u_v.at(f"m{m}", n, back=1))
                full(act, G_SU + n, m)
                nc.scalar.activation(page(S_TMP + m), bank[m][:], func).then_inc(bank_free[m], 1)

        def dve_sgu_gate(v, n, tile):
            for m in range(4):
                v.wait_ge(bank_free[m], G_SU + n + 2)
                nc.vector.tensor_tensor(page(P_MX + tile + m), page(P_MX + tile + m), page(S_TMP + m),
                                        ALU.mult).then_inc(u_v.sem, 1)

        def mix3(f):
            return P_YB + f if f < LRU_TILES else P_YA + f - LRU_TILES

        def mix4(f):
            return P_MX + f

        ga_v = steps("ga_v", "m0 m1 m2 m3")

        def act_attn_gate(act, g0, task, n, tmp):
            for m in range(4):
                act.wait_ge(ga_v.sem, ga_v.at(f"m{m}", task + n, back=1))
                full(act, g0 + n, m)
                nc.scalar.activation(page(tmp + m), bank[m][:], ACT.Silu).then_inc(bank_free[m], 1)

        def dve_attn_gate(v, g0, task, n, tmp, ya):
            for m in range(4):
                v.wait_ge(bank_free[m], g0 + n + 2)
                nc.vector.tensor_tensor(page(ya + 4 * n + m), page(ya + 4 * n + m), page(tmp + m),
                                        ALU.mult).then_inc(ga_v.sem, 1)

        cols_in, ident_in = sem("cols_in"), sem("ident_in")
        x_loaded = [sem(f"x_loaded{t}") for t in range(TT)]
        first_square = sem("first_square")
        out_done = sem("out_done")

        def mix1(f):
            return P_XL + f if f < LRU_TILES else P_GA + f - LRU_TILES

        block = ctx.enter_context(nc.Block())

        @block.sync
        def _(sp):
            def weights(g, per=0, block=0):
                for c in range(NCH):
                    sp.wait_ge(w_ready, NCH * g + c + 1 + WREADY0 - RAW_SLOTS)
                    sp.dma_start(w_raw[:, c % RAW_SLOTS, :],
                                 wall[bass.ds(g, 1), :, c * CH * W:(c + 1) * CH * W]
                                 .rearrange("a p n -> p (a n)")).then_inc(raw_in[c % RAW_SLOTS], 16)
                    first_slab = {0: None, 1: 2 * c - NCH, 2: 2 * c}[per]
                    for i in () if first_slab is None or first_slab < 0 else (first_slab, first_slab + 1):
                        b, mc = block + i // NCH, i % NCH
                        if mc < 2:
                            sp.wait_ge(mod_sum.sem, mod_sum.at(f"k{13 + 2 * mc}", b, back=1))
                        else:
                            sp.wait_ge(mod_sum.sem, mod_sum.at(f"k{2 * mc - 3}", b))
                        sp.dma_start(page(MOD_RING + 2 * (mc % 2), 2),
                                     mods[bass.ds(b, 1), :, mc * CH * W:(mc + 1) * CH * W]
                                     .rearrange("a p n -> p (a n)")).then_inc(mod_in[mc % 2], 16)

            for m in range(4):
                sp.sem_inc(bank_free[m], 1)
            at = 0
            for first, n, per, block in RIDES:
                if at < first:
                    with sp.Fori(at, first) as g:
                        weights(g)
                if first == G_ZA:
                    sp.wait_ge(att3.s_v.sem, att3.s_v.at("out", HEADS - 1))
                with sp.Fori(0, n) as i:
                    weights(first + i, per, block + per * i)
                at = first + n
            with sp.Fori(at, GROUPS) as g:
                weights(g)

        @block.gpsimd
        def _(pool):
            pool.sem_inc(w_ready, WREADY0)
            pool.wait_ge(setup_v.sem, setup_v.at("zero"))

            def split(g, c, shift):
                raw, s = w_raw[:, c % RAW_SLOTS, :], (c + shift) % SPLIT_SLOTS
                pool.wait_ge(raw_in[c % RAW_SLOTS], 16 * (2 * g + c // RAW_SLOTS + 1))
                nc.gpsimd.tensor_tensor(w_hi[:, s, :], raw, zero[:].to_broadcast([P, CH * W]),
                                        ALU.add).then_inc(w_hi_done, 1)
                pool.wait_ge(w_hi_done, NCH * g + c + 1)
                nc.gpsimd.tensor_tensor(w_lo[:, s, :], raw, w_hi[:, s, :].bitcast(F32),
                                        ALU.subtract).then_inc(w_ready, 1)

            def group(g, first, shift):
                for c in range(first, NCH):
                    if c == 1:
                        pool.wait_ge(bank_full, 4 * g + FULL0)
                    else:
                        pool.wait_ge(w_used, (NCH - 1) * g + WUSED0 + (c - 1 if c else 0))
                    split(g, c, shift)

            with pool.Fori(0, G_MV) as g:
                group(g, 0, 0)
            pool.wait_ge(gate_in, 16)
            pool.wait_ge(w_used, (NCH - 1) * G_MV + WUSED0)
            nc.gpsimd.tensor_tensor(w_hi[:, 0, 0:W], page(GW), zero[:].to_broadcast([P, W]), ALU.add).then_inc(gate_split, 1)
            pool.wait_ge(gate_split, 1)
            nc.gpsimd.tensor_tensor(w_lo[:, 0, 0:W], page(GW), w_hi[:, 0, 0:W].bitcast(F32),
                                    ALU.subtract).then_inc(gate_split, 1)
            pool.wait_ge(bank_full, 4 * G_MV + FULL0)
            split(G_MV, 0, 1)
            pool.wait_ge(gate_p.sem, gate_p.at("rows"))
            split(G_MV, 1, 1)
            group(G_MV, 2, 1)
            with pool.Fori(G_MV + 1, GROUPS) as g:
                group(g, 0, 1)

        @block.vector
        def _(v):
            for st in (mod_sum, norm_v, res_v, final_v, lru_v, lru_c, att1.rot_v, att1.val_v, att1.s_v, att3.rot_v, att3.val_v,
                       att3.s_v, qk_v, setup_v, gate_v, m_v, o_v, z_v,
                       modc_v, modg_v, cv_v, ln_v, u_v, ga_v):
                v.sem_inc(st.sem, st.start)
            nc.vector.memset(zero[:], 0.0).then_inc(setup_v.sem, 1)
            nc.vector.memset(one[:], 1.0).then_inc(setup_v.sem, 1)
            nc.vector.memset(eps[:], EPS).then_inc(setup_v.sem, 1)
            nc.vector.memset(small[:], 0.0).then_inc(setup_v.sem, 1)
            nc.vector.memset(ones[:], 1.0).then_inc(setup_v.sem, 1)
            v.wait_ge(setup_a.sem, setup_a.at("ln"))
            low = page(ROWS)[:, 0:2 * LRU_TILES]
            nc.vector.tensor_scalar(low, col("lam", 0, 2 * LRU_TILES), 0.0, None, ALU.min).then_inc(setup_v.sem, 1)
            v.wait_ge(setup_v.sem, setup_v.at("min"))
            nc.vector.tensor_tensor(lru_decay[:], low, lru_decay[:], ALU.subtract).then_inc(setup_v.sem, 1)
            v.wait_ge(setup_v.sem, setup_v.at("sub"))
            nc.vector.tensor_scalar(lru_half[:], lru_decay[:], LRU_C / 2, None, ALU.mult).then_inc(setup_v.sem, 1)
            v.wait_ge(setup_v.sem, setup_v.at("half"))
            nc.vector.tensor_scalar(lru_decay[:], lru_decay[:], LRU_C, None, ALU.mult).then_inc(setup_v.sem, 1)
            v.wait_ge(setup_v.sem, setup_v.at("scale"))

            v.wait_ge(ident_in, 16)
            v.wait_ge(first_square, TT)
            dve_norm(v, 0)
            dve_turn(v, 0, TMP)
            keys1 = lambda kv: att1.dve_keys(v, kv, head_cols(qkv, 0, kv), rs_of(kv), gain_of(1))
            query1 = lambda h, kv: att1.dve_q(v, h, kv, head_cols(qkv, W, h), rs_of(h + KV_HEADS), gain_of(0))
            vals1 = lambda kv: att1.dve_vals(v, kv, kv * (HEADS // KV_HEADS), head_cols(qkv, KV_HEADS * HD, kv))
            dve_qk_stats(v, 0)
            dve_mods(v, G_Q, 0)
            dve_qk_stats(v, 1)
            v.wait_ge(rope_in, 32)
            keys1(0)
            query1(0, 0)
            vals1(0)
            dve_mods(v, G_Q, 1)
            dve_qk_stats(v, 2)

            def head1(h, *ahead):
                att1.dve_head(v, h, page(P_GA + h), lambda: [f(*of) for f, *of in ahead])

            with v.Fori(0, 3) as h:
                head1(h, (query1, h + 1, 0))
            head1(3, (keys1, 1), (query1, 4, 1))
            vals1(1)
            with v.Fori(4, 7) as h:
                head1(h, (query1, h + 1, 1))
            head1(7)
            group_written(v, G_GL + 1)
            dve_lru_conv(v, 0, 0)
            with v.Fori(0, 2) as i:
                for n in range(2):
                    dve_lru_conv(v, 2 * i + n + 1, 1 - n)
                    dve_lru(v, 2 * i + n, n)
            dve_attn_gate(v, G_GA, 0, 0, GA_TMP, P_GA)
            for j in range(4, LRU_TILES):
                if j + 1 < LRU_TILES:
                    dve_lru_conv(v, j + 1, (j + 1) % 2)
                dve_lru(v, j, j % 2)
            dve_split(v, 1, mix1, 0, 4)
            dve_attn_gate(v, G_GA, 0, 1, GA_TMP, P_GA)
            dve_split(v, 1, mix1, 4, KT)
            dve_residual(v, 0, G_OUT1, False)

            v.wait_ge(res_a.sem, res_a.at("q3", 3))
            dve_norm(v, 1)
            dve_turn(v, 2, TMP)
            with v.Fori(0, 3) as i:
                dve_mods(v, G_MQ + 1, i)
            dve_gates(v)
            with v.Fori(0, M_HEADS // 2) as i:
                for k in range(2):
                    group_written(v, G_MV + i)
                    v.wait_ge(tri_in, 16)
                    dve_mlstm(v, 2 * i + k)
            v.wait_ge(m_v.sem, m_v.at("n3", M_HEADS - 1))
            dve_mo(v, 0)
            with v.Fori(0, 3) as n:
                dve_mods(v, G_MO + 1, n)
                dve_mo(v, n + 1)
            v.wait_ge(m_root, 1)
            nc.vector.reciprocal(head_rstd[:, 0:32], head_rstd[:, 0:32]).then_inc(m_rec, 1)
            v.wait_ge(m_rec, 1)
            v.wait_ge(gain_in, 16)
            with v.Fori(0, 4) as n:
                dve_mods(v, G_MZ, n)
                dve_mz(v, n)
            dve_turn(v, 3, TMP)
            dve_residual(v, 1, G_OUT2, False)
            v.wait_ge(res_a.sem, res_a.at("q3", 7))
            dve_norm(v, 2)
            dve_final(v, 0)

            v.wait_ge(final_a.sem, final_a.at("q3", 0))
            dve_norm(v, 3)
            dve_turn(v, 4, TMP)
            v.wait_ge(rope_in, 48)
            v.wait_ge(mask_in, 16)
            with v.Fori(0, 2) as j:
                g = G_ATT + 7 * j
                def rotate3(i):
                    att3.dve_keys(v, 4 * j + i, half_cols(P_KH, i))
                    att3.dve_q(v, 4 * j + i, 4 * j + i, half_cols(P_QH, i))

                group_written(v, g + 1)
                rotate3(0)
                group_written(v, g + 2)
                for i in range(4):
                    h = 4 * j + i
                    att3.dve_vals(v, h, h, half_cols(P_VH, i))
                    att3.dve_head(v, h, page(P_YA + h), (lambda: rotate3(i + 1)) if i < 3 else None)
                    if i:
                        (dve_conv_c, dve_conv_b, dve_conv_z)[i - 1](v, j, g + 3 + i)
            dve_mods(v, G_ZA, 0)
            dve_attn_gate(v, G_ZA, 2, 0, C_U, P_YA)
            dve_mods(v, G_ZA, 1)
            dve_split(v, 5, mix3, 0, 4)
            dve_attn_gate(v, G_ZA, 2, 1, C_U, P_YA)
            dve_split(v, 5, mix3, 4, KT)
            dve_residual(v, 2, G_OUT3, True)

            v.wait_ge(res_a.sem, res_a.at("q3", 11))
            dve_norm(v, 4)
            dve_turn(v, 6, TMP)
            dve_sgu_values(v)
            dve_sgu(v)
            with v.Fori(0, 4) as n:
                dve_sgu_gate(v, n, 4 * n)
            with v.Fori(0, 3) as n:
                dve_sgu_gate(v, 4 + n, 4 * n)
            dve_split(v, 7, mix4, 0, 4)
            dve_sgu_gate(v, 7, 12)
            dve_split(v, 7, mix4, 4, KT)
            dve_residual(v, 3, G_OUT4, True)
            v.wait_ge(res_a.sem, res_a.at("q3", 15))
            dve_norm(v, 5)
            dve_final(v, 1)

        @block.scalar
        def _(act):
            for st in (setup_a, norm_a, res_a, final_a, lru_a, att1.kv_a, att1.a, att3.kv_a, att3.a, qk_a, gate_a, m_a, ln_a):
                act.sem_inc(st.sem, st.start)
            act.sem_inc(mod_out, 16)
            act.dma_start(cols[:], cols_d).then_inc(cols_in, 16)
            for t in range(TT):
                act.dma_start(xp[:, t, :], x_in[t * P:(t + 1) * P, :]).then_inc(x_loaded[t], 16)
            act.dma_start(ident[:], ident_d).then_inc(ident_in, 16)
            act.wait_ge(cols_in, 16)
            nc.scalar.activation(c_silu[:], col("c", 0, KT), ACT.Silu).then_inc(setup_a.sem, 1)
            nc.scalar.activation(lru_decay[:], col("lam", 0, 2 * LRU_TILES), ACT.Abs).then_inc(setup_a.sem, 1)
            act.wait_ge(setup_a.sem, setup_a.at("abs"))
            nc.scalar.activation(lru_decay[:], lru_decay[:], ACT.Exp, scale=-1.0).then_inc(setup_a.sem, 1)
            act.wait_ge(setup_a.sem, setup_a.at("exp"))
            act.wait_ge(setup_v.sem, setup_v.at("sums"))
            nc.scalar.activation(lru_decay[:], lru_decay[:], ACT.Ln, bias=one[:]).then_inc(setup_a.sem, 1)

            for t in range(TT):
                act.wait_ge(x_loaded[t], 16)
                if t:
                    act.wait_ge(first_square, t)
                nc.scalar.activation(page(JUNK, 4), xp[:, t, :], ACT.Square,
                                     accum_out=square_sum[:, t, 0:1]).then_inc(first_square, 1)
            act_norm(act, 0)
            act_turn(act, 0, TMP, lambda f: col("norm0", f), lambda f: col("zero", f))
            act.wait_ge(h_ready, KT)
            act_load_rope(act, 0, att1)
            act.dma_start(gains, rows_d[:, ROW["q_gain"]:ROW["q_gain"] + 2 * HD]).then_inc(rope_in, 16)
            for g in range(G_XL):
                if g >= G_Q:
                    act_mods(act, G_Q, g - G_Q)
                act_evac(act, g, lambda m: qkv[:, m, bass.ds(g * W, W)])
                act_qk_root(act, g)
            for kv, dst, func in ((0, P_XL, ACT.Copy), (1, P_GL, ACT.Silu)):
                att1.act_kv(act, kv)
                with act.Fori(0, 2) as i:
                    for n in range(2):
                        att1.act_head(act, kv * (HEADS // KV_HEADS) + 2 * i + n)
                    act.wait_ge(att1.p.sem, att1.p.at("o", kv * (HEADS // KV_HEADS) + 2 * i + 1))
                    act_evac(act, G_XL + 2 * kv + i, lambda m: page(dst + 4 * i + m), func)
            act_lru_load(act, 0, 0)
            with act.Fori(0, 2) as i:
                for n in range(2):
                    act_lru_load(act, 2 * i + n + 1, 1 - n)
                    act_lru(act, 2 * i + n, n)
            act_attn_gate(act, G_GA, 0, 0, GA_TMP)
            for j in range(4, LRU_TILES):
                if j + 1 < LRU_TILES:
                    act_lru_load(act, j + 1, (j + 1) % 2)
                act_lru(act, j, j % 2)
            lru_or_attn = lambda f: (lru_v, "yg", f) if f < LRU_TILES else (ga_v, f"m{f % 4}", f // 4 - 2)
            full(act, G_GA + 1, 0)
            act_split(act, mix1, 0, 4, lru_or_attn)
            act_attn_gate(act, G_GA, 0, 1, GA_TMP)
            act_split(act, mix1, 4, KT, lru_or_attn)
            act_residual(act, 0, G_OUT1, x_in, False, True)

            act.dma_start(page(GW), gate_w).then_inc(gate_in, 16)
            act_norm(act, 1)
            act_turn(act, 2, TMP, lambda f: col("norm1", f), lambda f: col("zero", f))
            act.wait_ge(new_out, 64)
            act.dma_start(page(TRI)[:, 0:2 * P], tri_d).then_inc(tri_in, 16)
            for n, dst, scale in ((0, P_MQ, 1.0), (2, P_MK, HD ** -0.5)):
                for i in range(2):
                    if n + i:
                        act_mods(act, G_MQ + 1, n + i - 1)
                    act_evac(act, G_MQ + n + i, lambda m: page(dst + 4 * i + m), scale=scale)
            act_gates(act)
            act_evac(act, G_MV, lambda m: v3[:, m, 0:W])
            with act.Fori(0, 3) as i:
                group_written(act, G_MV + i)
                for k in range(2):
                    act_mlstm(act, 2 * i + k)
                act_evac(act, G_MV + 1 + i, lambda m: v3[:, m, bass.ds((i + 1) * W, W)])
            group_written(act, G_MV + 3)
            for h in range(M_HEADS - 2, M_HEADS):
                act_mlstm(act, h)
            act.wait_ge(m_v.sem, m_v.at("n3", M_HEADS - 1))
            act_gate_evac(act, G_MO, o_v, "g", 0, ACT.Sigmoid)
            act.dma_start(page(MZ_GAIN, 4), row("m_gain", D)).then_inc(gain_in, 16)
            with act.Fori(0, 3) as n:
                act_mods(act, G_MO + 1, n)
                act_gate_evac(act, G_MO + 1 + n, o_v, "g", n + 1, ACT.Sigmoid)
            act.wait_ge(o_v.sem, o_v.at("r3", 3))
            nc.scalar.activation(head_rstd[:, 0:32], head_sq[:, 0:32], ACT.Sqrt, bias=eps[:],
                                 scale=1.0 / M_V).then_inc(m_root, 1)
            with act.Fori(0, 4) as n:
                act_mods(act, G_MZ, n)
                act_gate_evac(act, G_MZ + n, z_v, "z", n, ACT.Silu)
            act_turn(act, 3, TMP)
            act_residual(act, 1, G_OUT2, x_mid, False, False)
            act_norm(act, 2)
            act_final(act, 0)
            act.dma_start(x_mid.rearrange("(t p) n -> p t n", p=P), xp).then_inc(new_out, 16)

            act_norm(act, 3)
            act.wait_ge(modc_v.sem, modc_v.at("gain", 0))
            act_turn(act, 4, TMP, lambda f: mod_scale[:, f:f + 1], lambda f: mod_shift[:, f:f + 1])
            act.wait_ge(new_out, 80)
            act.wait_ge(h_ready, 5 * KT)
            act_load_rope(act, 1, att3)
            act.dma_start(page(att3.pg["mask"], 4), mask_d).then_inc(mask_in, 16)
            with act.Fori(0, 2) as j:
                g = G_ATT + 7 * j
                act.wait_ge(att3.s_v.sem, att3.s_v.at("out", 4 * j, back=1))
                for n, p in enumerate((P_QH, P_KH, P_VH)):
                    act_evac(act, g + n, lambda m: page(p + m))
                for i in range(4):
                    att3.act_kv(act, 4 * j + i)
                    att3.act_head(act, 4 * j + i)
                    if i == 0:
                        act_conv_u(act, j, g + 3)
                    if i == 3:
                        act_conv_z(act, j, g + 6)
            act.wait_ge(cv_v.sem, cv_v.at("z3", 1))
            act_mods(act, G_ZA, 0)
            act_attn_gate(act, G_ZA, 2, 0, C_U)
            act_mods(act, G_ZA, 1)
            conv_or_attn = lambda f: ((cv_v, f"z{f % 4}", f // 4) if f < LRU_TILES else (ga_v, f"m{f % 4}", f // 4))
            full(act, G_ZA + 1, 0)
            act_split(act, mix3, 0, 4, conv_or_attn)
            act_attn_gate(act, G_ZA, 2, 1, C_U)
            act_split(act, mix3, 4, KT, conv_or_attn)
            act_residual(act, 2, G_OUT3, x_mid, True, True)

            act_norm(act, 4)
            act.wait_ge(modc_v.sem, modc_v.at("gain", 1))
            act_turn(act, 6, TMP, lambda f: mod_scale[:, f:f + 1], lambda f: mod_shift[:, f:f + 1])
            act_sgu_values(act)
            with act.Fori(0, 4) as n:
                act_sgu_gate(act, n, ACT.Gelu_apprx_tanh)
            with act.Fori(4, 7) as n:
                act_sgu_gate(act, n, ACT.Silu)
            gated = lambda f: (u_v, f"m{f % 4}", 4 + f // 4)
            full(act, G_SZ + 3, 0)
            act_split(act, mix4, 0, 4, gated)
            act_sgu_gate(act, 7, ACT.Silu)
            act_split(act, mix4, 4, KT, gated)
            act_residual(act, 3, G_OUT4, x_mid, True, False)
            act_norm(act, 5)
            for t in range(TT):
                act.wait_ge(final_v.sem, final_v.at(f"r{t}", 1))
                act.dma_start(out[t * P:(t + 1) * P, :], xp[:, t, :]).then_inc(out_done, 16)
            act.wait_ge(out_done, 16 * TT)
            act.wait_ge(new_out, 144)

        @block.tensor
        def _(pe):
            for st in (lru_p, att1.kv_p, att1.p, att3.kv_p, att3.p, gate_p, m_p, modc_p, modg_p):
                pe.sem_inc(st.sem, st.start)
            pe.sem_inc(bank_full, FULL0)
            pe.sem_inc(w_used, WUSED0)

            pe.wait_ge(norm_v.sem, norm_v.at("d3"))
            x_tile = lambda f, t: xp[:, t, f * P:(f + 1) * P]
            pe_turned_group(pe, G_KV, True, 0, x_tile, diag)
            with pe.Fori(G_Q, G_XL) as g:
                pe_group(pe, g, True, 0)
            for kv in range(KV_HEADS):
                att1.pe_kv(pe, kv, kv * (HEADS // KV_HEADS))
                with pe.Fori(0, 2) as i:
                    for n in range(2):
                        h, g = kv * (HEADS // KV_HEADS) + 2 * i + n, G_XL + 2 * kv + i
                        att1.pe_queries(pe, h, kv)
                        pe_chunks(pe, g, 4 * n, 4 * n + 1, False, 0)
                        att1.pe_scores(pe, h, kv, (0, 1))
                        pe_chunks(pe, g, 4 * n + 1, 4 * n + 2, False, 0)
                        att1.pe_turn_probs(pe, h, (0, 1))
                        att1.pe_scores(pe, h, kv, (2, 3))
                        pe_chunks(pe, g, 4 * n + 2, 4 * n + 3, False, 0)
                        att1.pe_turn_probs(pe, h, (2, 3))
                        att1.pe_values(pe, h, kv)
                        pe_chunks(pe, g, 4 * n + 3, 4 * n + 4, False, 0)
            with pe.Fori(0, 2) as i:
                for n in range(4):
                    pe_chunks(pe, G_GA + i, 2 * n, 2 * n + 1, False, 0)
                    pe_lru(pe, 2 * i + n // 2, n % 2)
                    pe_chunks(pe, G_GA + i, 2 * n + 1, 2 * n + 2, False, 0)
            with pe.Fori(G_OUT1, G_OUT1 + 4) as g:
                pe_group(pe, g, True, KT)

            pe.wait_ge(norm_v.sem, norm_v.at("d3", 1))
            pe_turned_group(pe, G_MQ, False, 2, x_tile, diag)
            with pe.Fori(G_MQ + 1, G_MV) as g:
                pe_group(pe, g, False, 2 * KT)
            pe_gates(pe)
            slot_shift["pe"] = 1
            pe_chunks(pe, G_MV, 0, 6, True, 2 * KT)
            pe_gate_cols(pe)
            pe_chunks(pe, G_MV, 6, NCH, True, 2 * KT)
            with pe.Fori(0, M_HEADS // 2) as i:
                pe_m_group(pe, G_MV + 1 + i, 2 * i)
            with pe.Fori(G_MO + 1, G_OUT2) as g:
                pe_group(pe, g, True, 2 * KT)
            pe.wait_ge(z_v.sem, z_v.at("z3", 3))
            pe_turned_group(pe, G_OUT2, True, 3, lambda f, t: v3[:, t, f * P:(f + 1) * P], None)
            with pe.Fori(G_OUT2 + 1, G_OUT2 + 3) as g:
                pe_group(pe, g, True, 3 * KT)
            pe_mod_cols(pe, 0)
            pe_group(pe, G_OUT2 + 3, True, 3 * KT)

            pe.wait_ge(norm_v.sem, norm_v.at("d3", 3))
            pe_turned_group(pe, G_ATT, True, 4, x_tile, diag)
            for j in range(2):
                g = G_ATT + 7 * j
                with pe.Fori(1 - j, 3) as n:
                    pe_group(pe, g + n, True, 4 * KT)
                with pe.Fori(0, 4) as i:
                    h = 4 * j + i
                    att3.pe_kv(pe, h, h)
                    att3.pe_queries(pe, h, h)
                    pe_chunks(pe, g + 3 + i, 0, 2, False, 4 * KT)
                    att3.pe_scores(pe, h, h, (0, 1))
                    pe_chunks(pe, g + 3 + i, 2, 3, False, 4 * KT)
                    att3.pe_turn_probs(pe, h, (0, 1))
                    att3.pe_scores(pe, h, h, (2, 3))
                    pe_chunks(pe, g + 3 + i, 3, 4, False, 4 * KT)
                    att3.pe_turn_probs(pe, h, (2, 3))
                    att3.pe_values(pe, h, h)
                    pe_chunks(pe, g + 3 + i, 4, NCH, False, 4 * KT)
            with pe.Fori(G_ZA, G_OUT3) as g:
                pe_group(pe, g, False, 4 * KT)
            pe_group(pe, G_OUT3, True, 5 * KT)
            pe_gate(pe, 2)
            with pe.Fori(G_OUT3 + 1, G_OUT3 + 3) as g:
                pe_group(pe, g, True, 5 * KT)
            pe.wait_ge(modg_v.sem, modg_v.at("g3", 0))
            pe_mod_cols(pe, 1)
            pe_group(pe, G_OUT3 + 3, True, 5 * KT)

            pe.wait_ge(norm_v.sem, norm_v.at("d3", 4))
            pe_turned_group(pe, G_SV, True, 6, x_tile, diag)
            with pe.Fori(G_SV + 1, G_SU) as g:
                pe_group(pe, g, True, 6 * KT)
            pe_chunks(pe, G_SU, 0, 6, False, 6 * KT)
            for n in range(2):
                pe_sgu(pe, 8 * n, 8 * n + 8)
                pe_chunks(pe, G_SU, 6 + n, 7 + n, False, 6 * KT)
            with pe.Fori(G_SU + 1, G_OUT4) as g:
                pe_group(pe, g, False, 6 * KT)
            pe_group(pe, G_OUT4, True, 7 * KT)
            pe_gate(pe, 3)
            with pe.Fori(G_OUT4 + 1, GROUPS) as g:
                pe_group(pe, g, True, 7 * KT)


def _rope_table(angle_lo, angle_hi=None):
    both = []
    for fn, sign in ((np.cos, 1.0), (np.sin, -1.0)):
        pieces = []
        for angle in ((angle_lo, angle_hi) if angle_hi is not None else (angle_lo,)):
            pieces += [np.float32(sign) * fn(angle), fn(angle)]
        both.append(np.concatenate(pieces, axis=1).astype(np.float32))
    return np.stack(both).reshape(2, TT, P, HD).transpose(2, 0, 1, 3)


def kernel(**inputs):
    import concourse.bacc as _bacc
    from concourse.bass_utils import run_bass_kernel_spmd as _run

    a = {k: np.asarray(v) for k, v in inputs.items()}

    def groups(w, *parts):
        w = np.concatenate([w[:, b:e] for b, e in parts], axis=1) if parts else w
        return w.reshape(KT, P, -1, W).transpose(2, 1, 0, 3).reshape(-1, P, KT * W)

    w1, w3, w5, w7 = a["even_w_in"][0], a["odd_w_in"][0], a["ab_w_in_2"][0], a["sg_w_in_2"][0]
    h = LRU_W
    half = lambda b, j: (b * h + j * W, b * h + (j + 1) * W)
    swap = lambda w: np.concatenate([w[h:], w[:h]])
    ab_groups = [half(b, j) for j in range(2) for b in (0, 1, 2, 4, 6, 5, 7)] + [half(3, 0), half(3, 1)]
    kv = 2 * KV_HEADS * HD
    wall = np.concatenate([
        groups(w1, (h, h + kv), (0, h), (2 * h + kv, 4 * h + kv), (h + kv, 2 * h + kv)),
        groups(swap(a["even_w_out"][0])),
        groups(w3, (0, 2 * h + 3 * D)), groups(a["odd_w_out"][0]),
        groups(w5, *ab_groups), groups(swap(a["ab_w_out_2"][0])),
        groups(w7, (D, 2 * D), (0, D), (2 * D, 3 * D)), groups(a["sg_w_out_2"][0])])
    mods = np.concatenate([groups(a["ab_w_mod_2"][0]), groups(a["sg_w_mod_2"][0])])
    b2, b3 = a["ab_b_mod_2"][0], a["sg_b_mod_2"][0]
    gate_bias = np.pad(a["odd_gate_bias"].reshape(-1), (0, P - 4 * M_HEADS))
    columns = {"norm0": a["norm_gain"][0], "norm1": a["norm_gain"][1], "conv_w": a["conv_w"], "conv_b": a["conv_b"],
               "ba": a["lru_ba"], "bx": a["lru_bx"], "lam": a["lru_lambda"], "c": a["c_2"],
               "norm2": a["ab_norm_g_2"], "shift_b2": b2[0:D], "scale_b2": b2[D:2 * D], "conv3_w": a["ab_conv_w_2"],
               "norm3": a["sg_norm_g_2"], "m_bias": gate_bias, "shift_b3": b3[0:D], "scale_b3": b3[D:2 * D],
               "zero": np.zeros(D, np.float32)}
    assert list(columns) == list(COLS)
    cols = np.concatenate([v.reshape(-1, P) for v in columns.values()]).T
    long_rows = {"final0": a["final_gain"], "final1": a["final_norm_g_2"], "gate_b2": b2[2 * D:], "gate_b3": b3[2 * D:],
                 "m_gain": a["odd_norm_gain"], "ln_g": a["sg_ln_g_2"], "ln_b": a["sg_ln_b_2"], "b_s": a["sg_b_s_2"],
                 "q_gain": a["q_norm_gain"], "k_gain": a["k_norm_gain"]}
    assert list(long_rows) == list(ROW)
    rows = np.broadcast_to(np.concatenate([v.reshape(-1) for v in long_rows.values()]), (P, NROWS))
    lru_w = np.stack([a["lru_wa"][0, 0], a["lru_wx"][0, 0], a["lru_wa"][0, 1], a["lru_wx"][0, 1]])
    lru_w = lru_w.transpose(1, 2, 0, 3).reshape(LRU_TILES, P, 4 * P)
    gate_w = w3[:, 2 * h + 3 * D:].reshape(KT, P, 32).transpose(1, 0, 2).reshape(P, KT * 32)

    f32 = np.float32
    inv = f32(10000.0) ** (-np.arange(0, HD // 2, 2, dtype=f32) / f32(HD // 2))
    tok = np.arange(S)
    rope1 = _rope_table((tok // 64).astype(f32)[:, None] * inv, (tok % 64).astype(f32)[:, None] * inv)
    inv3 = f32(10000.0) ** (-np.arange(HD // 2, dtype=f32) / f32(HD // 2))
    rope3 = _rope_table(tok.astype(f32)[:, None] * inv3)
    rope = np.stack([rope1, rope3]).reshape(2, P, 2 * TT * HD)
    gap = np.abs(tok[:, None] - tok[None, :])
    count = (gap <= 64).astype(int) + ((gap % 4 == 0) & (gap <= 256)) + (gap % 16 == 0)
    mask = np.where(count > 0, np.log(np.maximum(count, 1)) / SCALE, -1e30).astype(f32)
    mask = mask.reshape(TT, P, S).transpose(1, 0, 2).reshape(P, TT * S)
    i = np.arange(P)
    tri = np.stack([i[:, None] <= i[None, :], i[:, None] >= i[None, :]], axis=1).astype(f32).reshape(P, 2 * P)
    arrays = {"x": a["x"][0], "wall": wall, "mods": mods, "cols": cols, "rows": rows, "lru_w": lru_w,
              "gate_w": gate_w, "ident": np.eye(P, dtype=f32), "rope": rope, "mask": mask, "tri": tri,
              "ws": a["sg_w_s_2"][0].transpose(2, 0, 1).reshape(P, 8 * P)}
    arrays = {k: np.ascontiguousarray(v) for k, v in arrays.items()}

    nc = _bacc.Bacc("TRN2", target_bir_lowering=False, num_devices=1)
    args = [nc.dram_tensor(f"in_{k}", v.shape, F32, kind="ExternalInput").ap() for k, v in arrays.items()]
    x_mid = nc.dram_tensor("x_mid", (S, D), F32, kind="Internal").ap()
    mod_mid = nc.dram_tensor("mod_mid", (MODS, P, W), F32, kind="Internal").ap()
    out = nc.dram_tensor("out_0", (S, D), F32, kind="ExternalOutput").ap()
    build_program(nc, *args, x_mid, mod_mid, out)
    r = _run(nc, [{f"in_{k}": v for k, v in arrays.items()}], core_ids=[0])
    return r.results[0]["out_0"].reshape(1, S, D)
```
